# Optimizing a Trainium2 kernel written in Bass

```python
import math
import jax
import jax.numpy as jnp
from jax import lax
import numpy as np

D_MODEL = 1024
BATCH = 1
SEQ = 512
DEPTH = 2

CTX_LEN = 256
GRID_W = 64
N_MIXERS = 4
N_GQA = (DEPTH + 3) // N_MIXERS
N_S5 = (DEPTH + 2) // N_MIXERS
N_SSD = (DEPTH + 1) // N_MIXERS
N_NA = DEPTH // N_MIXERS
N_MOD = 6
D_FF = 4 * D_MODEL
NORM_EPS = 1e-6

GQA_HEAD_DIM = 128
GQA_HEADS = D_MODEL // GQA_HEAD_DIM
GQA_KV_HEADS = 2
GQA_GROUP = GQA_HEADS // GQA_KV_HEADS
Q_BLOCK = 128
ROPE_THETA = 10000.0

S5_GROUP = 16
S5_GROUPS = D_MODEL // S5_GROUP
S5_STATE = 64
S5_DT_MIN = 0.001
S5_DT_MAX = 0.1

SSD_D_INNER = 2 * D_MODEL
SSD_HEAD_DIM = 64
SSD_HEADS = SSD_D_INNER // SSD_HEAD_DIM
SSD_GROUPS = 4
SSD_STATE = 128
SSD_CONV = 5
SSD_CHUNK = 128
SSD_CONV_CH = SSD_D_INNER + 2 * SSD_GROUPS * SSD_STATE
SSD_IN = SSD_D_INNER + SSD_CONV_CH + 2 * SSD_HEADS
SSD_DT_MIN = 0.001
SSD_DT_MAX = 0.1

NA_HEAD_DIM = 64
NA_HEADS = D_MODEL // NA_HEAD_DIM
NA_WIN_ROWS = 8
NA_WIN_COLS = 16

kernel_name = "hybrid_interleaved_flow_trunk"

def _rms(x, g):
    xf = x.astype(jnp.float32)
    y = xf * lax.rsqrt(jnp.mean(xf * xf, axis=-1, keepdims=True) + NORM_EPS)
    return (y * g.astype(jnp.float32)).astype(x.dtype)

def _mlp(h, w1, w2):
    return jnp.square(jax.nn.relu(h @ w1)) @ w2

def _attend(q, k, v):
    s = jnp.einsum("bqkgd,bskd->bkgqs", q, k, preferred_element_type=jnp.float32)
    p = jax.nn.softmax(s * (q.shape[-1] ** -0.5), axis=-1).astype(v.dtype)
    return jnp.einsum("bkgqs,bskd->bqkgd", p, v)

def _axial_rope_tables(n_tok, head_dim):
    pos = jnp.arange(n_tok)
    row = (pos // GRID_W).astype(jnp.float32)
    col = (pos % GRID_W).astype(jnp.float32)
    half = head_dim // 2
    inv_freq = 1.0 / (ROPE_THETA ** (jnp.arange(0, half, 2, dtype=jnp.float32) / half))
    ang_r = row[:, None] * inv_freq
    ang_c = col[:, None] * inv_freq
    return jnp.cos(ang_r), jnp.sin(ang_r), jnp.cos(ang_c), jnp.sin(ang_c)

def _rotate(x, cos, sin):
    x1, x2 = jnp.split(x, 2, axis=-1)
    cos = cos[None, :, None, :]
    sin = sin[None, :, None, :]
    return jnp.concatenate([x1 * cos - x2 * sin, x1 * sin + x2 * cos], axis=-1)

def _apply_axial_rope(x, tables):
    cr, sr, cc, sc = tables
    xf = x.astype(jnp.float32)
    half = x.shape[-1] // 2
    out = jnp.concatenate([_rotate(xf[..., :half], cr, sr), _rotate(xf[..., half:], cc, sc)], axis=-1)
    return out.astype(x.dtype)

def _gqa_mixer(hc, h, w_qkv, q_norm, k_norm, w_o, need_ctx):
    n_q = GQA_HEADS * GQA_HEAD_DIM

    def q_of(z):
        q = (z @ w_qkv[:, :n_q]).reshape(z.shape[:2] + (GQA_KV_HEADS, GQA_GROUP, GQA_HEAD_DIM))
        return _rms(q, q_norm)

    def kv_of(z):
        kv = (z @ w_qkv[:, n_q:]).reshape(z.shape[:2] + (2, GQA_KV_HEADS, GQA_HEAD_DIM))
        return _rms(kv[:, :, 0], k_norm), kv[:, :, 1]

    bsz, n_lat, _ = h.shape
    tables = _axial_rope_tables(n_lat, GQA_HEAD_DIM)
    q = _apply_axial_rope(q_of(h).reshape(bsz, n_lat, GQA_HEADS, GQA_HEAD_DIM), tables)
    k, v = kv_of(h)
    k = _apply_axial_rope(k, tables)
    kc, vc = kv_of(hc)
    k_all = jnp.concatenate([kc, k], axis=1)
    v_all = jnp.concatenate([vc, v], axis=1)
    q_blocks = jnp.moveaxis(
        q.reshape(bsz, n_lat // Q_BLOCK, Q_BLOCK, GQA_KV_HEADS, GQA_GROUP, GQA_HEAD_DIM), 1, 0)
    o = lax.map(lambda qb: _attend(qb, k_all, v_all), q_blocks)
    y = jnp.moveaxis(o, 0, 1).reshape(bsz, n_lat, n_q) @ w_o
    yc = None
    if need_ctx:
        yc = _attend(q_of(hc), kc, vc).reshape(hc.shape[0], hc.shape[1], n_q) @ w_o
    return yc, y

def _lin_combine(e1, e2):
    a1, b1 = e1
    a2, b2 = e2
    return a1 * a2, a2 * b1 + b2

def _s5_discretise(a_re, a_im, log_dt, b_re, b_im):
    lam = lax.complex(a_re.astype(jnp.float32), a_im.astype(jnp.float32))
    a_bar = jnp.exp(lam * jnp.exp(log_dt.astype(jnp.float32))[:, None])
    b = lax.complex(b_re.astype(jnp.float32), b_im.astype(jnp.float32))
    b_bar = ((a_bar - 1.0) / lam)[..., None] * b
    return a_bar, b_bar

def _s5_states(u, a_bar, b_bar, s0, reverse):
    bu = jnp.einsum("blgc,gpc->blgp", u, b_bar)
    if reverse:
        bu = jnp.flip(bu, 1)
    if s0 is not None:
        bu = bu.at[:, 0].add(a_bar * s0)
    a_seq = jnp.broadcast_to(a_bar, (1, bu.shape[1]) + a_bar.shape)
    _, st = lax.associative_scan(_lin_combine, (a_seq, bu), axis=1)
    return jnp.flip(st, 1) if reverse else st

def _s5_readout(st, c_re, c_im):
    c = lax.complex(c_re.astype(jnp.float32), c_im.astype(jnp.float32))
    y = jnp.einsum("blgp,gcp->blgc", st, c).real
    return y.reshape(st.shape[0], st.shape[1], D_MODEL)

def _s5_mixer(hc, h, a_re, a_im, log_dt, b_re, b_im, c_re, c_im, d_skip, glu_w, glu_b, need_ctx):
    bsz, n_lat, _ = h.shape
    hf = h.astype(jnp.float32)
    hcf = hc.astype(jnp.float32)
    u = hf.reshape(bsz, n_lat, S5_GROUPS, S5_GROUP).astype(jnp.complex64)
    uc = hcf.reshape(bsz, hc.shape[1], S5_GROUPS, S5_GROUP).astype(jnp.complex64)
    d = d_skip.astype(jnp.float32)
    y = hf * d
    yc = hcf * d if need_ctx else None
    for direction, reverse in ((0, False), (1, True)):
        a_bar, b_bar = _s5_discretise(a_re[direction], a_im[direction], log_dt[direction],
                                      b_re[direction], b_im[direction])
        st_c = _s5_states(uc, a_bar, b_bar, None, reverse)
        s_end = st_c[:, 0] if reverse else st_c[:, -1]
        st = _s5_states(u, a_bar, b_bar, s_end, reverse)
        y = y + _s5_readout(st, c_re[direction], c_im[direction])
        if need_ctx:
            yc = yc + _s5_readout(st_c, c_re[direction], c_im[direction])

    def glu(z):
        g = jax.nn.gelu(z).astype(h.dtype)
        return g * jax.nn.sigmoid(g @ glu_w + glu_b)

    yc_out = glu(yc) if need_ctx else None
    return yc_out, glu(y)

def _dwconv_centred(x, w, b):
    ch = x.shape[-1]
    width = w.shape[0]
    y = lax.conv_general_dilated(
        x, w.astype(x.dtype)[:, None, :], window_strides=(1,),
        padding=[(width // 2, width // 2)], dimension_numbers=("NWC", "WIO", "NWC"),
        feature_group_count=ch)
    return y + b.astype(x.dtype)

def _segsum_exp(a_cum):
    t = a_cum.shape[-1]
    diff = a_cum[..., :, None] - a_cum[..., None, :]
    mask = jnp.tril(jnp.ones((t, t), dtype=bool))
    return jnp.exp(jnp.where(mask, diff, -jnp.inf))

def _ssd_chunked(xs, dt, a, bm, cm, h0, need_y):
    bsz, n, nh, hp = xs.shape
    ng, ns = bm.shape[-2:]
    nj = nh // ng
    nc = n // SSD_CHUNK
    xdt = (xs * dt[..., None]).reshape(bsz, nc, SSD_CHUNK, ng, nj, hp)
    a_cum = jnp.cumsum(
        jnp.moveaxis((dt * a).reshape(bsz, nc, SSD_CHUNK, ng, nj), (1, 2), (3, 4)), axis=-1)
    bm = bm.reshape(bsz, nc, SSD_CHUNK, ng, ns)
    cm = cm.reshape(bsz, nc, SSD_CHUNK, ng, ns)
    decay_states = jnp.exp(a_cum[..., -1:] - a_cum)
    states = jnp.einsum("bclgn,bgjcl,bclgjp->bcgjpn", bm, decay_states, xdt)
    states = jnp.concatenate([h0.reshape(bsz, 1, ng, nj, hp, ns), states], axis=1)
    chunk_cum = jnp.cumsum(jnp.pad(a_cum[..., -1], ((0, 0), (0, 0), (0, 0), (1, 0))), axis=-1)
    decay_chunk = _segsum_exp(chunk_cum)
    new_states = jnp.einsum("bgjzc,bcgjpn->bzgjpn", decay_chunk, states)
    h_final = new_states[:, -1].reshape(bsz, nh, hp, ns)
    if not need_y:
        return None, h_final
    lmat = _segsum_exp(a_cum)
    scores = jnp.einsum("bclgn,bcsgn->bgcls", cm, bm)
    y_diag = jnp.einsum("bgcls,bgjcls,bcsgjp->bclgjp", scores, lmat, xdt)
    y_off = jnp.einsum("bclgn,bcgjpn,bgjcl->bclgjp", cm, new_states[:, :-1], jnp.exp(a_cum))
    return (y_diag + y_off).reshape(bsz, n, nh, hp), h_final

def _flip_if(t, reverse):
    return jnp.flip(t, 1) if reverse else t

def _ssd_mixer(hc, h, w_in, conv_w, conv_b, dt_bias, a_log, d_skip, norm_g, w_out, need_ctx):
    nbc = SSD_GROUPS * SSD_STATE

    def prep(z, with_gate):
        bz, lz, _ = z.shape
        proj = z @ w_in[:, SSD_D_INNER:]
        xbc = jax.nn.silu(_dwconv_centred(proj[..., :SSD_CONV_CH], conv_w, conv_b)).astype(jnp.float32)
        xs = xbc[..., :SSD_D_INNER].reshape(bz, lz, SSD_HEADS, SSD_HEAD_DIM)
        bm = xbc[..., SSD_D_INNER:SSD_D_INNER + nbc].reshape(bz, lz, SSD_GROUPS, SSD_STATE)
        cm = xbc[..., SSD_D_INNER + nbc:].reshape(bz, lz, SSD_GROUPS, SSD_STATE)
        dt = jax.nn.softplus(proj[..., SSD_CONV_CH:].astype(jnp.float32).reshape(bz, lz, 2, SSD_HEADS)
                             + dt_bias.astype(jnp.float32))
        gate = z @ w_in[:, :SSD_D_INNER] if with_gate else None
        return gate, xs, bm, cm, dt

    gate, xs, bm, cm, dt = prep(h, True)
    gate_c, xs_c, bm_c, cm_c, dt_c = prep(hc, need_ctx)
    a = -jnp.exp(a_log.astype(jnp.float32))
    d = d_skip.astype(jnp.float32)[:, None]
    y = xs * d
    yc = xs_c * d if need_ctx else None
    h0 = jnp.zeros((h.shape[0], SSD_HEADS, SSD_HEAD_DIM, SSD_STATE), jnp.float32)
    for direction, reverse in ((0, False), (1, True)):
        y_c, s_c = _ssd_chunked(_flip_if(xs_c, reverse), _flip_if(dt_c[:, :, direction], reverse), a[direction],
                                _flip_if(bm_c, reverse), _flip_if(cm_c, reverse), h0, need_ctx)
        y_l, _ = _ssd_chunked(_flip_if(xs, reverse), _flip_if(dt[:, :, direction], reverse), a[direction],
                              _flip_if(bm, reverse), _flip_if(cm, reverse), s_c, True)
        y = y + _flip_if(y_l, reverse)
        if need_ctx:
            yc = yc + _flip_if(y_c, reverse)

    def out(yy, gt):
        bz, lz = yy.shape[:2]
        yg = yy.reshape(bz, lz, SSD_D_INNER) * jax.nn.silu(gt.astype(jnp.float32))
        yg = _rms(yg.reshape(bz, lz, SSD_GROUPS, SSD_D_INNER // SSD_GROUPS),
                  norm_g.reshape(SSD_GROUPS, SSD_D_INNER // SSD_GROUPS))
        return yg.reshape(bz, lz, SSD_D_INNER).astype(h.dtype) @ w_out

    yc_out = out(yc, gate_c) if need_ctx else None
    return yc_out, out(y, gate)

def _na_mixer(hc, h, w_qkv, rpb, w_o, need_ctx):
    bsz, n_lat, _ = h.shape
    rows = n_lat // GRID_W
    wr = min(NA_WIN_ROWS, rows)
    n_loc = wr * NA_WIN_COLS
    scale = NA_HEAD_DIM ** -0.5

    def q_of(z):
        return (z @ w_qkv[:, :D_MODEL]).reshape(z.shape[:2] + (NA_HEADS, NA_HEAD_DIM))

    def kv_of(z):
        kv = (z @ w_qkv[:, D_MODEL:]).reshape(z.shape[:2] + (2, NA_HEADS, NA_HEAD_DIM))
        return kv[:, :, 0], kv[:, :, 1]

    k, v = kv_of(h)
    kc, vc = kv_of(hc)
    k_grid = k.reshape(bsz, rows, GRID_W, NA_HEADS, NA_HEAD_DIM)
    v_grid = v.reshape(bsz, rows, GRID_W, NA_HEADS, NA_HEAD_DIM)
    q_rows = jnp.moveaxis(q_of(h).reshape(bsz, rows, GRID_W, NA_HEADS, NA_HEAD_DIM), 1, 0)
    cols = np.arange(GRID_W)
    col_start = np.clip(cols - NA_WIN_COLS // 2, 0, GRID_W - NA_WIN_COLS)
    col_idx = col_start[:, None] + np.arange(NA_WIN_COLS)[None, :]
    col_rel = col_idx - cols[:, None] + (NA_WIN_COLS - 1)

    def row_attend(args):
        r, q_row = args
        r0 = jnp.clip(r - wr // 2, 0, rows - wr)
        k_win = lax.dynamic_slice_in_dim(k_grid, r0, wr, axis=1)[:, :, col_idx]
        v_win = lax.dynamic_slice_in_dim(v_grid, r0, wr, axis=1)[:, :, col_idx]
        row_rel = r0 + jnp.arange(wr) - r + (NA_WIN_ROWS - 1)
        bias = rpb[:, row_rel[None, :, None], col_rel[:, None, :]]
        s_loc = jnp.einsum("bqhd,brqchd->bhqrc", q_row, k_win, preferred_element_type=jnp.float32) * scale
        s_loc = s_loc + bias.astype(jnp.float32)[None]
        s_ctx = jnp.einsum("bqhd,bshd->bhqs", q_row, kc, preferred_element_type=jnp.float32) * scale
        p = jax.nn.softmax(
            jnp.concatenate([s_loc.reshape(bsz, NA_HEADS, GRID_W, n_loc), s_ctx], axis=-1), axis=-1
        ).astype(v.dtype)
        p_loc = p[..., :n_loc].reshape(bsz, NA_HEADS, GRID_W, wr, NA_WIN_COLS)
        return (jnp.einsum("bhqrc,brqchd->bqhd", p_loc, v_win)
                + jnp.einsum("bhqs,bshd->bqhd", p[..., n_loc:], vc))

    o = lax.map(row_attend, (jnp.arange(rows), q_rows))
    y = jnp.moveaxis(o, 0, 1).reshape(bsz, n_lat, D_MODEL) @ w_o
    yc = None
    if need_ctx:
        yc = _attend(q_of(hc)[:, :, :, None], kc, vc).reshape(hc.shape[0], hc.shape[1], D_MODEL) @ w_o
    return yc, y

def setup_inputs(seed: int = 0) -> dict:
    key = jax.random.key(seed)
    keys = iter(jax.random.split(key, 48))
    f32 = jnp.float32

    def nrm(shape, scale=1.0):
        return jax.random.normal(next(keys), shape, f32) * scale

    def unif(shape, lo, hi):
        return jax.random.uniform(next(keys), shape, f32, lo, hi)

    d = D_MODEL
    s5_shape = (N_S5, 2, S5_GROUPS, S5_STATE)
    n_q = GQA_HEADS * GQA_HEAD_DIM
    ssd_dt = jnp.exp(unif((N_SSD, 2, SSD_HEADS), math.log(SSD_DT_MIN), math.log(SSD_DT_MAX)))
    return {
        "x": nrm((BATCH, SEQ, d)),
        "c": nrm((BATCH, d)),
        "ctx": nrm((BATCH, CTX_LEN, d)),
        "c_ctx": nrm((d,)),
        "ada_w": nrm((DEPTH, d, N_MOD * d), d ** -0.5),
        "ada_b": nrm((DEPTH, N_MOD * d), 0.02),
        "norm_g": 1.0 + nrm((DEPTH, 4, d), 0.05),
        "mlp_w1": nrm((DEPTH, d, D_FF), d ** -0.5),
        "mlp_w2": nrm((DEPTH, D_FF, d), D_FF ** -0.5),
        "gqa_w_qkv": nrm((N_GQA, d, n_q + 2 * GQA_KV_HEADS * GQA_HEAD_DIM), d ** -0.5),
        "gqa_q_norm": 1.0 + nrm((N_GQA, GQA_HEAD_DIM), 0.05),
        "gqa_k_norm": 1.0 + nrm((N_GQA, GQA_HEAD_DIM), 0.05),
        "gqa_w_o": nrm((N_GQA, n_q, d), n_q ** -0.5),
        "s5_a_re": -0.5 * jnp.exp(nrm(s5_shape, 0.02)),
        "s5_a_im": jnp.broadcast_to(jnp.pi * jnp.arange(S5_STATE, dtype=f32), s5_shape),
        "s5_log_dt": unif((N_S5, 2, S5_GROUPS), math.log(S5_DT_MIN), math.log(S5_DT_MAX)),
        "s5_b_re": nrm((N_S5, 2, S5_GROUPS, S5_STATE, S5_GROUP), (2 * S5_GROUP) ** -0.5),
        "s5_b_im": nrm((N_S5, 2, S5_GROUPS, S5_STATE, S5_GROUP), (2 * S5_GROUP) ** -0.5),
        "s5_c_re": nrm((N_S5, 2, S5_GROUPS, S5_GROUP, S5_STATE), (2 * S5_STATE) ** -0.5),
        "s5_c_im": nrm((N_S5, 2, S5_GROUPS, S5_GROUP, S5_STATE), (2 * S5_STATE) ** -0.5),
        "s5_d": nrm((N_S5, d)),
        "s5_glu_w": nrm((N_S5, d, d), d ** -0.5),
        "s5_glu_b": nrm((N_S5, d), 0.02),
        "ssd_w_in": nrm((N_SSD, d, SSD_IN), d ** -0.5),
        "ssd_conv_w": nrm((N_SSD, SSD_CONV, SSD_CONV_CH), SSD_CONV ** -0.5),
        "ssd_conv_b": nrm((N_SSD, SSD_CONV_CH), 0.02),
        "ssd_dt_bias": ssd_dt + jnp.log(-jnp.expm1(-ssd_dt)),
        "ssd_a_log": jnp.log(unif((N_SSD, 2, SSD_HEADS), 1.0, 16.0)),
        "ssd_d": 1.0 + nrm((N_SSD, SSD_HEADS), 0.05),
        "ssd_norm_g": 1.0 + nrm((N_SSD, SSD_D_INNER), 0.05),
        "ssd_w_out": nrm((N_SSD, SSD_D_INNER, d), SSD_D_INNER ** -0.5),
        "na_w_qkv": nrm((N_NA, d, 3 * d), d ** -0.5),
        "na_rpb": nrm((N_NA, NA_HEADS, 2 * NA_WIN_ROWS - 1, 2 * NA_WIN_COLS - 1), 0.02),
        "na_w_o": nrm((N_NA, d, d), d ** -0.5),
    }

def reference(x, c, ctx, c_ctx, ada_w, ada_b, norm_g, mlp_w1, mlp_w2,
              gqa_w_qkv, gqa_q_norm, gqa_k_norm, gqa_w_o,
              s5_a_re, s5_a_im, s5_log_dt, s5_b_re, s5_b_im, s5_c_re, s5_c_im, s5_d, s5_glu_w, s5_glu_b,
              ssd_w_in, ssd_conv_w, ssd_conv_b, ssd_dt_bias, ssd_a_log, ssd_d, ssd_norm_g, ssd_w_out,
              na_w_qkv, na_rpb, na_w_o):
    bsz = x.shape[0]
    xc = ctx
    silu_c = jax.nn.silu(c)
    silu_cc = jax.nn.silu(c_ctx)
    for i in range(DEPTH):
        kind = i % N_MIXERS
        j = i // N_MIXERS
        need_ctx = i < DEPTH - 1
        mod = (silu_c @ ada_w[i] + ada_b[i]).reshape(bsz, N_MOD, 1, D_MODEL)
        modc = (silu_cc @ ada_w[i] + ada_b[i]).reshape(N_MOD, D_MODEL)
        g = norm_g[i]
        h = _rms(x, g[0]) * (1.0 + mod[:, 1]) + mod[:, 0]
        hc = _rms(xc, g[0]) * (1.0 + modc[1]) + modc[0]
        if kind == 0:
            yc, y = _gqa_mixer(hc, h, gqa_w_qkv[j], gqa_q_norm[j], gqa_k_norm[j], gqa_w_o[j], need_ctx)
        elif kind == 1:
            yc, y = _s5_mixer(hc, h, s5_a_re[j], s5_a_im[j], s5_log_dt[j], s5_b_re[j], s5_b_im[j],
                              s5_c_re[j], s5_c_im[j], s5_d[j], s5_glu_w[j], s5_glu_b[j], need_ctx)
        elif kind == 2:
            yc, y = _ssd_mixer(hc, h, ssd_w_in[j], ssd_conv_w[j], ssd_conv_b[j], ssd_dt_bias[j],
                               ssd_a_log[j], ssd_d[j], ssd_norm_g[j], ssd_w_out[j], need_ctx)
        else:
            yc, y = _na_mixer(hc, h, na_w_qkv[j], na_rpb[j], na_w_o[j], need_ctx)
        x = x + mod[:, 2] * _rms(y, g[1])
        h = _rms(x, g[2]) * (1.0 + mod[:, 4]) + mod[:, 3]
        x = x + mod[:, 5] * _rms(_mlp(h, mlp_w1[i], mlp_w2[i]), g[3])
        if need_ctx:
            xc = xc + modc[2] * _rms(yc, g[1])
            hc = _rms(xc, g[2]) * (1.0 + modc[4]) + modc[3]
            xc = xc + modc[5] * _rms(_mlp(hc, mlp_w1[i], mlp_w2[i]), g[3])
    return x


_drawn_inputs = setup_inputs


def setup_inputs(seed=0):
    import zlib

    import numpy as np

    out = dict(_drawn_inputs(seed))
    spreads = {}
    factors = {'gqa_q_norm': 7.885,
     'gqa_k_norm': 8.0,
     's5_a_re': 200.0,
     's5_glu_b': 8.0,
     's5_a_im': 29.4,
     's5_log_dt': 39.576,
     's5_b_re': 39.904,
     's5_b_im': 39.512,
     's5_c_re': 39.296,
     's5_c_im': 40.336}
    for name, (base, spread) in spreads.items():
        noise = np.random.default_rng([zlib.crc32(name.encode()), seed]).standard_normal(out[name].shape)
        drawn = base * np.exp(spread * noise) if base else spread * noise
        out[name] = jnp.asarray(drawn.astype(out[name].dtype))
    for name, factor in factors.items():
        out[name] = (out[name] * factor).astype(out[name].dtype)
    return out
```

```python
import math
from contextlib import ExitStack

import numpy as np

import concourse.bass as bass
from concourse import mybir

F32 = mybir.dt.float32
F32R = mybir.dt.float32r
ACT = mybir.ActivationFunctionType
ALU = mybir.AluOpType
AX = mybir.AxisListType

P = 128
D = 1024
KT = D // P
SEQ, CTX = 512, 256
T = CTX + SEQ
CH = 8
NCC, NCL = CTX // CH, SEQ // CH
NCH = NCC + NCL
FF = 4 * D
EPS = 1e-6
HD = 128
HEADS, KVH = 8, 2
GROUPS, SC = 64, 16
NP = 64
UNIT = 2048
NRAW = 4
MODC = 384
TWO_PI = 2 * math.pi
MAGIC = 1.5 * 2 ** 23
PI_HI, PI_MID = 6.28125, 0.0019350051879882812
C3 = 8192
PI_LO = TWO_PI - PI_HI - PI_MID


def build(nc, a, out):
    ctx = ExitStack()
    with ctx:
        sems = {}

        def sem(name):
            if name not in sems:
                sems[name] = ctx.enter_context(nc.semaphore(name))
            return sems[name]

        def sb(stack, name, shape, dt=F32):
            return stack.enter_context(nc.sbuf_tensor(name, shape, dt))

        ps = ctx.enter_context(nc.psum_tensor("ps", [P, 8, 512], F32))
        xT = sb(ctx, "xT", [P, KT, T])
        sq = sb(ctx, "sq", [P, 2, T])
        tmp = sb(ctx, "tmp", [P, 2, T])
        rst = sb(ctx, "rst", [P, T])
        consts = sb(ctx, "squares_rot", [P, 3 * P])
        ident, ones, rotm = consts[:, 0:P], consts[:, P:2 * P], consts[:, 2 * P:3 * P]
        cmask = sb(ctx, "cmask", [P, SC])
        dcol = sb(ctx, "dcol", [P, SC])
        epsc = sb(ctx, "epsc", [P, 1])
        rows = sb(ctx, "rows", [96, 2, P])
        cols = sb(ctx, "cols", [P, 96])
        adab = sb(ctx, "adab", [P, 96])
        sil = sb(ctx, "sil", [P, 2, KT])
        mod = sb(ctx, "mod", [P, 2, 6, KT, 2])
        coef = sb(ctx, "coef", [P, 2, 4, KT, 2])
        nmax = sb(ctx, "nmax", [P, 2])
        rsum = sb(ctx, "rsum", [P, 2])
        rinv = sb(ctx, "rinv", [P, 2])

        A = ExitStack()
        raw = sb(A, "raw", [P, NRAW, UNIT])
        h_hi = sb(A, "h_hi", [P, KT, T], F32R)
        h_lo = sb(A, "h_lo", [P, KT, T], F32R)
        w_hi = sb(A, "w_hi", [P, 2, UNIT], F32R)
        w_lo = sb(A, "w_lo", [P, 2, UNIT], F32R)
        with ExitStack() as s:
            xtok = sb(s, "xtok", [P, 6, D])
        with ExitStack() as s:
            qk = sb(s, "qk", [P, HEADS + KVH, T])
            vt = sb(s, "vt", [P, 6, KVH * HD])
            pT = sb(s, "pT", [P, 2, 6, 256])
            rope = pT[:, :, :, :].rearrange("p a b c -> p (a b c)")
        with ExitStack() as s:
            ybuf = sb(s, "ybuf", [P, KT, T])
            a_hi = sb(s, "a_hi", [P, 4, T], F32R)
            a_lo = sb(s, "a_lo", [P, 4, T], F32R)
        A.close()
        with ExitStack() as s:
            ytok = sb(s, "ytok", [P, CH, D])
            pv = sb(s, "pv", [P, 2 * GROUPS * SC + SC])
            qv = sb(s, "qv", [P, 2 * GROUPS, SC])
            powT = sb(s, "powT", [P, 2, 9, P])
            a8 = sb(s, "a8", [P, 2, 2, 2, 32])
            S = sb(s, "S", [P, 97 * P])
            with ExitStack() as s1:
                U = sb(s1, "U", [P, GROUPS, NCH])
                pw = sb(s1, "pw", [P, 2 * GROUPS, SC])
                qw = sb(s1, "qw", [P, 2 * GROUPS, SC])
                wp = sb(s1, "wp", [P, 8, P])
                wT = sb(s1, "wT", [P, 8, P])
                kf = sb(s1, "kf", [P, 2, 15 * SC])
                ml = sb(s1, "ml", [P, 8, CH, SC])
                sdm = sb(s1, "sdm", [P, 2, SC])
            with ExitStack() as s1:
                sst = sb(s1, "sst", [P, 2, GROUPS, NCL])
                xv = sb(s1, "xv", [P, 2, 8, P])
        flat_tok = ytok[:, :, :].rearrange("p t n -> p (t n)")
        htok = flat_tok.rearrange("p (g t c) -> p g t c", g=GROUPS, t=CH)
        Sv = S[:, :].rearrange("p (i d r q) -> p i d r q", d=2, r=2, q=32)
        h1 = S[:, 0:KT * T].rearrange("p (k t c) -> p k t c", k=KT, t=CH)

        units = []

        def square_units(w, n0, n):
            v = w.rearrange("(k p) n -> p k n", p=P)
            return [(True, v[:, :, n0 + 256 * i:n0 + 256 * (i + 1)]) for i in range(n)]

        def ada_units(l, j0, j1):
            v = a["ada_w"][l].rearrange("(k p) n -> p k n", p=P)
            return [(False, v[:, :, 256 * i:256 * (i + 1)]) for i in range(4 * j0, 4 * j1)]

        first = ada_units(0, 0, 2) + square_units(a["gqa_w_qkv"][0], 0, 6) + ada_units(0, 2, 6) \
            + square_units(a["gqa_w_o"][0], 0, 4)
        NG = FF // 256
        w1v = [a["mlp_w1"][l].rearrange("(k p) (g n) -> g p k n", p=P, n=256) for l in range(2)]
        w2v = [a["mlp_w2"][l].rearrange("(g k p) n -> g p k n", p=P, k=2) for l in range(2)]
        adav = a["ada_w"][1].rearrange("(k p) (u n) -> u p k n", p=P, n=256)
        glu = square_units(a["s5_glu_w"][0], 0, 4)

        def slot_view(n, k):
            return raw[:, n % NRAW, :].rearrange("p (k n) -> p k n", k=k)

        N_MLP0 = len(first)
        M_MLP0 = sum(s for s, _ in first)
        N_GLU = N_MLP0 + 2 * NG + 24
        M_GLU = M_MLP0 + 2 * NG
        N_MLP1 = N_GLU + len(glu)
        M_MLP1 = M_GLU + len(glu)
        G_Q, G_WO = 0, 16
        G_MLP0 = G_WO + 8
        G_GLU = G_MLP0 + 10 * NG
        G_MLP1 = G_GLU + 8
        assert G_MLP0 % 4 == 0 and G_MLP1 % 4 == 0
        LOOPS = 7

        def groups_after(m):
            for l, m0, g0 in ((1, M_MLP1, G_MLP1), (0, M_MLP0, G_MLP0)):
                if m0 <= m < m0 + 2 * NG:
                    c = m - m0
                    if c == 2 * NG - 1:
                        return g0 + 10 * NG
                    return g0 + 2 + 10 * (c // 2) - (8 if c % 2 else 0) if c else g0 + 2
            if m >= M_GLU:
                return G_GLU + 2 * (m - M_GLU + 1)
            return 2 * (m + 1) + (4 if m >= 5 else 0)

        def unit_of_split(m):
            if m < M_MLP0:
                return [n for n, (s, _) in enumerate(first) if s][m]
            if m < M_GLU:
                c = m - M_MLP0
                return N_MLP0 + (0 if c == 0 else 2 * c - 1 if c <= 24 else c + 24)
            return N_GLU + m - M_GLU

        L0 = [(0, 384), (384, 384)]
        L1 = [(0, 512)]
        SEG0 = [(0, CTX, 1), (CTX, SEQ, 0)]

        def banks(b, chunks, parts=P):
            n = chunks[0][1]
            return ps[0:parts, b:b + len(chunks), 0:n]

        def ring(g, chunks):
            return banks(2 * (g % 4), chunks)

        def by_chunk(ap, chunks):
            return ap.rearrange("p (c n) -> p c n", c=len(chunks))

        def norm_src(n, k):
            if n in (0, 2):
                return xT[:, k, :]
            if n in (1, 3):
                return ybuf[:, k, :]
            if n == 4:
                return xT[:, k, :]
            if n == 6:
                return xT[:, k, CTX:T]
            return ybuf[:, k, 0:SEQ]

        def norm_chunks(n):
            return L0 if n < 5 else L1

        def mul_buf(t):
            return t[:, :, :].rearrange("p a b -> p (a b)")[:, 0:1024].rearrange("p (g t c) -> p g t c", g=8, t=CH)

        def per_t(t, b, d):
            g0 = d * GROUPS + 8 * b
            return t[:, g0:g0 + 8, :].unsqueeze(2).to_broadcast([P, 8, CH, SC])

        def power(r, b, d, inward):
            g0 = d * GROUPS + 8 * b
            lo = 0 if inward else 1
            v = powT[:, r, lo:lo + 8, g0:g0 + 8]
            if (d == 0) == inward:
                v = powT[:, r, lo:lo + 8, g0:g0 + 8][:, ::-1, :]
            return v.rearrange("p t g -> p g t").unsqueeze(3).to_broadcast([P, 8, CH, SC])

        def pow_src(r, e):
            return flat_tok[:, (r * 9 + e) * P:(r * 9 + e + 1) * P]

        def bc_src(lo, is_b, c):
            if is_b:
                v = S[:, 2048:2048 + 3072].rearrange("p (r s c) -> p r s c", r=3, s=NP)
                return v[:, lo:lo + 2, :, c].rearrange("p r s -> p (r s)")
            return S[:, C3 + 192 * c + NP * lo:C3 + 192 * c + NP * lo + P]

        att = [(hd, q0, nk) for hd in range(HEADS) for q0, nk in ((0, 2), (CTX, 6), (CTX + 256, 6))]

        def wide_units(u):
            return sum(nk == 6 for _, _, nk in att[:u])

        def tile64(i):
            return S[:, 11456 + 64 * i:11456 + 64 * (i + 1)]
        are, aim, dtl, dtc = S[:, 11264:11328], S[:, 11328:11392], S[:, 11392:11393], S[:, 11393:11394]
        lr, li, mag, ang, ang2, sn, cs, t0_, t1_, t2_, den, cre, cim, arm1, kk = (tile64(i) for i in range(15))

        block = ctx.enter_context(nc.Block())

        @block.sync
        def _(sp):
            def x_rows(t, is_ctx):
                src = a["ctx" if is_ctx else "x"][0].rearrange("(j t) n -> t j n", t=CH)[t]
                nch = NCC if is_ctx else NCL
                per = P // nch
                tile = t // per + (0 if is_ctx else 2)
                return tile, xtok[nch * (t % per):nch * (t % per + 1), tile, :], src

            def load(n, src, k):
                sp.dma_start(slot_view(n, k), src).then_inc(sem(f"raw_landed{n % NRAW}"), 16)

            kinds = [s for s, _ in first]

            for is_ctx in (True, False):
                for t in range(CH):
                    tile, dst, src = x_rows(t, is_ctx)
                    sp.dma_start(dst, src).then_inc(sem(f"x_landed{tile}"), 16)
            for n, (is_split, src) in enumerate(first):
                if n >= NRAW:
                    o = n - NRAW
                    if kinds[o]:
                        sp.wait_ge(sem("w_split"), sum(kinds[:o]) + 1)
                    else:
                        sp.wait_ge(sem("ada_used"), o - sum(kinds[:o]) + 1)
                load(n, src, 8)

            def free_split(m, i=0):
                sp.wait_ge(sem("w_split"), m + 1 + i)

            free_split(M_MLP0 - 4)
            load(N_MLP0, w1v[0][0], 8)
            base = N_MLP0 + 1
            m = M_MLP0 + 1
            ada0 = 24

            def mlp0_slot_free(c, i, loop):
                if not loop and i == 0 and c < 4:
                    sp.wait_ge(sem("w_split"), M_MLP0 - 3 + c + 1)
                elif c % 2:
                    sp.wait_ge(sem("ada_used"), 4 * i + ada0 + (c - 5) // 2 + 1 + 0)
                else:
                    sp.wait_ge(sem("w_split"), 4 * i + m + (c - 4) // 2 + 1)

            def mlp0_double(i, loop):
                for c in range(8):
                    mlp0_slot_free(c, i, loop)
                    step = c // 4
                    if c % 4 == 0:
                        load(base + c, w1v[0][2 * i + 1 + step], 8)
                    elif c % 4 == 2:
                        load(base + c, w2v[0][2 * i + step], 2)
                    else:
                        load(base + c, adav[4 * i + c // 2], 8)

            mlp0_double(0, False)
            with sp.Fori(1, 6) as i:
                mlp0_double(i, True)
            n = base + 48
            mm = m + 24
            tail = [(w1v[0][13], 8), (w2v[0][12], 2), (w1v[0][14], 8), (w2v[0][13], 2),
                    (w1v[0][15], 8), (w2v[0][14], 2), (w2v[0][15], 2)]
            for c, (src, k) in enumerate(tail):
                if c < 4:
                    if c % 2:
                        sp.wait_ge(sem("ada_used"), 24 + 24 - 2 + c // 2 + 1)
                    else:
                        sp.wait_ge(sem("w_split"), mm - 2 + c // 2 + 1)
                else:
                    sp.wait_ge(sem("w_split"), mm + c - 4 + 1)
                load(n + c, src, k)
            assert n + 7 == N_GLU and mm + 7 == M_GLU

            sp.wait_ge(sem("x_added"), 2 * KT)
            for r, name in enumerate(("s5_b_re", "s5_b_im")):
                sp.dma_start(S[:, 1024 * r:1024 * (r + 1)],
                             a[name][0].rearrange("d g p c -> (d g) (p c)")).then_inc(sem("s5_in"), 16)
            for r, name in enumerate(("s5_c_re", "s5_c_im")):
                sp.dma_start(S[:, 6144 + 1024 * r:6144 + 1024 * (r + 1)],
                             a[name][0].rearrange("d g c p -> (d g) (c p)")).then_inc(sem("s5_in"), 16)
            for r, name in enumerate(("s5_a_re", "s5_a_im")):
                sp.dma_start((are, aim)[r],
                             a[name][0].rearrange("d g p -> (d g) p")).then_inc(sem("s5_in"), 16)
            sp.wait_ge(sem("d_zero"), 1)
            with nc.allow_non_contiguous_dma(reason="1 KiB and 4 KiB of parameters"):
                sp.dma_start(dtl, a["s5_log_dt"][0].rearrange("d (g o) -> (d g) o", o=1)) \
                    .then_inc(sem("s5_in"), 16)
                dsrc = a["s5_d"][0].rearrange("(b s c) -> s c b", s=4, c=SC)
                for s in range(4):
                    sp.dma_start(dcol[32 * s:32 * s + SC, :], dsrc[s]).then_inc(sem("d_in"), 16)

            sp.wait_ge(sem("yT_ready"), KT)
            for c, (_, src) in enumerate(glu):
                load(N_GLU + c, src, 8)
            free_split(M_GLU)
            load(N_MLP1, w1v[1][0], 8)

            def mlp1_double(i):
                for c, (v, o, k) in enumerate(((w1v[1], 1, 8), (w2v[1], 0, 2), (w1v[1], 2, 8), (w2v[1], 1, 2))):
                    free_split(M_MLP1 + 1 + c - 4, 4 * i)
                    load(N_MLP1 + 1 + c, v[2 * i + o], k)

            with sp.Fori(0, LOOPS) as i:
                mlp1_double(i)
            for c, (src, k) in enumerate(((w1v[1][15], 8), (w2v[1][14], 2), (w2v[1][15], 2))):
                free_split(M_MLP1 + 29 + c - 4)
                load(N_MLP1 + 29 + c, src, k)

            ov = out[0].rearrange("(j t) n -> t j n", t=CH)
            for r in range(4):
                sp.wait_ge(sem("o_act"), r + 1)
                sp.wait_ge(sem("o_dve"), r + 1)
                for t in (2 * r, 2 * r + 1):
                    sp.dma_start(ov[t], xtok[64 * (t % 2):64 * (t % 2) + 64, r, :]).then_inc(sem("stored"), 16)
            sp.wait_ge(sem("stored"), 16 * CH)

        @block.gpsimd
        def _(pool):
            nc.gpsimd.memset(epsc[:, :], EPS).then_inc(sem("eps_set"), 1)

            def zero_y(n):
                pool.wait_ge(sem("x_added"), n)
                nc.gpsimd.memset(ybuf[:, :, :], 0.0).then_inc(sem("y_zero"), 1)

            nc.gpsimd.memset(dcol[:, :], 0.0).then_inc(sem("d_zero"), 1)
            zero_y(KT)

            pool.wait_ge(sem("prep_over"), 1)
            pool.wait_ge(sem("h1_ready"), KT)
            for b in range(8):
                for d in range(2):
                    i = 2 * b + d
                    if i >= 1:
                        pool.wait_ge(sem("wp_sum"), i)
                    nc.gpsimd.tensor_tensor(mul_buf(tmp), per_t(qw, b, d), power(1, b, d, True), ALU.mult) \
                        .then_inc(sem("m2_ready"), 1)
            for b in range(8):
                for d in range(2):
                    i = 16 + 2 * b + d
                    pool.wait_ge(sem("wp_sum"), i)
                    nc.gpsimd.tensor_tensor(mul_buf(tmp), per_t(qv, b, d), power(1, b, d, False), ALU.mult) \
                        .then_inc(sem("m2_ready"), 1)
            zero_y(3 * KT)

        @block.tensor
        def _(pe):
            mm = nc.tensor.matmul

            def split_matmul(o, l_hi, l_lo, r_hi, r_lo, chunks, first_, last_):
                q = None
                for i, (lw, rw) in enumerate(((l_hi, r_hi), (l_hi, r_lo), (l_lo, r_hi))):
                    for c, (t0, n) in enumerate(chunks):
                        q = mm(o[:, c, :], lw, rw[:, t0:t0 + n], start=first_ and i == 0,
                               stop=last_ and i == 2)
                return q

            def open_group(g, i=0, static=True):
                if not static or g >= 4:
                    pe.wait_ge(sem("acc_taken"), g - 3 + i)

            def tiles(m, g0, k_tiles, width, moving, chunks, gi=0, wi=0, static=True, between=None):
                pe.wait_ge(sem("w_split"), m + 1 + wi)
                wh = w_hi[:, m % 2, :].rearrange("p (k n) -> p k n", k=k_tiles)
                wl = w_lo[:, m % 2, :].rearrange("p (k n) -> p k n", k=k_tiles)
                q = None
                for j in range(width // P):
                    g = g0 + j
                    if between and g % 4 == 2:
                        pe.wait_ge(sem("acc_taken"), g - 2 + gi)
                        between.pop(0)()
                    open_group(g, gi, static)
                    o = ring(g, chunks)
                    for k in range(k_tiles):
                        rh, rl = moving(k)
                        q = split_matmul(o, wh[:, k, P * j:P * j + P], wl[:, k, P * j:P * j + P],
                                         rh, rl, chunks, k == 0, k == k_tiles - 1)
                    q.then_inc(sem("acc_ready"), 1)
                return q

            def ada(n, col, ni=0):
                pe.wait_ge(sem(f"raw_landed{n % NRAW}"), 16 * (n // NRAW + 1) + ni)
                w = slot_view(n, 8)
                for j in range(2):
                    for k in range(KT):
                        q = mm(ps[:, 7, bass.ds(col + 2 * j, 2)], w[:, k, P * j:P * j + P], sil[:, :, k],
                               start=k == 0, stop=k == KT - 1)
                q.then_inc(sem("ada_used"), 1)

            def norm_sum(n):
                for k in range(KT):
                    pe.wait_ge(sem("sq_ready"), KT * n + k + 1)
                    for c, (t0, w) in enumerate(norm_chunks(n)):
                        q = mm(ps[:, c, 0:w], ones, sq[:, k % 2, t0:t0 + w], start=k == 0, stop=k == KT - 1)
                    q.then_inc(sem("sq_used"), 1)

            pe.wait_ge(sem("const_in"), 16 * 2)
            pe.wait_ge(sem("rows_in"), 16 * 7)
            nc.tensor.transpose(ps[:, 6, 0:90], rows[0:90, 0, :], ident[0:90, 0:90])
            nc.tensor.transpose(ps[:, 6, 128:224], rows[0:96, 1, :], ident[0:96, 0:96]).then_inc(sem("cols_ready"), 1)
            for r in range(6):
                pe.wait_ge(sem(f"x_landed{r}"), 16 * (4 if r < 2 else 2))
                for half in range(2):
                    e = 2 * r + half
                    if e >= 6:
                        pe.wait_ge(sem("xT_act" if e % 2 == 0 else "xT_dve"), (e - 6) // 2 + 1)
                    for k in range(4):
                        q = nc.tensor.transpose(ps[:, e % 6, P * k:P * k + P],
                                                xtok[:, r, P * (4 * half + k):P * (4 * half + k) + P], ident)
                    q.then_inc(sem("xT_ready"), 1)
            pe.wait_ge(sem("sil_ready"), 1)
            for u in range(8):
                ada(u, MODC + 4 * u)
            pe.wait_ge(sem("xT_act"), 6)
            pe.wait_ge(sem("xT_dve"), 6)
            norm_sum(0)

            pe.wait_ge(sem("rstd_ready"), 1)
            pe.wait_ge(sem("mod_ready"), 2)

            def h_tile(k):
                return h_hi[:, k, :], h_lo[:, k, :]

            pe.wait_ge(sem("h_split"), KT)
            for u in range(5):
                tiles(u, 2 * u, KT, 256, h_tile, L0)
            pe.wait_ge(sem("w_split"), 6)
            wh = w_hi[:, 5 % 2, :].rearrange("p (k n) -> p k n", k=KT)
            wl = w_lo[:, 5 % 2, :].rearrange("p (k n) -> p k n", k=KT)
            for r in range(6):
                g = 10 + r
                open_group(g)
                for k in range(KT):
                    q = split_matmul(ring(g, [(0, 256)]), h_hi[:, k, P * r:P * r + P], h_lo[:, k, P * r:P * r + P],
                                     wh[:, k, :], wl[:, k, :], [(0, 256)], k == 0, k == KT - 1)
                q.then_inc(sem("acc_ready"), 1)
            pe.wait_ge(sem("acc_taken"), 16)

            for hd in range(HEADS + KVH + 1):
                if hd < HEADS + KVH:
                    pe.wait_ge(sem("hsq_ready"), hd + 1)
                    if hd >= 2:
                        pe.wait_ge(sem("hln_done"), hd - 1)
                    for c, (t0, w) in enumerate(L0):
                        q = mm(ps[:, 2 * (hd % 2) + c, 0:w], ones, sq[:, hd % 2, t0:t0 + w], start=True, stop=True)
                    q.then_inc(sem("hsum_ready"), 1)
                if hd >= 1:
                    pe.wait_ge(sem("q_normed"), hd)
                    if hd >= 3:
                        pe.wait_ge(sem("q_sin"), hd - 2)
                    mm(ps[:, 4 + (hd - 1) % 2, :], rotm, qk[:, hd - 1, CTX:T], start=True, stop=True) \
                        .then_inc(sem("rot_ready"), 1)
                for u in ([8 + 2 * hd, 9 + 2 * hd] if hd < 8 else []):
                    ada(u + 6, MODC + 4 * u)

            pe.wait_ge(sem("q_roped"), HEADS + KVH)
            pe.wait_ge(sem("mod_ready"), 6)

            def scores(t):
                hd, q0, nk = att[t // 2]
                if t >= 2:
                    pe.wait_ge(sem("exp_done"), t - 1)
                lhs = qk[:, hd, q0 + P * (t % 2):q0 + P * (t % 2) + P]
                key = qk[:, HEADS + hd // 4, :]
                chunks = L0 if nk == 6 else [(0, 256)]
                for c, (t0, w) in enumerate(chunks):
                    q = mm(ps[:, 2 * (t % 2) + c, 0:w], lhs, key[:, t0:t0 + w], start=True, stop=True)
                q.then_inc(sem("s_ready"), 1)

            scores(0)
            scores(1)
            for u, (hd, q0, nk) in enumerate(att):
                for t in (2 * u, 2 * u + 1):
                    if t + 2 < 2 * len(att):
                        scores(t + 2)
                for t in (2 * u, 2 * u + 1):
                    pe.wait_ge(sem("p_ready"), t + 1)
                    if t == 2 * u and u >= 1:
                        pe.wait_ge(sem("pT_act"), u)
                        if wide_units(u):
                            pe.wait_ge(sem("pT_dve"), wide_units(u))
                    for kt in range(nk):
                        o = 256 * (kt % 2) + P * (t % 2)
                        q = nc.tensor.transpose(ps[:, 4 + kt // 2, o:o + P], sq[:, t % 2, P * kt:P * kt + P], ident)
                    q.then_inc(sem("pT_ready"), 1)
                pe.wait_ge(sem("pT_act"), u + 1)
                if nk == 6:
                    pe.wait_ge(sem("pT_dve"), wide_units(u + 1))
                if u >= 1:
                    pe.wait_ge(sem("o_taken"), u)
                for kt in range(nk):
                    q = mm(ps[:, 7, 0:256], vt[:, kt, HD * (hd // 4):HD * (hd // 4) + HD],
                           pT[:, u % 2, kt, :], start=kt == 0, stop=kt == nk - 1)
                q.then_inc(sem("o_ready"), 1)
            pe.wait_ge(sem("o_taken"), len(att))

            for u in range(4):
                tiles(6 + u, G_WO + 2 * u, KT, 256, h_tile, L0)
            pe.wait_ge(sem("acc_taken"), G_MLP0)
            norm_sum(1)
            norm_sum(2)

            def mlp(l, m0, g0, n0, chunks):
                def z_unit(m, g, static=True, gi=0, wi=0):
                    tiles(m, g, KT, 256, h_tile, chunks, gi, wi, static)

                def y_unit(group, m, g, ai=0, static=True, gi=0, wi=0, between=None):
                    slot = 2 * (group % 2)
                    pe.wait_ge(sem("a_split"), 2 * NG * l + 2 * group + 2 + ai)
                    tiles(m, g, 2, D, lambda k: (a_hi[:, slot + k, :], a_lo[:, slot + k, :]), chunks, gi, wi, static,
                          between)

                def double(i, with_ada, static=False):
                    for st in range(2):
                        c = 2 * st
                        z_unit(m0 + 1 + c, g0 + 2 + 10 * st, static, 20 * i, 4 * i)
                        adas = [lambda o=o: ada(n0 + 2 + 4 * st + 2 * o, MODC + 4 * (c + o) + 16 * i, 32 * i)
                                for o in range(2)] if with_ada else None
                        y_unit(st, m0 + 2 + c, g0 + 4 + 10 * st, 4 * i, static, 20 * i, 4 * i, adas)

                z_unit(m0, g0)
                with pe.Fori(0, 6) as i:
                    double(i, l == 0)
                double(6, False, True)
                z_unit(m0 + 29, g0 + 142)
                y_unit(14, m0 + 30, g0 + 144)
                y_unit(15, m0 + 31, g0 + 152)

            pe.wait_ge(sem("h_split"), 2 * KT)
            mlp(0, M_MLP0, G_MLP0, N_MLP0, L0)
            pe.wait_ge(sem("acc_taken"), G_GLU)
            norm_sum(3)
            norm_sum(4)

            def turn(i, srcs, name="turned"):
                if i >= 4:
                    pe.wait_ge(sem("turn_taken"), i - 3)
                for c, (src, p, w) in enumerate(srcs):
                    q = nc.tensor.transpose(ps[0:w, i % 4, P * c:P * c + p], src, ident[0:p, 0:p])
                q.then_inc(sem("turned"), 1)

            pe.wait_ge(sem("rstd_ready"), 5)
            pe.wait_ge(sem("prep_ready"), 1)
            i = 0
            for r in range(2):
                for e0 in (0, 4, 8):
                    turn(i, [(pow_src(r, e), P, P) for e in range(e0, min(e0 + 4, 9))])
                    i += 1
            for v, (lo, is_b) in enumerate(((1, True), (0, True), (0, False), (1, False))):
                for c0 in range(0, SC, 4):
                    turn(i, [(bc_src(lo, is_b, c), P, P) for c in range(c0, c0 + 4)])
                    i += 1
            pe.wait_ge(sem("turn_taken"), i)
            pe.wait_ge(sem("h1_ready"), KT)
            for t in range(CH):
                for half in range(2):
                    turn(i, [(h1[:, 4 * half + k, t, :], P, NCH) for k in range(4)])
                    i += 1
            pe.wait_ge(sem("turn_taken"), i)
            for b in range(16):
                if i >= 4:
                    pe.wait_ge(sem("turn_taken"), i - 3)
                for c in range(4):
                    q = nc.tensor.transpose(ps[:, i % 4, NCH * c:NCH * c + NCH],
                                            htok[0:NCH, 4 * b + c, :, :].rearrange("p t c -> p (t c)"),
                                            ident[0:NCH, 0:NCH])
                q.then_inc(sem("turned"), 1)
                i += 1
            pe.wait_ge(sem("turn_taken"), i)

            for b in range(8):
                for d in range(2):
                    j = 2 * b + d
                    pe.wait_ge(sem("wp_sum"), j + 1)
                    if j >= 1:
                        pe.wait_ge(sem("wT_taken"), j)
                    for g in range(8):
                        q = nc.tensor.transpose(ps[:, g // 4, P * (g % 4):P * (g % 4) + P], wp[:, g, :], ident)
                    q.then_inc(sem("wT_ready"), 1)
                    if d == 0 and b >= 1:
                        pe.wait_ge(sem("kf_taken"), b)
                    for g in range(8):
                        g0 = SC * (GROUPS * d + 8 * b + g)
                        c0 = 256 * d + P * (g // 4)
                        q = mm(ps[32 * (g % 4):32 * (g % 4) + 32, 2, c0:c0 + P], pv[:, g0:g0 + 32], wp[:, g, :],
                               start=True, stop=True)
                    q.then_inc(sem("kf_ready"), 1)
                    pe.wait_ge(sem("wT_taken"), j + 1)
                    if j >= 1:
                        pe.wait_ge(sem("bu_taken"), j)
                    for r in range(2):
                        for g in range(8):
                            q = mm(ps[64 * (g % 2):64 * (g % 2) + 64, 3 + r, NCH * (g // 2):NCH * (g // 2) + NCH],
                                   wT[:, g, NP * r:NP * r + NP], U[:, 8 * b + g, :], start=True, stop=True)
                    q.then_inc(sem("bu_ready"), 1)
                pe.wait_ge(sem("kf_taken"), b + 1)
                for h in range(4):
                    i2 = 4 * b + h
                    if i2 >= 2:
                        pe.wait_ge(sem("ml_taken"), i2 - 1)
                    for t in range(4):
                        tt = 4 * (h % 2) + t
                        q = nc.tensor.transpose(ps[:, 5 + h % 2, P * t:P * t + P],
                                                kf[:, h // 2, SC * (7 - tt):SC * (7 - tt) + P], ident)
                    q.then_inc(sem("ml_ready"), 1)
                pe.wait_ge(sem("ml_taken"), 4 * b + 4)
                for hf in range(2):
                    i2 = 2 * b + hf
                    if i2 >= 1:
                        pe.wait_ge(sem("yl_taken"), i2)
                    for g in range(4):
                        q = mm(ps[0:NCL, 7, P * g:P * g + P], U[:, 8 * b + 4 * hf + g, NCC:NCH],
                               ml[:, 4 * hf + g, :, :].rearrange("p t c -> p (t c)"), start=True, stop=True)
                    q.then_inc(sem("yl_ready"), 1)

            pe.wait_ge(sem("restacked"), 8)
            for b in range(8):
                pe.wait_ge(sem("wp_sum"), 16 + 2 * b + 2)
                for hf in range(2):
                    i2 = 2 * b + hf
                    if i2 >= 4:
                        pe.wait_ge(sem("ys_taken"), i2 - 3)
                    for g in range(4):
                        for d in range(2):
                            q = mm(ps[0:NCL, i2 % 4, P * g:P * g + P], sst[:, d, 8 * b + 4 * hf + g, :],
                                   xv[:, d, 4 * hf + g, :], start=d == 0, stop=d == 1)
                    q.then_inc(sem("ys_ready"), 1)
            pe.wait_ge(sem("ys_taken"), 16)
            for k in range(KT):
                if k >= 4:
                    pe.wait_ge(sem("g_ready"), k - 3)
                for t in range(CH):
                    q = nc.tensor.transpose(ps[:, 4 + k % 4, NCL * t:NCL * t + NCL], ytok[0:NCL, t, P * k:P * k + P],
                                            ident[0:NCL, 0:NCL])
                q.then_inc(sem("yT_ready"), 1)
            pe.wait_ge(sem("h_split"), 3 * KT)
            for u in range(4):
                tiles(M_GLU + u, G_GLU + 2 * u, KT, 256, h_tile, L1)
            pe.wait_ge(sem("acc_taken"), G_MLP1)
            norm_sum(5)
            norm_sum(6)
            pe.wait_ge(sem("h_split"), 4 * KT)
            mlp(1, M_MLP1, G_MLP1, N_MLP1, L1)
            pe.wait_ge(sem("acc_taken"), G_MLP1 + 10 * NG)
            norm_sum(7)
            pe.wait_ge(sem("x_added"), 4 * KT)
            for r in range(4):
                for half in range(2):
                    for k in range(4):
                        q = nc.tensor.transpose(ps[:, 2 * r + half, P * k:P * k + P],
                                                xT[:, 4 * half + k, CTX + P * r:CTX + P * r + P], ident)
                    q.then_inc(sem("oT_ready"), 1)

        @block.scalar
        def _(act):
            A_ = nc.scalar.activation

            act.dma_start(consts[:, :], a["consts"][:, 0:3 * P]).then_inc(sem("const_in"), 16)
            act.dma_start(cmask[:, :], a["consts"][:, 3 * P:3 * P + SC]).then_inc(sem("const_in"), 16)
            act.dma_start(rope[:, 0:2 * SEQ], a["consts"][:, 3 * P + SC:]).then_inc(sem("rope_in"), 16)
            for r0, src in ((0, a["c"][0]), (8, a["c_ctx"]), (16, a["norm_g"]), (80, a["s5_glu_b"]),
                            (88, a["gqa_q_norm"]), (89, a["gqa_k_norm"])):
                names = " ".join("abc"[:len(src.shape)])
                flat = src.rearrange(f"{names} -> ({names})") if len(src.shape) > 1 else src
                v = flat.rearrange("(r n) -> r n", n=P)
                act.dma_start(rows[r0:r0 + v.shape[0], 0, :], v).then_inc(sem("rows_in"), 16)
            act.dma_start(rows[0:96, 1, :], a["ada_b"].rearrange("l n -> (l n)").rearrange("(r n) -> r n", n=P)) \
                .then_inc(sem("rows_in"), 16)

            def split_hi(m, n, mi=0, ni=0):
                act.wait_ge(sem(f"raw_landed{n % NRAW}"), 16 * (n // NRAW + 1) + ni)
                if m >= 2:
                    act.wait_ge(sem("acc_ready"), groups_after(m - 2) + 5 * mi)
                A_(w_hi[:, m % 2, :], raw[:, n % NRAW, :], ACT.Copy).then_inc(sem("w_hi_done"), 1)

            def norm_rstd(n, src_ready):
                ch = norm_chunks(n)
                w = sum(c[1] for c in ch)
                for k in range(KT):
                    src_ready(k)
                    if k >= 2:
                        act.wait_ge(sem("sq_used"), KT * n + k - 1)
                    A_(sq[:, k % 2, 0:w], norm_src(n, k), ACT.Square).then_inc(sem("sq_ready"), 1)
                act.wait_ge(sem("sq_used"), KT * (n + 1))
                A_(by_chunk(rst[:, 0:w], ch), banks(0, ch), ACT.Ln, bias=epsc[:, :], scale=1.0 / D) \
                    .then_inc(sem("rln_done"), 1)
                act.wait_ge(sem("rln_done"), n + 1)
                A_(rst[:, 0:w], rst[:, 0:w], ACT.Exp, scale=-0.5).then_inc(sem("rstd_ready"), 1)

            def h_heads(base, w):
                for k in range(KT):
                    act.wait_ge(sem("h_full"), base + k + 1)
                    A_(h_hi[:, k, 0:w], tmp[:, k % 2, 0:w], ACT.Copy).then_inc(sem("h_hi_done"), 1)

            for r in range(6):
                if r == 0:
                    act.wait_ge(sem("cols_taken"), 1)
                    A_(sil[:, :, :].rearrange("p v k -> p (v k)"), cols[:, 0:16], ACT.Silu).then_inc(sem("sil_ready"), 1)
                act.wait_ge(sem("xT_ready"), 2 * r + 1)
                A_(xT[:, 0:4, P * r:P * r + P], ps[:, (2 * r) % 6, :].rearrange("p (k t) -> p k t", k=4), ACT.Copy) \
                    .then_inc(sem("xT_act"), 1)
            act.wait_ge(sem("eps_set"), 1)

            def x_there(k):
                if k == 0:
                    act.wait_ge(sem("xT_act"), 6)
                    act.wait_ge(sem("xT_dve"), 6)
            norm_rstd(0, x_there)
            split_hi(0, 8)
            h_heads(0, T)
            for m in range(1, 6):
                split_hi(m, 8 + m)

            def head_square(hd):
                act.wait_ge(sem("acc_taken"), hd + 1)
                if hd >= 2:
                    act.wait_ge(sem("hsum_ready"), hd - 1)
                A_(sq[:, hd % 2, :], qk[:, hd, :], ACT.Square).then_inc(sem("hsq_ready"), 1)

            act.wait_ge(sem("sq_used"), KT)
            head_square(0)
            for hd in range(HEADS + KVH):
                if hd + 1 < HEADS + KVH:
                    head_square(hd + 1)
                act.wait_ge(sem("hsum_ready"), hd + 1)
                if hd >= 2:
                    act.wait_ge(sem("q_roped"), hd - 1)
                A_(by_chunk(tmp[:, hd % 2, :], L0), banks(2 * (hd % 2), L0), ACT.Ln, bias=epsc[:, :], scale=1.0 / HD) \
                    .then_inc(sem("hln_done"), 1)
                act.wait_ge(sem("hln_done"), hd + 1)
                A_(tmp[:, hd % 2, :], tmp[:, hd % 2, :], ACT.Exp, scale=-0.5).then_inc(sem("hrstd_ready"), 1)
            act.wait_ge(sem("acc_taken"), 10)
            split_hi(6, 8 + 6 + 16)

            def softmax_exp(t):
                nk = att[t // 2][2]
                ch = L0 if nk == 6 else [(0, 256)]
                act.wait_ge(sem("nmax_ready"), t + 1)
                if t >= 2:
                    act.wait_ge(sem("pT_ready"), t - 1)
                A_(by_chunk(sq[:, t % 2, 0:P * nk], ch), banks(2 * (t % 2), ch), ACT.Exp,
                   bias=nmax[:, t % 2:t % 2 + 1], accum_out=rsum[:, t % 2:t % 2 + 1]).then_inc(sem("exp_done"), 1)

            softmax_exp(0)
            softmax_exp(1)
            for u, (hd, q0, nk) in enumerate(att):
                act.wait_ge(sem("pT_ready"), 2 * u + 2)
                if u >= 2:
                    act.wait_ge(sem("o_ready"), u - 1)
                for b in ((0, 2) if nk == 6 else (0,)):
                    q = A_(pT[:, u % 2, 2 * b:2 * b + 2, :], ps[:, 4 + b, :].rearrange("p (k t) -> p k t", k=2), ACT.Copy)
                q.then_inc(sem("pT_act"), 1)
                for t in (2 * u + 2, 2 * u + 3):
                    if t < 2 * len(att):
                        softmax_exp(t)
                act.wait_ge(sem("o_ready"), u + 1)
                A_(h_hi[:, hd, q0:q0 + 256], ps[:, 7, 0:256], ACT.Copy) \
                    .then_inc(sem("o_hi_done"), 1)
            n_wo = 8 + 6 + 16
            for u in range(1, 4):
                split_hi(6 + u, n_wo + u)
            split_hi(M_MLP0, N_MLP0)

            def y_there(g0):
                def f(k):
                    act.wait_ge(sem("acc_taken"), g0 + k + 1)
                return f

            def x_updated(base):
                def f(k):
                    act.wait_ge(sem("x_added"), base + k + 1)
                return f

            norm_rstd(1, y_there(G_WO))
            norm_rstd(2, x_updated(0))
            h_heads(KT, T)

            def mlp(l, m0, g0, n0, chunks, period):
                w = sum(c[1] for c in chunks)

                def z_tile(j, group, g, gi=0, zi=0, wi=0, static=True):
                    z = 2 * NG * l + 2 * group + j
                    act.wait_ge(sem("acc_ready"), g + 1 + gi)
                    if group >= 1:
                        act.wait_ge(sem("acc_taken"), g - (9 if group >= 2 else 1) + gi)
                    A_(by_chunk(sq[:, j, 0:w], chunks), ring(g, chunks), ACT.Relu).then_inc(sem("relu_done"), 1)
                    act.wait_ge(sem("acc_taken"), g + 1 + gi)
                    if group >= 2:
                        act.wait_ge(sem("acc_ready"), groups_after(m0 + 2 * group - 2) + 5 * wi)
                    A_(a_hi[:, 2 * (group % 2) + j, 0:w], tmp[:, j, 0:w], ACT.Copy).then_inc(sem("a_hi_done"), 1)

                def z_unit(group, g, gi=0, zi=0, wi=0, static=True):
                    for j in range(2):
                        z_tile(j, group, g + j, gi, zi, wi, static)

                def nn(c, i, loop_n):
                    return n0 + 1 + (2 * c if period == 8 else c)

                split_hi(m0 + 1, n0 + 1)
                z_unit(0, g0)

                def double(i, rel, static, last=False):
                    for st in range(2):
                        c = 2 * st
                        split_hi(m0 + 2 + c, nn(c + 1, i, 0), 4 * i, 16 * (period // 4) * i)
                        z_unit(2 * rel + st + 1, g0 + 2 + 10 * st + (20 * rel), 20 * (i - rel), 0, 4 * (i - rel), static)
                        if st == 0:
                            split_hi(m0 + 3 + c, nn(c + 2, i, 0), 4 * i, 16 * (period // 4) * i)
                        elif not last:
                            split_hi(m0 + 3 + c, n0 + 1 + period, 4 * i, 16 * (period // 4) * i)

                double(0, 0, True)
                with act.Fori(1, 6 if period == 8 else 7) as i:
                    double(i, 1, False)
                if period == 8:
                    n = n0 + 49
                    for st in range(2):
                        split_hi(m0 + 26 + 2 * st, n + 1 + 2 * st)
                        z_unit(13 + st, g0 + 122 + 10 * st)
                        split_hi(m0 + 27 + 2 * st, n + 2 + 2 * st)
                    n = n0 + 53
                else:
                    n = n0 + 29
                split_hi(m0 + 30, n + 1)
                z_unit(15, g0 + 142)
                split_hi(m0 + 31, n + 2)

            mlp(0, M_MLP0, G_MLP0, N_MLP0, L0, 8)
            norm_rstd(3, y_there(G_GLU - 8))
            norm_rstd(4, x_updated(KT))

            act.wait_ge(sem("s5_in"), 16 * 7)
            A_(dtc, dtl, ACT.Exp).then_inc(sem("dt_ready"), 1)
            act.wait_ge(sem("lam_dt"), 1)
            A_(mag, lr, ACT.Exp).then_inc(sem("mag_ready"), 1)
            act.wait_ge(sem("angles"), 1)
            A_(sn, ang, ACT.Sin)
            A_(cs, ang2, ACT.Sin).then_inc(sem("sin_ready"), 1)

            def turned(i):
                act.wait_ge(sem("turned"), i + 1)

            i = 22
            act.wait_ge(sem("turn_taken"), 22)
            for b in range(8):
                for d in range(2):
                    j = 2 * b + d
                    act.wait_ge(sem("wT_ready"), j + 1)
                    if j >= 1:
                        act.wait_ge(sem("bu_ready"), j)
                    A_(wT[:, :, :], ps[:, 0:2, :].rearrange("p a (b n) -> p (a b) n", n=P), ACT.Copy) \
                        .then_inc(sem("wT_taken"), 1)
                for h in range(4):
                    act.wait_ge(sem("ml_ready"), 4 * b + h + 1)
                    if h == 0 and b >= 1:
                        act.wait_ge(sem("yl_ready"), 2 * b)
                    src = ps[:, 5 + h % 2, :].rearrange("p (t g c) -> p t g c", t=4, g=4)[:, :, :, 0:SC]
                    dst = ml[:, 4 * (h // 2):4 * (h // 2) + 4, 4 * (h % 2):4 * (h % 2) + 4, :] \
                        .rearrange("p g t c -> p t g c")
                    A_(dst, src, ACT.Copy).then_inc(sem("ml_taken"), 1)

            for k in range(KT):
                act.wait_ge(sem("yT_ready"), k + 1)
                A_(ybuf[:, k, 0:SEQ], ps[:, 4 + k % 4, :], ACT.Gelu_apprx_tanh).then_inc(sem("g_ready"), 1)
                act.wait_ge(sem("g_ready"), k + 1)
                A_(h_hi[:, k, 0:SEQ], ybuf[:, k, 0:SEQ], ACT.Copy).then_inc(sem("h_hi_done"), 1)
            for u in range(4):
                split_hi(M_GLU + u, N_GLU + u) if u == 0 else None
                if u + 1 < 4:
                    split_hi(M_GLU + u + 1, N_GLU + u + 1)
                else:
                    split_hi(M_MLP1, N_MLP1)
                for j in range(2):
                    g = G_GLU + 2 * u + j
                    act.wait_ge(sem("acc_ready"), g + 1)
                    if 2 * u + j >= 2:
                        act.wait_ge(sem("acc_taken"), g - 1)
                    A_(sq[:, j, 0:SEQ], ring(g, L1)[:, 0, :], ACT.Sigmoid, bias=cols[:, 80 + 2 * u + j:81 + 2 * u + j]) \
                        .then_inc(sem("sig_ready"), 1)
            act.wait_ge(sem("acc_taken"), G_MLP1)
            norm_rstd(5, y_there(G_GLU))
            norm_rstd(6, x_updated(2 * KT))
            h_heads(2 * KT, SEQ)
            mlp(1, M_MLP1, G_MLP1, N_MLP1, L1, 4)
            norm_rstd(7, y_there(G_MLP1 + 10 * NG - 8))
            for r in range(4):
                act.wait_ge(sem("oT_ready"), 2 * r + 1)
                A_(xtok[:, r, 0:512], ps[:, 2 * r, :], ACT.Copy).then_inc(sem("o_act"), 1)

        @block.vector
        def _(dve):
            TT = nc.vector.tensor_tensor
            STT = nc.vector.scalar_tensor_tensor
            TS = nc.vector.tensor_scalar
            CP = nc.vector.tensor_copy
            linked = [0]

            def link(q):
                linked[0] += 1
                q.then_inc(sem("dve_step"), 1)
                dve.wait_ge(sem("dve_step"), linked[0])

            def split_lo(m, mi=0):
                dve.wait_ge(sem("w_hi_done"), m + 1 + mi)
                raw_n = unit_of_split(m)
                for p in range(2):
                    s = slice(1024 * p, 1024 * p + 1024)
                    q = TT(w_lo[:, m % 2, s], raw[:, raw_n % NRAW, s], w_hi[:, m % 2, s].bitcast(F32), ALU.subtract)
                q.then_inc(sem("w_split"), 1)

            def mods(l, j, c0):
                b = adab[:, 48 * l + 8 * j:48 * l + 8 * j + 8].unsqueeze(2).to_broadcast([P, KT, 2])
                q = TT(mod[:, l, j, :, :], ps[:, 7, MODC + 16 * j:MODC + 16 * j + 16].rearrange("p (k v) -> p k v", v=2),
                       b, ALU.add)
                if j == 2 or j == 5:
                    link(q)
                    g = gain(l, 1 if j == 2 else 3)
                    q = TT(coef[:, l, 1 if j == 2 else 3, :, :], mod[:, l, j, :, :], g, ALU.mult)
                elif j == 1 or j == 4:
                    link(q)
                    q = STT(coef[:, l, 0 if j == 1 else 2, :, :], mod[:, l, j, :, :], 1.0, gain(l, 0 if j == 1 else 2),
                            ALU.add, ALU.mult)
                q.then_inc(sem("mod_ready"), 1)

            def gain(l, i):
                c0 = 16 + (4 * l + i) * KT
                return cols[:, c0:c0 + KT].unsqueeze(2).to_broadcast([P, KT, 2])

            def apply_norm(l, i, n, base, segs, x0, w, split=True):
                dve.wait_ge(sem("rstd_ready"), n + 1)

                def rest(k):
                    dve.wait_ge(sem("h_hi_done"), base + k + 1)
                    TT(h_lo[:, k, 0:w], tmp[:, k % 2, 0:w], h_hi[:, k, 0:w].bitcast(F32), ALU.subtract) \
                        .then_inc(sem("h_split"), 1)

                for k in range(KT):
                    if k >= 2 and split:
                        dve.wait_ge(sem("h_split"), base + k - 1)
                    elif k >= 2:
                        dve.wait_ge(sem("h1_ready"), k - 1)
                    link(TT(tmp[:, k % 2, 0:w], xT[:, k, x0:x0 + w], rst[:, 0:w], ALU.mult))
                    for t0, m, v in segs:
                        src = tmp[:, k % 2, t0:t0 + m]
                        dst = src
                        if not split:
                            nch = m // CH
                            c0 = 0 if v else NCC
                            dst = h1[:, k, :, c0:c0 + nch]
                            src = src.rearrange("p (t c) -> p t c", t=CH)
                        q = TS(dst, src, coef[:, l, 2 * i, k, v:v + 1], mod[:, l, 3 * i, k, v:v + 1], ALU.mult, ALU.add)
                    q.then_inc(sem("h_full" if split else "h1_ready"), 1)
                    if split and k >= 1:
                        rest(k - 1)
                if split:
                    rest(KT - 1)

            def add_branch(l, i, n, xbase, segs, x0, w):
                dve.wait_ge(sem("rstd_ready"), n + 1)
                for k in range(KT):
                    if k >= 2:
                        dve.wait_ge(sem("x_added"), xbase + k - 1)
                    for t0, m, v in segs:
                        q = STT(tmp[:, k % 2, t0:t0 + m], ybuf[:, k, t0:t0 + m], coef[:, l, 2 * i + 1, k, v:v + 1],
                                rst[:, t0:t0 + m], ALU.mult, ALU.mult)
                    link(q)
                    TT(xT[:, k, x0:x0 + w], xT[:, k, x0:x0 + w], tmp[:, k % 2, 0:w], ALU.add).then_inc(sem("x_added"), 1)

            dve.wait_ge(sem("cols_ready"), 1)
            CP(cols[:, 0:90], ps[:, 6, 0:90])
            link(CP(adab[:, :], ps[:, 6, 128:224]))
            TS(cols[:, 89:90], cols[:, 89:90], HD ** -0.5, None, ALU.mult).then_inc(sem("cols_taken"), 1)
            for r in range(6):
                dve.wait_ge(sem("xT_ready"), 2 * r + 2)
                CP(xT[:, 4:8, P * r:P * r + P], ps[:, (2 * r + 1) % 6, :].rearrange("p (k t) -> p k t", k=4)) \
                    .then_inc(sem("xT_dve"), 1)
            dve.wait_ge(sem("ada_used"), 8)
            dve.wait_ge(sem("cols_taken"), 1)
            mods(0, 0, 0)
            mods(0, 1, 0)
            dve.wait_ge(sem("mod_ready"), 2)
            apply_norm(0, 0, 0, 0, SEG0, 0, T)
            split_lo(0)
            for u in range(6):
                if u + 1 < 6:
                    split_lo(u + 1)
                for j in range(2 if u < 5 else 6):
                    g = 2 * u + j
                    dve.wait_ge(sem("acc_ready"), g + 1)
                    if u < 5:
                        q = CP(by_chunk(qk[:, g, :], L0), ring(g, L0))
                    else:
                        q = CP(vt[:, j, :], ring(g, [(0, 256)])[:, 0, :])
                    q.then_inc(sem("acc_taken"), 1)

            dve.wait_ge(sem("rope_in"), 16)
            for hd in range(HEADS + KVH):
                qh = qk[:, hd, :]
                dve.wait_ge(sem("hrstd_ready"), hd + 1)
                g = 88 if hd < HEADS else 89
                STT(qh, qh, cols[:, g:g + 1], tmp[:, hd % 2, :], ALU.mult, ALU.mult).then_inc(sem("q_normed"), 1)
                dve.wait_ge(sem("rot_ready"), hd + 1)
                TT(tmp[:, hd % 2, 0:SEQ], ps[:, 4 + hd % 2, :], rope[:, SEQ:2 * SEQ], ALU.mult).then_inc(sem("q_sin"), 1)
                link(TT(qh[:, CTX:T], qh[:, CTX:T], rope[:, 0:SEQ], ALU.mult))
                dve.wait_ge(sem("q_sin"), hd + 1)
                TT(qh[:, CTX:T], qh[:, CTX:T], tmp[:, hd % 2, 0:SEQ], ALU.add).then_inc(sem("q_roped"), 1)
            dve.wait_ge(sem("ada_used"), 24)
            for j in range(2, 6):
                mods(0, j, 0)
            dve.wait_ge(sem("mod_ready"), 6)
            split_lo(6)

            def row_max(t):
                nk = att[t // 2][2]
                ch = L0 if nk == 6 else [(0, 256)]
                dve.wait_ge(sem("s_ready"), t + 1)
                nc.vector.tensor_reduce(nmax[:, t % 2:t % 2 + 1], banks(2 * (t % 2), ch), AX.XY, ALU.max, negate=True) \
                    .then_inc(sem("nmax_ready"), 1)

            def normalise(t):
                nk = att[t // 2][2]
                dve.wait_ge(sem("exp_done"), t + 1)
                link(nc.vector.reciprocal(rinv[:, t % 2:t % 2 + 1], rsum[:, t % 2:t % 2 + 1]))
                TS(sq[:, t % 2, 0:P * nk], sq[:, t % 2, 0:P * nk], rinv[:, t % 2:t % 2 + 1], None, ALU.mult) \
                    .then_inc(sem("p_ready"), 1)

            row_max(0)
            row_max(1)
            normalise(0)
            normalise(1)
            for u, (hd, q0, nk) in enumerate(att):
                more = u + 1 < len(att)
                if more:
                    row_max(2 * u + 2)
                    row_max(2 * u + 3)
                dve.wait_ge(sem("pT_ready"), 2 * u + 2)
                if nk == 6:
                    if u >= 2:
                        dve.wait_ge(sem("o_ready"), u - 1)
                    CP(pT[:, u % 2, 2:4, :], ps[:, 5, :].rearrange("p (k t) -> p k t", k=2)) \
                        .then_inc(sem("pT_dve"), 1)
                if more:
                    normalise(2 * u + 2)
                    normalise(2 * u + 3)
                dve.wait_ge(sem("o_hi_done"), u + 1)
                TT(h_lo[:, hd, q0:q0 + 256], ps[:, 7, 0:256],
                   h_hi[:, hd, q0:q0 + 256].bitcast(F32), ALU.subtract).then_inc(sem("o_taken"), 1)
            for u in range(4):
                split_lo(7 + u)
                for j in range(2):
                    g = G_WO + 2 * u + j
                    dve.wait_ge(sem("acc_ready"), g + 1)
                    CP(by_chunk(ybuf[:, 2 * u + j, :], L0), ring(g, L0)).then_inc(sem("acc_taken"), 1)
            add_branch(0, 0, 1, 0, SEG0, 0, T)
            apply_norm(0, 1, 2, KT, SEG0, 0, T)

            def mlp(l, m0, g0, chunks):
                w = sum(c[1] for c in chunks)

                def z_unit(group, g, gi=0, zi=0, static=True):
                    for j in range(2):
                        z = 2 * NG * l + 2 * group + j
                        if not static or group >= 1:
                            dve.wait_ge(sem("a_split"), z - 1 + zi)
                        dve.wait_ge(sem("relu_done"), z + 1 + zi)
                        STT(by_chunk(tmp[:, j, 0:w], chunks), ring(g + j, chunks), 0.0, by_chunk(sq[:, j, 0:w], chunks),
                            ALU.max, ALU.mult).then_inc(sem("acc_taken"), 1)
                        dve.wait_ge(sem("a_hi_done"), z + 1 + zi)
                        slot = 2 * (group % 2) + j
                        TT(a_lo[:, slot, 0:w], tmp[:, j, 0:w], a_hi[:, slot, 0:w].bitcast(F32), ALU.subtract) \
                            .then_inc(sem("a_split"), 1)

                def y_unit(group, g, gi=0, static=True):
                    for j in range(KT):
                        dve.wait_ge(sem("acc_ready"), g + j + 1 + gi)
                        if not static or group >= 1:
                            dve.wait_ge(sem("acc_taken"), g + j - (7 if group == NG - 1 else 9) + gi)
                        else:
                            dve.wait_ge(sem("y_zero"), l + 1)
                        y = by_chunk(ybuf[:, j, 0:w], chunks)
                        TT(y, y, ring(g + j, chunks), ALU.add).then_inc(sem("acc_taken"), 1)

                split_lo(m0 + 1)
                z_unit(0, g0)

                def double(i, rel, static, last=False):
                    for st in range(2):
                        c = 2 * st
                        o = 4 * (i - rel)
                        split_lo2(m0 + 2 + c + 4 * rel, o)
                        z_unit(2 * rel + st + 1, g0 + 2 + 10 * st + 20 * rel, 20 * (i - rel), o, static)
                        split_lo2(m0 + 3 + c + 4 * rel, o)
                        y_unit(2 * rel + st, g0 + 4 + 10 * st + 20 * rel, 20 * (i - rel), static)

                def split_lo2(m, o):
                    split_lo(m, o)

                double(0, 0, True)
                with dve.Fori(1, 6) as i:
                    double(i, 1, False)
                double(6, 6, True)
                split_lo(m0 + 30)
                z_unit(15, g0 + 142)
                split_lo(m0 + 31)
                y_unit(14, g0 + 144)
                y_unit(15, g0 + 152)

            mlp(0, M_MLP0, G_MLP0, L0)
            dve.wait_ge(sem("ada_used"), 48)
            for j in range(6):
                mods(1, j, 0)
            dve.wait_ge(sem("mod_ready"), 12)
            add_branch(0, 1, 3, KT, SEG0, 0, T)
            dve.wait_ge(sem("x_added"), 2 * KT)

            dve.wait_ge(sem("s5_in"), 16 * 7)
            dve.wait_ge(sem("dt_ready"), 1)
            TS(lr, are, dtc, None, ALU.mult)
            TS(li, aim, dtc, None, ALU.mult).then_inc(sem("lam_dt"), 1)
            dve.wait_ge(sem("lam_dt"), 1)
            link(TS(kk, li, 1.0 / TWO_PI, MAGIC, ALU.mult, ALU.add))
            link(TS(kk, kk, -MAGIC, None, ALU.add))
            link(STT(t0_, kk, -PI_HI, li, ALU.mult, ALU.add))
            link(STT(t1_, kk, -PI_MID, t0_, ALU.mult, ALU.add))
            link(STT(t2_, kk, -PI_LO, t1_, ALU.mult, ALU.add))
            link(TS(ang, t2_, 3.1415925, -3.1415925, ALU.min, ALU.max))
            link(STT(t0_, ang, -1.0, ang, ALU.mult, ALU.max))
            TS(ang2, t0_, -1.0, math.pi / 2, ALU.mult, ALU.add).then_inc(sem("angles"), 1)
            dve.wait_ge(sem("mag_ready"), 1)
            dve.wait_ge(sem("sin_ready"), 1)
            pw9 = lambda r, e: flat_tok[:, (r * 9 + e) * P:(r * 9 + e) * P + NP]
            nc.vector.memset(pw9(0, 0), 1.0)
            nc.vector.memset(pw9(1, 0), 0.0)
            TT(pw9(0, 1), mag, cs, ALU.mult)
            link(TT(pw9(1, 1), mag, sn, ALU.mult))
            ar, ai = pw9(0, 1), pw9(1, 1)
            for e in range(2, 9):
                TT(t0_, pw9(0, e - 1), ar, ALU.mult)
                TT(t1_, pw9(1, e - 1), ai, ALU.mult)
                TT(t2_, pw9(0, e - 1), ai, ALU.mult)
                link(TT(den, pw9(1, e - 1), ar, ALU.mult))
                TT(pw9(0, e), t0_, t1_, ALU.subtract)
                link(TT(pw9(1, e), t2_, den, ALU.add))
            pw2 = flat_tok[:, 0:18 * P].rearrange("p (n u s) -> p n u s", u=2, s=NP)
            CP(pw2[:, :, 1, :], pw2[:, :, 0, :])
            TS(arm1, ar, -1.0, None, ALU.add)
            TT(t0_, are, are, ALU.mult)
            link(TT(t1_, aim, aim, ALU.mult))
            link(TT(t2_, t0_, t1_, ALU.add))
            link(nc.vector.reciprocal(den, t2_))
            TT(t0_, arm1, are, ALU.mult)
            link(TT(t1_, ai, aim, ALU.mult))
            link(TT(t2_, t0_, t1_, ALU.add))
            link(TT(cre, t2_, den, ALU.mult))
            TT(t0_, ai, are, ALU.mult)
            link(TT(t1_, arm1, aim, ALU.mult))
            link(TT(t2_, t0_, t1_, ALU.subtract))
            link(TT(cim, t2_, den, ALU.mult))
            br = S[:, 0:1024].rearrange("p (s c) -> p s c", s=NP)
            bi = S[:, 1024:2048].rearrange("p (s c) -> p s c", s=NP)
            bb = S[:, 2048:5120].rearrange("p (r s c) -> p r s c", r=3, s=NP)
            f1 = S[:, 5120:6144].rearrange("p (s c) -> p s c", s=NP)
            wide = lambda v: v.unsqueeze(2).to_broadcast([P, NP, SC])
            link(TT(bb[:, 1, :, :], br, wide(cre), ALU.mult))
            link(TT(f1, bi, wide(cim), ALU.mult))
            link(TT(bb[:, 1, :, :], bb[:, 1, :, :], f1, ALU.subtract))
            link(TT(bb[:, 2, :, :], br, wide(cim), ALU.mult))
            link(TT(f1, bi, wide(cre), ALU.mult))
            link(TT(bb[:, 2, :, :], bb[:, 2, :, :], f1, ALU.add))
            TS(S[:, 2048:3072], S[:, 4096:5120], -1.0, None, ALU.mult)
            c3 = S[:, C3:C3 + 3072].rearrange("p (c r s) -> p c r s", r=3, s=NP)
            cr, ci = (S[:, 6144 + 1024 * r:7168 + 1024 * r].rearrange("p (c s) -> p c s", s=NP) for r in range(2))
            CP(c3[:, :, 0, :], cr)
            TS(c3[:, :, 1, :], ci, -1.0, None, ALU.mult)
            TS(c3[:, :, 2, :], cr, -1.0, None, ALU.mult)
            nc.vector.memset(pv[:, 2 * GROUPS * SC:], 0.0).then_inc(sem("prep_ready"), 1)

            i = 0

            def taken(q):
                q.then_inc(sem("turn_taken"), 1)

            for r in range(2):
                for e0, ne in ((0, 4), (4, 4), (8, 1)):
                    dve.wait_ge(sem("turned"), i + 1)
                    taken(CP(powT[:, r, e0:e0 + ne, :], ps[:, i % 4, 0:P * ne].rearrange("p (e n) -> p e n", n=P)))
                    i += 1
            for dst in (pw[:, :, :], qw[:, :, :], pv[:, 0:2 * GROUPS * SC].rearrange("p (g c) -> p g c", c=SC), qv[:, :, :]):
                for c0 in range(0, SC, 4):
                    dve.wait_ge(sem("turned"), i + 1)
                    taken(CP(dst[:, :, c0:c0 + 4], ps[:, i % 4, :].rearrange("p (c n) -> p n c", c=4)))
                    i += 1
            dve.wait_ge(sem("turn_taken"), i)
            for g2 in range(2):
                p = slice(64 * g2, 64 * g2 + 64)
                for r in range(2):
                    src = powT[p, r, 8, :].rearrange("p (d q g) -> p d q g", d=2, g=2)[:, :, :, g2]
                    if r == 0:
                        CP(a8[p, 0, :, 0, :], src)
                        CP(a8[p, 0, :, 1, :], src)
                    else:
                        TS(a8[p, 1, :, 0, :], src, -1.0, None, ALU.mult)
                        q = CP(a8[p, 1, :, 1, :], src)
            q.then_inc(sem("prep_over"), 1)

            apply_norm(1, 0, 4, 0, SEG0, 0, T, split=False)
            dve.wait_ge(sem("h1_ready"), KT)
            for t in range(CH):
                for half in range(2):
                    dve.wait_ge(sem("turned"), i + 1)
                    taken(CP(htok[0:NCH, 32 * half:32 * half + 32, t, :],
                             ps[0:NCH, i % 4, :].rearrange("p (g c) -> p g c", c=SC)))
                    i += 1
            for b in range(16):
                dve.wait_ge(sem("turned"), i + 1)
                taken(CP(U[:, 4 * b:4 * b + 4, :], ps[:, i % 4, 0:4 * NCH].rearrange("p (g n) -> p g n", g=4)))
                i += 1
            dve.wait_ge(sem("turn_taken"), i)
            dve.wait_ge(sem("prep_over"), 1)
            dve.wait_ge(sem("d_in"), 16 * 4)
            nc.vector.memset(Sv[:, 0, :, :, :], 0.0).then_inc(sem("s_zero"), 1)

            def products(j, b, d, par, inward, dst):
                if j:
                    dve.wait_ge(sem("wp_sum"), j)
                link(TT(mul_buf(sq), per_t(par, b, d), power(0, b, d, inward), ALU.mult))
                dve.wait_ge(sem("m2_ready"), j + 1)
                TT(dst, mul_buf(sq), mul_buf(tmp), ALU.add).then_inc(sem("wp_sum"), 1)

            pvv = pv[:, 0:2 * GROUPS * SC].rearrange("p (g c) -> p g c", c=SC)
            wp4 = wp[:, :, :].rearrange("p g (t c) -> p g t c", t=CH)
            for b in range(8):
                for d in range(2):
                    j = 2 * b + d
                    if j >= 1:
                        dve.wait_ge(sem("kf_ready"), j)
                    products(j, b, d, pw, True, wp4)
                    dve.wait_ge(sem("bu_ready"), j + 1)
                    for r in range(2):
                        src = ps[:, 3 + r, 0:4 * NCH].rearrange("p (q n) -> p n q", n=NCH)
                        q0 = 4 * b
                        if d == 0:
                            q = CP(Sv[:, 1:1 + NCH, 0, r, q0:q0 + 4], src)
                        else:
                            CP(Sv[:, 1:1 + NCC, 1, r, q0:q0 + 4][:, ::-1, :], src[:, 0:NCC, :])
                            q = CP(Sv[:, 1 + NCC:1 + NCH, 1, r, q0:q0 + 4][:, ::-1, :], src[:, NCC:NCH, :])
                    q.then_inc(sem("bu_taken"), 1)
                dve.wait_ge(sem("kf_ready"), 2 * b + 2)
                if b >= 1:
                    dve.wait_ge(sem("ml_ready"), 4 * b)
                kp = ps[:, 2, :].rearrange("p (d q n) -> p d q n", d=2, q=2)
                CP(kf[:, :, 0:P], kp[:, 0, :, :])
                CP(kf[:, :, P:15 * SC], kp[:, 1, :, SC:P])
                for qd in range(2):
                    q = TS(sdm[:, qd, :], cmask[:, :], dcol[:, 2 * b + qd:2 * b + qd + 1], None, ALU.mult)
                link(q)
                link(TT(kf[:, :, 7 * SC:8 * SC], kf[:, :, 7 * SC:8 * SC], kp[:, 1, :, 0:SC], ALU.add))
                TT(kf[:, :, 7 * SC:8 * SC], kf[:, :, 7 * SC:8 * SC], sdm[:, :, :], ALU.add).then_inc(sem("kf_taken"), 1)
                for hf in range(2):
                    dve.wait_ge(sem("yl_ready"), 2 * b + hf + 1)
                    g0 = SC * (8 * b + 4 * hf)
                    CP(ytok[0:NCL, :, g0:g0 + 4 * SC].rearrange("p t (g c) -> p g t c", g=4),
                       ps[0:NCL, 7, :].rearrange("p (g t c) -> p g t c", g=4, t=CH)).then_inc(sem("yl_taken"), 1)

            dve.wait_ge(sem("bu_taken"), 16)
            dve.wait_ge(sem("s_zero"), 1)
            t1 = rst[:, 0:P].rearrange("p (d r q) -> p d r q", d=2, r=2)
            t2 = rst[:, P:2 * P].rearrange("p (d r q) -> p d r q", d=2, r=2)

            def scan_step(i, c):
                prev, cur = Sv[:, i, :, :, :], Sv[:, i + 1, :, :, :]
                prev2 = [Sv[:, i, :, 1 - r, :] for r in range(2)]
                TT(t1, a8[:, 0], prev, ALU.mult).then_inc(sem("scan"), 1)
                for r in range(2):
                    q = TT(t2[:, :, r, :], a8[:, 1, :, r, :], prev2[r], ALU.mult)
                q.then_inc(sem("scan"), 1)
                dve.wait_ge(sem("scan"), c + 1)
                TT(cur, cur, t1, ALU.add).then_inc(sem("scan"), 1)
                dve.wait_ge(sem("scan"), c + 3)
                TT(cur, cur, t2, ALU.add).then_inc(sem("scan"), 1)
                dve.wait_ge(sem("scan"), c + 4)

            with dve.Fori(0, NCH) as i:
                scan_step(i, 4 * i)

            for d in range(2):
                for g2 in range(2):
                    for r in range(2):
                        src = Sv[64 * g2:64 * g2 + 64, NCC:NCH, d, r, :]
                        if d == 1:
                            src = src[:, ::-1, :]
                        dst = sst[64 * r:64 * r + 64, d, :, :].rearrange("p (q g) n -> p n q g", g=2)[:, :, :, g2]
                        CP(dst, src).then_inc(sem("restacked"), 1)
            for b in range(8):
                for d in range(2):
                    j = 16 + 2 * b + d
                    if b >= 1:
                        dve.wait_ge(sem("ys_ready"), 2 * b)
                    products(j, b, d, pvv, False, xv[:, d, :, :].rearrange("p g (t c) -> p g t c", t=CH))
                for hf in range(2):
                    dve.wait_ge(sem("ys_ready"), 2 * b + hf + 1)
                    g0 = SC * (8 * b + 4 * hf)
                    y = ytok[0:NCL, :, g0:g0 + 4 * SC].rearrange("p t (g c) -> p g t c", g=4)
                    dve.wait_ge(sem("yl_taken"), 16)
                    TT(y, y, ps[0:NCL, (2 * b + hf) % 4, :].rearrange("p (g t c) -> p g t c", g=4, t=CH), ALU.add) \
                        .then_inc(sem("ys_taken"), 1)

            for k in range(KT):
                dve.wait_ge(sem("h_hi_done"), 2 * KT + k + 1)
                TT(h_lo[:, k, 0:SEQ], ybuf[:, k, 0:SEQ], h_hi[:, k, 0:SEQ].bitcast(F32), ALU.subtract) \
                    .then_inc(sem("h_split"), 1)
            split_lo(M_GLU)
            for u in range(4):
                split_lo(M_GLU + u + 1)
                for j in range(2):
                    g = G_GLU + 2 * u + j
                    dve.wait_ge(sem("sig_ready"), 2 * u + j + 1)
                    TT(ybuf[:, 2 * u + j, 0:SEQ], ybuf[:, 2 * u + j, 0:SEQ], sq[:, j, 0:SEQ], ALU.mult) \
                        .then_inc(sem("acc_taken"), 1)
            seg = [(0, SEQ, 0)]
            add_branch(1, 0, 5, 2 * KT, seg, CTX, SEQ)
            apply_norm(1, 1, 6, 3 * KT, seg, CTX, SEQ)
            mlp(1, M_MLP1, G_MLP1, L1)
            add_branch(1, 1, 7, 3 * KT, seg, CTX, SEQ)
            for r in range(4):
                dve.wait_ge(sem("oT_ready"), 2 * r + 2)
                CP(xtok[:, r, 512:1024], ps[:, 2 * r + 1, :]).then_inc(sem("o_dve"), 1)


_INS = ["x", "c", "ctx", "c_ctx", "ada_w", "ada_b", "norm_g", "mlp_w1", "mlp_w2", "gqa_w_qkv", "gqa_q_norm",
        "gqa_k_norm", "gqa_w_o", "s5_a_re", "s5_a_im", "s5_log_dt", "s5_b_re", "s5_b_im", "s5_c_re", "s5_c_im",
        "s5_d", "s5_glu_w", "s5_glu_b"]


def shape_constants():
    ident = np.eye(P, dtype=np.float32)
    ones = np.ones((P, P), np.float32)
    rot = np.zeros((P, P), np.float32)
    for m in range(P):
        if (m // 32) % 2 == 0:
            rot[m + 32, m] = -1.0
        else:
            rot[m - 32, m] = 1.0
    mask = (np.arange(P)[:, None] % 32 == np.arange(SC)[None, :]).astype(np.float32)
    half = HD // 2
    inv = (1.0 / (10000.0 ** (np.arange(0, half, 2, dtype=np.float32) / half))).astype(np.float32)
    tok = (np.arange(NCL)[None, :] * CH + np.arange(CH)[:, None]).reshape(-1)
    ang = np.concatenate([np.outer(np.tile(inv, 2), (tok // 64).astype(np.float32)),
                          np.outer(np.tile(inv, 2), (tok % 64).astype(np.float32))]).astype(np.float32)
    return np.concatenate([ident, ones, rot, mask, np.cos(ang), np.sin(ang)], axis=1).astype(np.float32)


def kernel(**inputs):
    import numpy as _np
    import concourse.bacc as _bacc
    from concourse import mybir as _mybir
    from concourse.bass_utils import run_bass_kernel_spmd as _run

    nc = _bacc.Bacc("TRN2", target_bir_lowering=False, num_devices=1)
    arrays, args = {}, {}
    for name in _INS + ["consts"]:
        v = shape_constants() if name == "consts" else _np.ascontiguousarray(inputs[name])
        arrays[f"in_{name}"] = v
        args[name] = nc.dram_tensor(f"in_{name}", v.shape, _mybir.dt.from_np(v.dtype), kind="ExternalInput").ap()
    out = nc.dram_tensor("out_0", (1, SEQ, D), F32, kind="ExternalOutput").ap()
    build(nc, args, out)
    r = _run(nc, [arrays], core_ids=[0])
    return r.results[0]["out_0"]
```

```python
import math
from contextlib import ExitStack

import numpy as np

import concourse.bass as bass
from concourse import mybir

F32 = mybir.dt.float32
F32R = mybir.dt.float32r
ACT = mybir.ActivationFunctionType
ALU = mybir.AluOpType
AX = mybir.AxisListType

P = 128
D = 1024
KT = D // P
SEQ, CTX = 512, 256
T = CTX + SEQ
CH = 8
NCC, NCL = CTX // CH, SEQ // CH
NCH = NCC + NCL
FF = 4 * D
EPS = 1e-6
HD = 128
HEADS, KVH = 8, 2
GROUPS, SC = 64, 16
NP = 64
UNIT = 2048
NRAW = 4
TWO_PI = 2 * math.pi
SCAN_INCS = 6
MAGIC = 1.5 * 2 ** 23
PI_HI, PI_MID = 6.28125, 0.0019350051879882812
C3 = 8192
PI_LO = TWO_PI - PI_HI - PI_MID


def build(nc, a, out):
    ctx = ExitStack()
    with ctx:
        sems = {}

        def sem(name):
            if name not in sems:
                sems[name] = ctx.enter_context(nc.semaphore(name))
            return sems[name]

        def sb(stack, name, shape, dt=F32):
            return stack.enter_context(nc.sbuf_tensor(name, shape, dt))

        ps = ctx.enter_context(nc.psum_tensor("ps", [P, 8, 512], F32))
        xT = sb(ctx, "xT", [P, KT, T])
        sq = sb(ctx, "sq", [P, 2, T])
        tmp = sb(ctx, "tmp", [P, 2, T])
        rst = sb(ctx, "rst", [P, T])
        consts = sb(ctx, "squares_rot", [P, 3 * P])
        ident, ones, rotm = consts[:, 0:P], consts[:, P:2 * P], consts[:, 2 * P:3 * P]
        cmask = sb(ctx, "cmask", [P, SC])
        dcol = sb(ctx, "dcol", [P, SC])
        epsc = sb(ctx, "epsc", [P, 1])
        rows = sb(ctx, "rows", [96, 2, P])
        cols = sb(ctx, "cols", [P, 96])
        adab = sb(ctx, "adab", [P, 96])
        mod = sb(ctx, "mod", [P, 2, 6, KT, 2])
        coef = sb(ctx, "coef", [P, 2, 4, KT, 2])
        nmax = sb(ctx, "nmax", [P, 2])
        rsum = sb(ctx, "rsum", [P, 2])
        rinv = sb(ctx, "rinv", [P, 2])
        q_rms = sb(ctx, "q_rms", [P, 6 * HEADS])

        A = ExitStack()
        sil = sb(A, "sil", [P, KT, 32])
        raw = sb(A, "raw", [P, NRAW, UNIT])
        h_hi = sb(A, "h_hi", [P, KT, T], F32R)
        h_lo = sb(A, "h_lo", [P, KT, T], F32R)
        w_hi = sb(A, "w_hi", [P, 2, UNIT], F32R)
        w_lo = sb(A, "w_lo", [P, 2, UNIT], F32R)
        with ExitStack() as s:
            xtok = sb(s, "xtok", [P, 6, D])
        with ExitStack() as s:
            qk = sb(s, "qk", [P, HEADS + KVH, T])
            vt = sb(s, "vt", [P, 6, KVH * HD])
            pT = sb(s, "pT", [P, 2, 6, 256])
            rope = pT[:, :, :, :].rearrange("p a b c -> p (a b c)")
        with ExitStack() as s:
            ybuf = sb(s, "ybuf", [P, KT, T])
            a_hi = sb(s, "a_hi", [P, 4, T], F32R)
            a_lo = sb(s, "a_lo", [P, 4, T], F32R)
        A.close()
        with ExitStack() as s:
            ytok = sb(s, "ytok", [P, 8, CH, P])
            pv = sb(s, "pv", [P, 2 * GROUPS * SC + SC])
            qv = sb(s, "qv", [P, 2 * GROUPS, SC])
            powT = sb(s, "powT", [P, 2, 9, P])
            a8 = sb(s, "a8", [P, 2, 2, 2, 32])
            S = sb(s, "S", [P, 97 * P])
            with ExitStack() as s1:
                U = sb(s1, "U", [P, GROUPS, NCH])
                pw = sb(s1, "pw", [P, 2 * GROUPS, SC])
                qw = sb(s1, "qw", [P, 2 * GROUPS, SC])
                wp = sb(s1, "wp", [P, 8, P])
                wT = sb(s1, "wT", [P, 8, P])
                ml = sb(s1, "ml", [P, 8, CH, SC])
                sdm = sb(s1, "sdm", [P, 16, SC])
            with ExitStack() as s1:
                sst = sb(s1, "sst", [P, 2, GROUPS, NCL])
                xv = sb(s1, "xv", [P, 2, 2, 8, P])
        flat_tok = ytok[:, :, :, :].rearrange("p b t n -> p (b t n)")
        mod_cols = mod[:, :, :, :, :].rearrange("p l j k v -> p (l j k v)")
        htok = flat_tok.rearrange("p (g t c) -> p g t c", g=GROUPS, t=CH)
        Sv = S[:, :].rearrange("p (i d r q) -> p i d r q", d=2, r=2, q=32)
        h1 = S[:, 0:KT * T].rearrange("p (k t c) -> p k t c", k=KT, t=CH)

        units = []

        def square_units(w, n0, n):
            v = w.rearrange("(k p) n -> p k n", p=P)
            return [(True, v[:, :, n0 + 256 * i:n0 + 256 * (i + 1)]) for i in range(n)]

        def ada_units(l, j0, j1):
            v = a["ada_w"][l].rearrange("(k p) n -> p k n", p=P)
            return [(False, v[:, :, 256 * i:256 * (i + 1)]) for i in range(4 * j0, 4 * j1)]

        qkv_units = square_units(a["gqa_w_qkv"][0], 0, 6)
        first = ada_units(0, 0, 2)
        for u in range(4):
            first += [qkv_units[u]] + ada_units(0, 2 + u, 3 + u)
        first += qkv_units[4:] + square_units(a["gqa_w_o"][0], 0, 4)

        seq = []
        for hd in range(HEADS + KVH):
            seq.append(("head", hd))
            if hd:
                seq.append(("turn", hd - 1))
            if 1 <= hd <= HEADS:
                seq.append(("cols", 4 + hd - 1))
            if hd < HEADS:
                seq.append(("rows", 4 + hd))
        seq += [("squares", HEADS), ("v", 0), ("turn", HEADS + 1), ("squares", HEADS + 1)]
        seq += [("v", r) for r in range(1, 6)]
        NG = FF // 256
        w1v = [a["mlp_w1"][l].rearrange("(k p) (g n) -> g p k n", p=P, n=256) for l in range(2)]
        w2v = [a["mlp_w2"][l].rearrange("(g k p) n -> g p k n", p=P, k=2) for l in range(2)]
        adav = a["ada_w"][1].rearrange("(k p) (u n) -> u p k n", p=P, n=256)
        glu = square_units(a["s5_glu_w"][0], 0, 4)

        def slot_view(n, k):
            return raw[:, n % NRAW, :].rearrange("p (k n) -> p k n", k=k)

        N_MLP0 = len(first)
        M_MLP0 = sum(s for s, _ in first)
        N_GLU = N_MLP0 + 2 * NG + 24
        M_GLU = M_MLP0 + 2 * NG
        N_MLP1 = N_GLU + len(glu)
        M_MLP1 = M_GLU + len(glu)
        G_WO = len(seq)
        G_MLP0 = G_WO + 8
        G_GLU = G_MLP0 + 10 * NG + 24
        G_MLP1 = G_GLU + 8
        assert G_MLP0 % 4 == 0 and G_MLP1 % 4 == 0
        ADA_STEPS = 12

        def step_base(l, i):
            g = (G_MLP0, G_MLP1)[l] + 2 + 10 * i
            return g + 2 * min(i, ADA_STEPS) if l == 0 else g

        def g_hidden(l, group, j=0):
            return j + (step_base(l, group - 1) if group else (G_MLP0, G_MLP1)[l])

        def g_rows(i):
            return step_base(0, i) + 2

        def g_cols(i):
            return step_base(0, i) + 7

        def g_out(l, i, j):
            g = step_base(l, i) + j
            if i == NG - 1:
                return g
            return g + 2 + ((1 if j < 4 else 2) if l == 0 and i < ADA_STEPS else 0)

        def double_groups(l):
            return 24 if l == 0 else 20

        def groups_after(m):
            for l, m0 in ((1, M_MLP1), (0, M_MLP0)):
                c = m - m0
                if 0 <= c < 2 * NG:
                    if c == 2 * NG - 1:
                        return g_out(l, NG - 1, KT - 1) + 1
                    if c == 0 or c % 2:
                        return g_hidden(l, (c + 1) // 2, 1) + 1
                    return g_out(l, c // 2 - 1, KT - 1) + 1
            if m >= M_GLU:
                return G_GLU + 2 * (m - M_GLU + 1)
            if m < 5:
                return seq.index(("head", 2 * m + 1)) + 1
            return G_WO + 2 * (m - 5)

        def unit_of_split(m):
            if m < M_MLP0:
                return [n for n, (s, _) in enumerate(first) if s][m]
            if m < M_GLU:
                c = m - M_MLP0
                return N_MLP0 + (0 if c == 0 else 2 * c - 1 if c <= 24 else c + 24)
            return N_GLU + m - M_GLU

        def unit_of_ada(u):
            return [n for n, (s, _) in enumerate(first) if not s][u]

        L0 = [(0, 384), (384, 384)]
        L1 = [(0, 512)]
        SEG0 = [(0, CTX, 1), (CTX, SEQ, 0)]

        def banks(b, chunks, parts=P):
            n = chunks[0][1]
            return ps[0:parts, b:b + len(chunks), 0:n]

        def ring(g, chunks):
            return banks(2 * (g % 4), chunks)

        def by_chunk(ap, chunks):
            return ap.rearrange("p (c n) -> p c n", c=len(chunks))

        def row_buf(s):
            return tmp[:, s % 2, 0:512] if s < 4 else rst[:, 0:512]

        def norm_src(n, k):
            if n in (0, 2):
                return xT[:, k, :]
            if n in (1, 3):
                return ybuf[:, k, :]
            if n == 4:
                return xT[:, k, :]
            if n == 6:
                return xT[:, k, CTX:T]
            return ybuf[:, k, 0:SEQ]

        def norm_chunks(n):
            return L0 if n < 5 else L1

        def mul_buf(t):
            return t[:, :, :].rearrange("p a b -> p (a b)")[:, 0:1024].rearrange("p (g t c) -> p g t c", g=8, t=CH)

        def per_t(t, b, d):
            g0 = d * GROUPS + 8 * b
            return t[:, g0:g0 + 8, :].unsqueeze(2).to_broadcast([P, 8, CH, SC])

        def power(r, b, d, inward):
            g0 = d * GROUPS + 8 * b
            lo = 0 if inward else 1
            v = powT[:, r, lo:lo + 8, g0:g0 + 8]
            if (d == 0) == inward:
                v = powT[:, r, lo:lo + 8, g0:g0 + 8][:, ::-1, :]
            return v.rearrange("p t g -> p g t").unsqueeze(3).to_broadcast([P, 8, CH, SC])

        def kernels(b):
            return flat_tok[:, 1024 * b:1024 * b + 30 * SC].rearrange("p (q n) -> p q n", q=2)

        def lag0_of_backward(b):
            return kernel_bank(b).rearrange("p (d q n) -> p d q n", d=2, q=2)[:, 1, :, 0:SC]

        def kernel_bank(b):
            return ps[:, (2, 5)[b % 2], :]

        POOL_BLOCKS = 3

        def xv_tile(b, d):
            if b < 2:
                return xv[:, b, d, :, :]
            if b == 2:
                return xT[:, :, P * d:P * d + P]
            return S[:, 1024 * (2 * (b - 3) + d):1024 * (2 * (b - 3) + d) + 1024].rearrange("p (g n) -> p g n", g=8)

        def out_half(b, hf):
            return ytok[0:NCL, b, :, 4 * SC * hf:4 * SC * hf + 4 * SC].rearrange("p t (g c) -> p g t c", g=4)

        def xv_block(b, d):
            return xv_tile(b, d).rearrange("p g (t c) -> p g t c", t=CH)

        def pow_src(r, e):
            return flat_tok[:, (r * 9 + e) * P:(r * 9 + e + 1) * P]

        def bc_src(lo, is_b, c):
            if is_b:
                v = S[:, 2048:2048 + 3072].rearrange("p (r s c) -> p r s c", r=3, s=NP)
                return v[:, lo:lo + 2, :, c].rearrange("p r s -> p (r s)")
            return S[:, C3 + 192 * c + NP * lo:C3 + 192 * c + NP * lo + P]

        att = [(hd, q0, nk) for hd in range(HEADS) for q0, nk in ((0, 2), (CTX, 6), (CTX + 256, 6))]

        def q_scale(t):
            hd, q0, _ = att[t // 2]
            c = 6 * hd + q0 // P + t % 2
            return q_rms[:, c:c + 1]

        def wide_units(u):
            return sum(nk == 6 for _, _, nk in att[:u])

        def tile64(i):
            return S[:, 11456 + 64 * i:11456 + 64 * (i + 1)]
        are, aim, dtl, dtc = S[:, 11264:11328], S[:, 11328:11392], S[:, 11392:11393], S[:, 11393:11394]
        lr, li, mag, ang, ang2, sn, cs, t0_, t1_, t2_, den, cre, cim, arm1, kk = (tile64(i) for i in range(15))

        def restack(eng, copy, d, g2, r):
            eng.wait_ge(sem("scan"), SCAN_INCS * NCH)
            eng.wait_ge(sem("yl_ready"), 16)
            src = Sv[64 * g2:64 * g2 + 64, NCC:NCH, d, r, :]
            if d == 1:
                src = src[:, ::-1, :]
            dst = sst[64 * r:64 * r + 64, d, :, :].rearrange("p (q g) n -> p n q g", g=2)[:, :, :, g2]
            copy(dst, src).then_inc(sem("restacked" if eng is nc.vector else "restacked_act"), 1)

        block = ctx.enter_context(nc.Block())

        @block.sync
        def _(sp):
            def x_rows(t, is_ctx):
                src = a["ctx" if is_ctx else "x"][0].rearrange("(j t) n -> t j n", t=CH)[t]
                nch = NCC if is_ctx else NCL
                per = P // nch
                tile = t // per + (0 if is_ctx else 2)
                return tile, xtok[nch * (t % per):nch * (t % per + 1), tile, :], src

            def load(n, src, k):
                sp.dma_start(slot_view(n, k), src).then_inc(sem(f"raw_landed{n % NRAW}"), 16)

            def free_ada(u):
                if u % 2 == 0:
                    sp.wait_ge(sem("ada_used"), u // 2 + 1)
                elif u < 8:
                    sp.wait_ge(sem("rows_ready"), u // 2 + 1)
                else:
                    sp.wait_ge(sem("acc_ready"), seq.index(("rows", u // 2)) + 1)

            kinds = [s for s, _ in first]

            for is_ctx in (True, False):
                for t in range(CH):
                    tile, dst, src = x_rows(t, is_ctx)
                    sp.dma_start(dst, src).then_inc(sem(f"x_landed{tile}"), 16)
            for n, (is_split, src) in enumerate(first):
                if n >= NRAW:
                    o = n - NRAW
                    if kinds[o]:
                        sp.wait_ge(sem("w_split"), sum(kinds[:o]) + 1)
                    else:
                        free_ada(o - sum(kinds[:o]))
                load(n, src, 8)

            def free_split(m, i=0):
                sp.wait_ge(sem("w_split"), m + 1 + i)

            free_split(M_MLP0 - 4)
            load(N_MLP0, w1v[0][0], 8)
            base = N_MLP0 + 1
            m = M_MLP0 + 1
            def mlp0_slot_free(c, i, loop):
                if not loop and i == 0 and c < 4:
                    sp.wait_ge(sem("w_split"), M_MLP0 - 3 + c + 1)
                elif c % 4 == 1:
                    sp.wait_ge(sem("ada_used"), 2 * i + 12 + c // 4)
                elif c % 4 == 3:
                    if loop:
                        sp.wait_ge(sem("acc_ready"), 24 * (i - 1) + g_rows(1 + c // 4) + 1)
                    else:
                        sp.wait_ge(sem("acc_ready"), g_rows(c // 4 - 1) + 1)
                else:
                    sp.wait_ge(sem("w_split"), 4 * i + m + (c - 4) // 2 + 1)

            def mlp0_double(i, loop):
                for c in range(8):
                    mlp0_slot_free(c, i, loop)
                    step = c // 4
                    if c % 4 == 0:
                        load(base + c, w1v[0][2 * i + 1 + step], 8)
                    elif c % 4 == 2:
                        load(base + c, w2v[0][2 * i + step], 2)
                    else:
                        load(base + c, adav[4 * i + c // 2], 8)

            mlp0_double(0, False)
            with sp.Fori(1, 6) as i:
                mlp0_double(i, True)
            n = base + 48
            mm = m + 24
            tail = [(w1v[0][13], 8), (w2v[0][12], 2), (w1v[0][14], 8), (w2v[0][13], 2),
                    (w1v[0][15], 8), (w2v[0][14], 2), (w2v[0][15], 2)]
            for c, (src, k) in enumerate(tail):
                if c < 4:
                    if c == 1:
                        sp.wait_ge(sem("ada_used"), 24)
                    elif c == 3:
                        sp.wait_ge(sem("acc_ready"), g_rows(ADA_STEPS - 1) + 1)
                    else:
                        sp.wait_ge(sem("w_split"), mm - 2 + c // 2 + 1)
                else:
                    sp.wait_ge(sem("w_split"), mm + c - 4 + 1)
                load(n + c, src, k)
            assert n + 7 == N_GLU and mm + 7 == M_GLU

            sp.wait_ge(sem("x_added"), 2 * KT)
            for r, name in enumerate(("s5_b_re", "s5_b_im")):
                sp.dma_start(S[:, 1024 * r:1024 * (r + 1)],
                             a[name][0].rearrange("d g p c -> (d g) (p c)")).then_inc(sem("s5_in"), 16)
            for r, name in enumerate(("s5_c_re", "s5_c_im")):
                sp.dma_start(S[:, 6144 + 1024 * r:6144 + 1024 * (r + 1)],
                             a[name][0].rearrange("d g c p -> (d g) (c p)")).then_inc(sem("s5_in"), 16)
            for r, name in enumerate(("s5_a_re", "s5_a_im")):
                sp.dma_start((are, aim)[r],
                             a[name][0].rearrange("d g p -> (d g) p")).then_inc(sem("s5_in"), 16)
            sp.wait_ge(sem("d_zero"), 1)
            with nc.allow_non_contiguous_dma(reason="1 KiB and 4 KiB of parameters"):
                sp.dma_start(dtl, a["s5_log_dt"][0].rearrange("d (g o) -> (d g) o", o=1)) \
                    .then_inc(sem("s5_in"), 16)
                dsrc = a["s5_d"][0].rearrange("(b s c) -> s c b", s=4, c=SC)
                for s in range(4):
                    sp.dma_start(dcol[32 * s:32 * s + SC, :], dsrc[s]).then_inc(sem("d_in"), 16)

            sp.wait_ge(sem("yT_ready"), KT)
            for c, (_, src) in enumerate(glu):
                load(N_GLU + c, src, 8)
            free_split(M_GLU)
            load(N_MLP1, w1v[1][0], 8)

            def mlp1_double(i):
                for c, (v, o, k) in enumerate(((w1v[1], 1, 8), (w2v[1], 0, 2), (w1v[1], 2, 8), (w2v[1], 1, 2))):
                    free_split(M_MLP1 + 1 + c - 4, 4 * i)
                    load(N_MLP1 + 1 + c, v[2 * i + o], k)

            with sp.Fori(0, 7) as i:
                mlp1_double(i)
            for c, (src, k) in enumerate(((w1v[1][15], 8), (w2v[1][14], 2), (w2v[1][15], 2))):
                free_split(M_MLP1 + 29 + c - 4)
                load(N_MLP1 + 29 + c, src, k)

            ov = out[0].rearrange("(j t) n -> t j n", t=CH)
            for r in range(4):
                sp.wait_ge(sem("o_act"), r + 1)
                sp.wait_ge(sem("o_dve"), r + 1)
                for t in (2 * r, 2 * r + 1):
                    sp.dma_start(ov[t], xtok[64 * (t % 2):64 * (t % 2) + 64, r, :]).then_inc(sem("stored"), 16)
            sp.wait_ge(sem("stored"), 16 * CH)

        @block.gpsimd
        def _(pool):
            nc.gpsimd.memset(epsc[:, :], EPS).then_inc(sem("eps_set"), 1)

            def zero_y(n):
                pool.wait_ge(sem("x_added"), n)
                nc.gpsimd.memset(ybuf[:, :, :], 0.0).then_inc(sem("y_zero"), 1)

            nc.gpsimd.memset(sil[:, :, :], 0.0).then_inc(sem("sil_zero"), 1)
            nc.gpsimd.memset(dcol[:, :], 0.0).then_inc(sem("d_zero"), 1)
            zero_y(KT)

            pool.wait_ge(sem("prep_over"), 1)
            pool.wait_ge(sem("h1_ready"), KT)
            for b in range(8):
                for d in range(2):
                    i = 2 * b + d
                    if i >= 1:
                        pool.wait_ge(sem("wp_sum"), i)
                    nc.gpsimd.tensor_tensor(mul_buf(tmp), per_t(qw, b, d), power(1, b, d, True), ALU.mult) \
                        .then_inc(sem("m2_ready"), 1)
            pvv = pv[:, 0:2 * GROUPS * SC].rearrange("p (g c) -> p g c", c=SC)
            pool.wait_ge(sem("wp_sum"), 16)
            pool.wait_ge(sem("bu_ready"), 16)
            pool.wait_ge(sem("h1_ready"), KT)
            for b in range(POOL_BLOCKS):
                for d in range(2):
                    j = 2 * b + d
                    if j:
                        pool.wait_ge(sem("xv_pool"), j)
                    nc.gpsimd.tensor_tensor(mul_buf(sq), per_t(pvv, b, d), power(0, b, d, False), ALU.mult) \
                        .then_inc(sem("m1_pool"), 1)
                    nc.gpsimd.tensor_tensor(mul_buf(tmp), per_t(qv, b, d), power(1, b, d, False), ALU.mult) \
                        .then_inc(sem("m2_ready"), 1)
                    pool.wait_ge(sem("m1_pool"), j + 1)
                    pool.wait_ge(sem("m2_ready"), 16 + j + 1)
                    nc.gpsimd.tensor_tensor(xv_block(b, d), mul_buf(sq), mul_buf(tmp), ALU.add) \
                        .then_inc(sem("xv_pool"), 1)
            pool.wait_ge(sem("xv_pool"), 2 * POOL_BLOCKS)
            for b in range(POOL_BLOCKS, 8):
                for d in range(2):
                    j = 2 * (b - POOL_BLOCKS) + d
                    if j:
                        pool.wait_ge(sem("wp_sum"), 16 + j)
                    nc.gpsimd.tensor_tensor(mul_buf(tmp), per_t(qv, b, d), power(1, b, d, False), ALU.mult) \
                        .then_inc(sem("m2_ready"), 1)
            zero_y(3 * KT)

        @block.tensor
        def _(pe):
            mm = nc.tensor.matmul

            def split_matmul(o, l_hi, l_lo, r_hi, r_lo, chunks, first_, last_):
                q = None
                for i, (lw, rw) in enumerate(((l_hi, r_hi), (l_hi, r_lo), (l_lo, r_hi))):
                    for c, (t0, n) in enumerate(chunks):
                        q = mm(o[:, c, :], lw, rw[:, t0:t0 + n], start=first_ and i == 0,
                               stop=last_ and i == 2)
                return q

            def open_group(g, i=0, static=True):
                if not static or g >= 4:
                    pe.wait_ge(sem("acc_taken"), g - 3 + i)

            def tile(m, j, g, k_tiles, moving, chunks, gi=0, wi=0, static=True):
                wh = w_hi[:, m % 2, :].rearrange("p (k n) -> p k n", k=k_tiles)
                wl = w_lo[:, m % 2, :].rearrange("p (k n) -> p k n", k=k_tiles)
                pe.wait_ge(sem("w_split"), m + 1 + wi)
                open_group(g, gi, static)
                for k in range(k_tiles):
                    rh, rl = moving(k)
                    q = split_matmul(ring(g, chunks), wh[:, k, P * j:P * j + P], wl[:, k, P * j:P * j + P],
                                     rh, rl, chunks, k == 0, k == k_tiles - 1)
                q.then_inc(sem("acc_ready"), 1)

            def ada_rows(bank, s, n, ni=0):
                for h in range(2):
                    u = n[h]
                    pe.wait_ge(sem(f"raw_landed{u % NRAW}"), 16 * (u // NRAW + 1) + ni)
                    w = slot_view(u, 8)
                    for k in range(KT):
                        q = mm(ps[32 * (k % 4):32 * (k % 4) + 32, bank, 256 * h:256 * h + 256], sil[:, k, :],
                               w[:, k, :], start=k < 4, stop=k >= 4)
                    if h == 0:
                        q.then_inc(sem("ada_used"), 1)
                return q

            def ada_cols(out_, rows_):
                for c in range(4):
                    q = mm(out_[:, 2 * c:2 * c + 2], rows_[:, P * c:P * c + P], cmask[:, 0:2], start=True, stop=True)
                return q

            def norm_sum(n):
                for k in range(KT):
                    pe.wait_ge(sem("sq_ready"), KT * n + k + 1)
                    for c, (t0, w) in enumerate(norm_chunks(n)):
                        q = mm(ps[:, c, 0:w], ones, sq[:, k % 2, t0:t0 + w], start=k == 0, stop=k == KT - 1)
                    q.then_inc(sem("sq_used"), 1)

            pe.wait_ge(sem("const_in"), 16 * 2)
            pe.wait_ge(sem("rows_in"), 16 * 7)
            nc.tensor.transpose(ps[:, 6, 0:90], rows[0:90, 0, :], ident[0:90, 0:90])
            nc.tensor.transpose(ps[:, 6, 128:224], rows[0:96, 1, :], ident[0:96, 0:96]).then_inc(sem("cols_ready"), 1)
            for r in range(6):
                pe.wait_ge(sem(f"x_landed{r}"), 16 * (4 if r < 2 else 2))
                for half in range(2):
                    e = 2 * r + half
                    if e >= 6:
                        pe.wait_ge(sem("xT_act" if e % 2 == 0 else "xT_dve"), (e - 6) // 2 + 1)
                    for k in range(4):
                        q = nc.tensor.transpose(ps[:, e % 6, P * k:P * k + P],
                                                xtok[:, r, P * (4 * half + k):P * (4 * half + k) + P], ident)
                    q.then_inc(sem("xT_ready"), 1)
            pe.wait_ge(sem("sil_ready"), 1)
            pe.wait_ge(sem("xT_act"), 6)
            pe.wait_ge(sem("xT_dve"), 6)
            norm_sum(0)
            for s in range(5):
                if s < 4:
                    if s >= 2:
                        pe.wait_ge(sem("rows_taken"), s - 1)
                    ada_rows(6 - s % 2, s, (2 * s, 2 * s + 1)).then_inc(sem("rows_ready"), 1)
                if s >= 1:
                    pe.wait_ge(sem("rows_taken"), s)
                    q = ada_cols(ps[:, 7, 8 * (s - 1):8 * s], row_buf(s - 1))
            q.then_inc(sem("cols_done"), 1)

            def h_tile(k):
                return h_hi[:, k, :], h_lo[:, k, :]

            def h_tile_after(base):
                def f(k):
                    pe.wait_ge(sem("h_split"), base + k + 1)
                    return h_tile(k)
                return f

            wh = w_hi[:, 5 % 2, :].rearrange("p (k n) -> p k n", k=KT)
            wl = w_lo[:, 5 % 2, :].rearrange("p (k n) -> p k n", k=KT)
            for g, (kind, i) in enumerate(seq):
                if kind == "head":
                    tile(i // 2, i % 2, g, KT, h_tile if i else h_tile_after(0), L0)
                elif kind == "turn":
                    pe.wait_ge(sem("acc_taken"), seq.index(("head", i)) + 1)
                    open_group(g)
                    b = 2 * (g % 4)
                    if i < HEADS:
                        for r in range(6):
                            mm(ps[:, b + 1, r:r + 1], sq[:, i % 2, P * r:P * r + P], ones[:, 0:1], start=True, stop=True)
                    mm(ps[:, b, :], rotm, qk[:, i, CTX:T], start=True, stop=True).then_inc(sem("acc_ready"), 1)
                elif kind == "squares":
                    pe.wait_ge(sem("hsq_ready"), i + 1)
                    open_group(g)
                    for c, (t0, w) in enumerate(L0):
                        q = mm(ring(g, L0)[:, c, :], ones, sq[:, i % 2, t0:t0 + w], start=True, stop=True)
                    q.then_inc(sem("acc_ready"), 1)
                elif kind == "rows":
                    open_group(g)
                    n = unit_of_ada(2 * i)
                    ada_rows(2 * (g % 4), i, (n, n + 1)).then_inc(sem("acc_ready"), 1)
                elif kind == "cols":
                    pe.wait_ge(sem("acc_taken"), seq.index(("rows", i)) + 1)
                    open_group(g)
                    ada_cols(ps[:, 2 * (g % 4), 0:8], row_buf(i)).then_inc(sem("acc_ready"), 1)
                else:
                    pe.wait_ge(sem("w_split"), 6)
                    open_group(g)
                    for k in range(KT):
                        q = split_matmul(ring(g, [(0, 256)]), h_hi[:, k, P * i:P * i + P], h_lo[:, k, P * i:P * i + P],
                                         wh[:, k, :], wl[:, k, :], [(0, 256)], k == 0, k == KT - 1)
                    q.then_inc(sem("acc_ready"), 1)
            pe.wait_ge(sem("acc_taken"), len(seq))

            pe.wait_ge(sem("q_roped"), HEADS + KVH)
            pe.wait_ge(sem("k_normed"), KVH)

            def scores(t):
                hd, q0, nk = att[t // 2]
                if t >= 2:
                    pe.wait_ge(sem("exp_done"), t - 1)
                lhs = qk[:, hd, q0 + P * (t % 2):q0 + P * (t % 2) + P]
                key = qk[:, HEADS + hd // 4, :]
                chunks = L0 if nk == 6 else [(0, 256)]
                for c, (t0, w) in enumerate(chunks):
                    q = mm(ps[:, 2 * (t % 2) + c, 0:w], lhs, key[:, t0:t0 + w], start=True, stop=True)
                q.then_inc(sem("s_ready"), 1)

            scores(0)
            scores(1)
            for u, (hd, q0, nk) in enumerate(att):
                for t in (2 * u, 2 * u + 1):
                    if t + 2 < 2 * len(att):
                        scores(t + 2)
                for t in (2 * u, 2 * u + 1):
                    pe.wait_ge(sem("p_ready"), t + 1)
                    if t == 2 * u and u >= 1:
                        pe.wait_ge(sem("pT_act"), u)
                        if wide_units(u):
                            pe.wait_ge(sem("pT_dve"), wide_units(u))
                    for kt in range(nk):
                        o = 256 * (kt % 2) + P * (t % 2)
                        q = nc.tensor.transpose(ps[:, 4 + kt // 2, o:o + P], sq[:, t % 2, P * kt:P * kt + P], ident)
                    q.then_inc(sem("pT_ready"), 1)
                pe.wait_ge(sem("pT_act"), u + 1)
                if nk == 6:
                    pe.wait_ge(sem("pT_dve"), wide_units(u + 1))
                if u >= 1:
                    pe.wait_ge(sem("o_taken"), u)
                for kt in range(nk):
                    q = mm(ps[:, 7, 0:256], vt[:, kt, HD * (hd // 4):HD * (hd // 4) + HD],
                           pT[:, u % 2, kt, :], start=kt == 0, stop=kt == nk - 1)
                q.then_inc(sem("o_ready"), 1)
            pe.wait_ge(sem("o_taken"), len(att))

            for u in range(4):
                for j in range(2):
                    tile(6 + u, j, G_WO + 2 * u + j, KT, h_tile, L0)
            pe.wait_ge(sem("acc_taken"), G_MLP0)
            norm_sum(1)
            norm_sum(2)

            def mlp(l, m0, n0, h_base, chunks):
                def hidden(m, group, i=0, static=True, moving=h_tile):
                    for j in range(2):
                        tile(m, j, g_hidden(l, group, j), KT, moving if j == 0 else h_tile, chunks,
                             double_groups(l) * i, 4 * i, static)

                def output(m, step, i=0, static=True, js=range(KT)):
                    slot = 2 * (step % 2)
                    pe.wait_ge(sem("a_split"), 2 * NG * l + 2 * step + 2 + 4 * i)
                    for j in js:
                        tile(m, j, g_out(l, step, j), 2, lambda k: (a_hi[:, slot + k, :], a_lo[:, slot + k, :]), chunks,
                             double_groups(l) * i, 4 * i, static)

                def double(i, with_ada, static=False):
                    s0, m1 = (12, m0 + 25) if static else (0, m0 + 1)
                    for st in range(2):
                        hidden(m1 + 2 * st, s0 + st + 1, i, static)
                        if with_ada:
                            g = g_rows(st)
                            n = n0 + 2 + 4 * st
                            open_group(g, 24 * i, False)
                            ada_rows(2 * (g % 4), None, (n, n + 2), 32 * i).then_inc(sem("acc_ready"), 1)
                            output(m1 + 1 + 2 * st, s0 + st, i, static, range(4))
                            g = g_cols(st)
                            pe.wait_ge(sem("acc_taken"), g_rows(st) + 1 + 24 * i)
                            open_group(g, 24 * i, False)
                            ada_cols(ps[:, 2 * (g % 4), 0:8], rst[:, 0:512]).then_inc(sem("acc_ready"), 1)
                            output(m1 + 1 + 2 * st, s0 + st, i, static, range(4, KT))
                        else:
                            output(m1 + 1 + 2 * st, s0 + st, i, static)

                hidden(m0, 0, moving=h_tile_after(h_base))
                with pe.Fori(0, 6) as i:
                    double(i, l == 0)
                double(0, False, True)
                hidden(m0 + 29, 15)
                output(m0 + 30, 14)
                output(m0 + 31, 15)

            mlp(0, M_MLP0, N_MLP0, KT, L0)
            pe.wait_ge(sem("acc_taken"), G_GLU)
            norm_sum(3)
            norm_sum(4)

            def turn(i, srcs, name="turned"):
                if i >= 4:
                    pe.wait_ge(sem("turn_taken"), i - 3)
                for c, (src, p, w) in enumerate(srcs):
                    q = nc.tensor.transpose(ps[0:w, i % 4, P * c:P * c + p], src, ident[0:p, 0:p])
                q.then_inc(sem("turned"), 1)

            pe.wait_ge(sem("rstd_ready"), 5)
            pe.wait_ge(sem("prep_ready"), 1)
            i = 0
            for r in range(2):
                for e0 in (0, 4, 8):
                    turn(i, [(pow_src(r, e), P, P) for e in range(e0, min(e0 + 4, 9))])
                    i += 1
            for v, (lo, is_b) in enumerate(((1, True), (0, True), (0, False), (1, False))):
                for c0 in range(0, SC, 4):
                    turn(i, [(bc_src(lo, is_b, c), P, P) for c in range(c0, c0 + 4)])
                    i += 1
            pe.wait_ge(sem("turn_taken"), i)
            pe.wait_ge(sem("h1_ready"), KT)
            for t in range(CH):
                for half in range(2):
                    turn(i, [(h1[:, 4 * half + k, t, :], P, NCH) for k in range(4)])
                    i += 1
            pe.wait_ge(sem("turn_taken"), i)
            for b in range(16):
                if i >= 4:
                    pe.wait_ge(sem("turn_taken"), i - 3)
                for c in range(4):
                    q = nc.tensor.transpose(ps[:, i % 4, NCH * c:NCH * c + NCH],
                                            htok[0:NCH, 4 * b + c, :, :].rearrange("p t c -> p (t c)"),
                                            ident[0:NCH, 0:NCH])
                q.then_inc(sem("turned"), 1)
                i += 1
            pe.wait_ge(sem("turn_taken"), i)

            def input_matrices(j):
                b, d = j // 2, j % 2
                pe.wait_ge(sem("wp_sum"), j + 1)
                if j >= 1:
                    pe.wait_ge(sem("wT_taken"), j)
                for g in range(8):
                    q = nc.tensor.transpose(ps[:, g // 4, P * (g % 4):P * (g % 4) + P], wp[:, g, :], ident)
                q.then_inc(sem("wT_ready"), 1)
                if d == 0 and b >= 2:
                    pe.wait_ge(sem("kf_taken"), b - 1)
                for g in range(8):
                    g0 = SC * (GROUPS * d + 8 * b + g)
                    c0 = 256 * d + P * (g // 4)
                    q = mm(kernel_bank(b)[32 * (g % 4):32 * (g % 4) + 32, c0:c0 + P], pv[:, g0:g0 + 32], wp[:, g, :],
                           start=True, stop=True)
                q.then_inc(sem("kf_ready"), 1)

            def chunk_inputs(j):
                pe.wait_ge(sem("wT_taken"), j + 1)
                if j >= 1:
                    pe.wait_ge(sem("bu_taken"), j)
                for r in range(2):
                    for g in range(8):
                        q = mm(ps[64 * (g % 2):64 * (g % 2) + 64, 3 + r, NCH * (g // 2):NCH * (g // 2) + NCH],
                               wT[:, g, NP * r:NP * r + NP], U[:, 8 * (j // 2) + g, :], start=True, stop=True)
                q.then_inc(sem("bu_ready"), 1)

            def within_chunks(b):
                for h in range(4):
                    if b:
                        pe.wait_ge(sem("ml_taken"), 4 * (b - 1) + h + 1)
                    for t in range(4):
                        tt = 4 * (h % 2) + t
                        q = nc.tensor.transpose(ps[:, h, P * t:P * t + P],
                                                kernels(b)[:, h // 2, SC * (7 - tt):SC * (7 - tt) + P], ident)
                    q.then_inc(sem("ml_ready"), 1)

            def chunk_outputs(b):
                pe.wait_ge(sem("ml_taken"), 4 * b + 4)
                for hf in range(2):
                    i2 = 2 * b + hf
                    if i2 >= 2:
                        pe.wait_ge(sem("yl_taken"), i2 - 1)
                    for g in range(4):
                        q = mm(ps[0:NCL, 6 + hf, P * g:P * g + P], U[:, 8 * b + 4 * hf + g, NCC:NCH],
                               ml[:, 4 * hf + g, :, :].rearrange("p t c -> p (t c)"), start=True, stop=True)
                    q.then_inc(sem("yl_ready"), 1)

            input_matrices(0)
            for j in range(16):
                if j + 1 < 16:
                    input_matrices(j + 1)
                chunk_inputs(j)
            pe.wait_ge(sem("kf_taken"), 8)
            pe.wait_ge(sem("wT_taken"), 16)
            pe.wait_ge(sem("bu_taken"), 16)
            for b in range(8):
                within_chunks(b)
                chunk_outputs(b)

            pe.wait_ge(sem("restacked"), 4)
            pe.wait_ge(sem("restacked_act"), 4)
            pe.wait_ge(sem("ml_taken"), 32)
            for b in range(8):
                if b < POOL_BLOCKS:
                    pe.wait_ge(sem("xv_pool"), 2 * b + 2)
                else:
                    pe.wait_ge(sem("wp_sum"), 16 + 2 * (b - POOL_BLOCKS) + 2)
                for hf in range(2):
                    i2 = 2 * b + hf
                    if i2 >= 4:
                        pe.wait_ge(sem("ys_taken"), i2 - 3)
                    for g in range(4):
                        for d in range(2):
                            q = mm(ps[0:NCL, i2 % 4, P * g:P * g + P], sst[:, d, 8 * b + 4 * hf + g, :],
                                   xv_tile(b, d)[:, 4 * hf + g, :], start=d == 0, stop=d == 1)
                    q.then_inc(sem("ys_ready"), 1)
            pe.wait_ge(sem("ys_taken"), 16)
            for k in range(KT):
                if k >= 4:
                    pe.wait_ge(sem("g_ready"), k - 3)
                for t in range(CH):
                    q = nc.tensor.transpose(ps[:, 4 + k % 4, NCL * t:NCL * t + NCL], ytok[0:NCL, k, t, :],
                                            ident[0:NCL, 0:NCL])
                q.then_inc(sem("yT_ready"), 1)
            for u in range(4):
                for j in range(2):
                    tile(M_GLU + u, j, G_GLU + 2 * u + j, KT, h_tile if u or j else h_tile_after(2 * KT), L1)
            pe.wait_ge(sem("acc_taken"), G_MLP1)
            norm_sum(5)
            norm_sum(6)
            mlp(1, M_MLP1, N_MLP1, 3 * KT, L1)
            pe.wait_ge(sem("acc_taken"), G_MLP1 + 10 * NG)
            norm_sum(7)
            pe.wait_ge(sem("x_added"), 4 * KT)
            for r in range(4):
                for half in range(2):
                    for k in range(4):
                        q = nc.tensor.transpose(ps[:, 2 * r + half, P * k:P * k + P],
                                                xT[:, 4 * half + k, CTX + P * r:CTX + P * r + P], ident)
                    q.then_inc(sem("oT_ready"), 1)

        @block.scalar
        def _(act):
            A_ = nc.scalar.activation

            act.dma_start(consts[:, :], a["consts"][:, 0:3 * P]).then_inc(sem("const_in"), 16)
            act.dma_start(cmask[:, :], a["consts"][:, 3 * P:3 * P + SC]).then_inc(sem("const_in"), 16)
            act.dma_start(rope[:, 0:2 * SEQ], a["consts"][:, 3 * P + SC:]).then_inc(sem("rope_in"), 16)
            for r0, src in ((0, a["c"][0]), (8, a["c_ctx"]), (16, a["norm_g"]), (80, a["s5_glu_b"]),
                            (88, a["gqa_q_norm"]), (89, a["gqa_k_norm"])):
                names = " ".join("abc"[:len(src.shape)])
                flat = src.rearrange(f"{names} -> ({names})") if len(src.shape) > 1 else src
                v = flat.rearrange("(r n) -> r n", n=P)
                act.dma_start(rows[r0:r0 + v.shape[0], 0, :], v).then_inc(sem("rows_in"), 16)
            act.dma_start(rows[0:96, 1, :], a["ada_b"].rearrange("l n -> (l n)").rearrange("(r n) -> r n", n=P)) \
                .then_inc(sem("rows_in"), 16)

            def split_hi(m, n, gi=0, ni=0):
                act.wait_ge(sem(f"raw_landed{n % NRAW}"), 16 * (n // NRAW + 1) + ni)
                if m >= 2:
                    act.wait_ge(sem("acc_ready"), groups_after(m - 2) + gi)
                A_(w_hi[:, m % 2, :], raw[:, n % NRAW, :], ACT.Copy).then_inc(sem("w_hi_done"), 1)

            def norm_rstd(n, src_ready):
                ch = norm_chunks(n)
                w = sum(c[1] for c in ch)
                for k in range(KT):
                    src_ready(k)
                    if k >= 2:
                        act.wait_ge(sem("sq_used"), KT * n + k - 1)
                    A_(sq[:, k % 2, 0:w], norm_src(n, k), ACT.Square).then_inc(sem("sq_ready"), 1)
                act.wait_ge(sem("sq_used"), KT * (n + 1))
                A_(by_chunk(rst[:, 0:w], ch), banks(0, ch), ACT.Ln, bias=epsc[:, :], scale=1.0 / D) \
                    .then_inc(sem("rln_done"), 1)
                act.wait_ge(sem("rln_done"), n + 1)
                A_(rst[:, 0:w], rst[:, 0:w], ACT.Exp, scale=-0.5).then_inc(sem("rstd_ready"), 1)

            def h_heads(base, w):
                for k in range(KT):
                    act.wait_ge(sem("h_full"), base + k + 1)
                    A_(h_hi[:, k, 0:w], tmp[:, k % 2, 0:w], ACT.Copy).then_inc(sem("h_hi_done"), 1)

            for r in range(6):
                if r == 0:
                    act.wait_ge(sem("cols_taken"), 1)
                    act.wait_ge(sem("sil_zero"), 1)
                    A_(sil[:, :, 0:2], cols[:, 0:16].rearrange("p (v k) -> p k v", v=2), ACT.Silu) \
                        .then_inc(sem("sil_ready"), 1)
                act.wait_ge(sem("xT_ready"), 2 * r + 1)
                A_(xT[:, 0:4, P * r:P * r + P], ps[:, (2 * r) % 6, :].rearrange("p (k t) -> p k t", k=4), ACT.Copy) \
                    .then_inc(sem("xT_act"), 1)
            act.wait_ge(sem("eps_set"), 1)

            def x_there(k):
                if k == 0:
                    act.wait_ge(sem("xT_act"), 6)
                    act.wait_ge(sem("xT_dve"), 6)
            norm_rstd(0, x_there)
            split_hi(0, 8)
            h_heads(0, T)

            act.wait_ge(sem("sq_used"), KT)
            for hd in range(HEADS + KVH):
                act.wait_ge(sem("acc_ready"), seq.index(("head", hd)) + 1)
                if hd >= 2:
                    act.wait_ge(sem("acc_ready"), seq.index(("turn", hd - 2)) + 1)
                A_(by_chunk(sq[:, hd % 2, :], L0), ring(seq.index(("head", hd)), L0), ACT.Square, scale=HD ** -0.5) \
                    .then_inc(sem("hsq_ready"), 1)
                if hd % 2:
                    m = (hd + 1) // 2
                    split_hi(m, unit_of_split(m))

            def key_rms(hd):
                return sq[:, hd % 2, :]

            act.wait_ge(sem("acc_taken"), seq.index(("turn", HEADS - 1)) + 1)
            A_(q_rms[:, :], q_rms[:, :], ACT.Ln, bias=epsc[:, :]).then_inc(sem("hln_done"), 1)
            for hd in (HEADS, HEADS + 1):
                act.wait_ge(sem("acc_taken"), seq.index(("squares", hd)) + 1)
                A_(key_rms(hd), tmp[:, hd % 2, :], ACT.Ln, bias=epsc[:, :]).then_inc(sem("hln_done"), 1)
            act.wait_ge(sem("hln_done"), 3)
            for hd in (HEADS, HEADS + 1):
                A_(key_rms(hd), key_rms(hd), ACT.Exp, scale=-0.5).then_inc(sem("k_rstd"), 1)
            A_(q_rms[:, :], q_rms[:, :], ACT.Exp, scale=-0.5).then_inc(sem("q_rstd"), 1)
            act.wait_ge(sem("q_rstd"), 1)
            split_hi(6, unit_of_split(6))

            def softmax_exp(t):
                nk = att[t // 2][2]
                ch = L0 if nk == 6 else [(0, 256)]
                act.wait_ge(sem("nmax_ready"), t + 1)
                if t >= 2:
                    act.wait_ge(sem("pT_ready"), t - 1)
                A_(by_chunk(sq[:, t % 2, 0:P * nk], ch), banks(2 * (t % 2), ch), ACT.Exp,
                   bias=nmax[:, t % 2:t % 2 + 1], scale=q_scale(t), accum_out=rsum[:, t % 2:t % 2 + 1]).then_inc(sem("exp_done"), 1)

            softmax_exp(0)
            softmax_exp(1)
            for u, (hd, q0, nk) in enumerate(att):
                act.wait_ge(sem("pT_ready"), 2 * u + 2)
                if u >= 2:
                    act.wait_ge(sem("o_ready"), u - 1)
                for b in ((0, 2) if nk == 6 else (0,)):
                    q = A_(pT[:, u % 2, 2 * b:2 * b + 2, :], ps[:, 4 + b, :].rearrange("p (k t) -> p k t", k=2), ACT.Copy)
                q.then_inc(sem("pT_act"), 1)
                for t in (2 * u + 2, 2 * u + 3):
                    if t < 2 * len(att):
                        softmax_exp(t)
                act.wait_ge(sem("o_ready"), u + 1)
                A_(h_hi[:, hd, q0:q0 + 256], ps[:, 7, 0:256], ACT.Copy) \
                    .then_inc(sem("o_hi_done"), 1)
            for u in range(1, 4):
                split_hi(6 + u, unit_of_split(6 + u))
            split_hi(M_MLP0, N_MLP0)

            def y_there(g0):
                def f(k):
                    act.wait_ge(sem("acc_taken"), g0 + k + 1)
                return f

            def x_updated(base):
                def f(k):
                    act.wait_ge(sem("x_added"), base + k + 1)
                return f

            norm_rstd(1, y_there(G_WO))
            norm_rstd(2, x_updated(0))
            h_heads(KT, T)

            def mlp(l, m0, n0, chunks, period):
                w = sum(c[1] for c in chunks)
                dg = double_groups(l)

                def hidden(group, i=0):
                    for j in range(2):
                        g = g_hidden(l, group, j)
                        act.wait_ge(sem("acc_ready"), g + 1 + dg * i)
                        if group >= 1:
                            act.wait_ge(sem("acc_taken"), g_hidden(l, group - 1, j) + 1 + dg * i)
                        A_(by_chunk(sq[:, j, 0:w], chunks), ring(g, chunks), ACT.Relu).then_inc(sem("relu_done"), 1)
                        act.wait_ge(sem("acc_taken"), g + 1 + dg * i)
                        if group >= 2:
                            act.wait_ge(sem("acc_ready"), g_out(l, group - 2, KT - 1) + 1 + dg * i)
                        A_(a_hi[:, 2 * (group % 2) + j, 0:w], tmp[:, j, 0:w], ACT.Copy).then_inc(sem("a_hi_done"), 1)

                split_hi(m0 + 1, n0 + 1)
                hidden(0)

                def double(i, rel):
                    landed = 4 * period * i
                    for st in range(2):
                        step = 2 * rel + st
                        m, n = m0 + 2 + 2 * st, n0 + 1 + (2 * st + 1) * period // 4
                        split_hi(m, n, dg * i, landed)
                        hidden(step + 1, i - rel)
                        split_hi(m + 1, n + period // 4, dg * i, landed)

                double(0, 0)
                with act.Fori(1, 6 if period == 8 else 7) as i:
                    double(i, 1)
                if period == 8:
                    n = n0 + 49
                    for st in range(2):
                        split_hi(m0 + 26 + 2 * st, n + 1 + 2 * st)
                        hidden(13 + st)
                        split_hi(m0 + 27 + 2 * st, n + 2 + 2 * st)
                    n = n0 + 53
                else:
                    n = n0 + 29
                split_hi(m0 + 30, n + 1)
                hidden(15)
                split_hi(m0 + 31, n + 2)

            mlp(0, M_MLP0, N_MLP0, L0, 8)
            norm_rstd(3, y_there(G_GLU - 8))
            norm_rstd(4, x_updated(KT))

            act.wait_ge(sem("s5_in"), 16 * 7)
            A_(dtc, dtl, ACT.Exp).then_inc(sem("dt_ready"), 1)
            act.wait_ge(sem("lam_dt"), 1)
            A_(mag, lr, ACT.Exp).then_inc(sem("mag_ready"), 1)
            act.wait_ge(sem("angles"), 1)
            A_(sn, ang, ACT.Sin)
            A_(cs, ang2, ACT.Sin).then_inc(sem("sin_ready"), 1)

            def turned(i):
                act.wait_ge(sem("turned"), i + 1)

            def matrices_out(j):
                act.wait_ge(sem("wT_ready"), j + 1)
                if j >= 1:
                    act.wait_ge(sem("bu_ready"), j)
                A_(wT[:, :, :], ps[:, 0:2, :].rearrange("p a (b n) -> p (a b) n", n=P), ACT.Copy) \
                    .then_inc(sem("wT_taken"), 1)

            matrices_out(0)
            for j in range(16):
                if j + 1 < 16:
                    matrices_out(j + 1)
                b, d = j // 2, j % 2
                if d:
                    act.wait_ge(sem("kf_ready"), j + 1)
                    if b == 0:
                        act.wait_ge(sem("s_zero"), 1)
                    kp = kernel_bank(b).rearrange("p (d q n) -> p d q n", d=2, q=2)
                    A_(kernels(b)[:, :, 0:P], kp[:, 0, :, :], ACT.Copy)
                    A_(kernels(b)[:, :, P:15 * SC], kp[:, 1, :, SC:P], ACT.Copy).then_inc(sem("kf_copied"), 1)
                act.wait_ge(sem("bu_ready"), j + 1)
                for r in range(2):
                    src = ps[:, 3 + r, 0:4 * NCH].rearrange("p (q n) -> p n q", n=NCH)
                    q0 = 4 * b
                    if d == 0:
                        q = A_(Sv[:, 1:1 + NCH, 0, r, q0:q0 + 4], src, ACT.Copy)
                    else:
                        A_(Sv[:, 1:1 + NCC, 1, r, q0:q0 + 4][:, ::-1, :], src[:, 0:NCC, :], ACT.Copy)
                        q = A_(Sv[:, 1 + NCC:1 + NCH, 1, r, q0:q0 + 4][:, ::-1, :], src[:, NCC:NCH, :], ACT.Copy)
                q.then_inc(sem("bu_taken"), 1)
            for b in range(8):
                for h in range(4):
                    act.wait_ge(sem("ml_ready"), 4 * b + h + 1)
                    if h == 0 and b >= 1:
                        act.wait_ge(sem("yl_ready"), 2 * b)
                    src = ps[:, h, :].rearrange("p (t g c) -> p t g c", t=4, g=4)[:, :, :, 0:SC]
                    dst = ml[:, 4 * (h // 2):4 * (h // 2) + 4, 4 * (h % 2):4 * (h % 2) + 4, :] \
                        .rearrange("p g t c -> p t g c")
                    A_(dst, src, ACT.Copy).then_inc(sem("ml_taken"), 1)
                for hf in range(2):
                    act.wait_ge(sem("yl_ready"), 2 * b + hf + 1)
                    A_(out_half(b, hf), ps[0:NCL, 6 + hf, :].rearrange("p (g t c) -> p g t c", g=4, t=CH), ACT.Copy) \
                        .then_inc(sem("yl_taken"), 1)
            for d in range(2):
                for r in range(2):
                    restack(act, lambda o, i_: A_(o, i_, ACT.Copy), d, 1, r)

            for k in range(KT):
                act.wait_ge(sem("yT_ready"), k + 1)
                A_(ybuf[:, k, 0:SEQ], ps[:, 4 + k % 4, :], ACT.Gelu_apprx_tanh).then_inc(sem("g_ready"), 1)
                act.wait_ge(sem("g_ready"), k + 1)
                A_(h_hi[:, k, 0:SEQ], ybuf[:, k, 0:SEQ], ACT.Copy).then_inc(sem("h_hi_done"), 1)
            for u in range(4):
                split_hi(M_GLU + u, N_GLU + u) if u == 0 else None
                if u + 1 < 4:
                    split_hi(M_GLU + u + 1, N_GLU + u + 1)
                else:
                    split_hi(M_MLP1, N_MLP1)
                for j in range(2):
                    g = G_GLU + 2 * u + j
                    act.wait_ge(sem("acc_ready"), g + 1)
                    if 2 * u + j >= 2:
                        act.wait_ge(sem("acc_taken"), g - 1)
                    A_(sq[:, j, 0:SEQ], ring(g, L1)[:, 0, :], ACT.Sigmoid, bias=cols[:, 80 + 2 * u + j:81 + 2 * u + j]) \
                        .then_inc(sem("sig_ready"), 1)
            act.wait_ge(sem("acc_taken"), G_MLP1)
            norm_rstd(5, y_there(G_GLU))
            norm_rstd(6, x_updated(2 * KT))
            h_heads(2 * KT, SEQ)
            mlp(1, M_MLP1, N_MLP1, L1, 4)
            norm_rstd(7, y_there(G_MLP1 + 10 * NG - 8))
            for r in range(4):
                act.wait_ge(sem("oT_ready"), 2 * r + 1)
                A_(xtok[:, r, 0:512], ps[:, 2 * r, :], ACT.Copy).then_inc(sem("o_act"), 1)

        @block.vector
        def _(dve):
            TT = nc.vector.tensor_tensor
            STT = nc.vector.scalar_tensor_tensor
            TS = nc.vector.tensor_scalar
            CP = nc.vector.tensor_copy
            linked = [0]

            def link(q):
                linked[0] += 1
                q.then_inc(sem("dve_step"), 1)
                dve.wait_ge(sem("dve_step"), linked[0])

            def split_lo(m, mi=0):
                dve.wait_ge(sem("w_hi_done"), m + 1 + mi)
                raw_n = unit_of_split(m)
                for p in range(2):
                    s = slice(1024 * p, 1024 * p + 1024)
                    q = TT(w_lo[:, m % 2, s], raw[:, raw_n % NRAW, s], w_hi[:, m % 2, s].bitcast(F32), ALU.subtract)
                q.then_inc(sem("w_split"), 1)

            def mods(l, j):
                b = adab[:, 48 * l + 8 * j:48 * l + 8 * j + 8].unsqueeze(2).to_broadcast([P, KT, 2])
                q = TT(mod[:, l, j, :, :], mod[:, l, j, :, :], b, ALU.add)
                if j == 2 or j == 5:
                    link(q)
                    g = gain(l, 1 if j == 2 else 3)
                    q = TT(coef[:, l, 1 if j == 2 else 3, :, :], mod[:, l, j, :, :], g, ALU.mult)
                elif j == 1 or j == 4:
                    link(q)
                    q = STT(coef[:, l, 0 if j == 1 else 2, :, :], mod[:, l, j, :, :], 1.0, gain(l, 0 if j == 1 else 2),
                            ALU.add, ALU.mult)
                q.then_inc(sem("mod_ready"), 1)

            def gain(l, i):
                c0 = 16 + (4 * l + i) * KT
                return cols[:, c0:c0 + KT].unsqueeze(2).to_broadcast([P, KT, 2])

            def apply_norm(l, i, n, base, segs, x0, w, split=True):
                dve.wait_ge(sem("rstd_ready"), n + 1)

                def rest(k):
                    dve.wait_ge(sem("h_hi_done"), base + k + 1)
                    TT(h_lo[:, k, 0:w], tmp[:, k % 2, 0:w], h_hi[:, k, 0:w].bitcast(F32), ALU.subtract) \
                        .then_inc(sem("h_split"), 1)

                for k in range(KT):
                    if k >= 2 and split:
                        dve.wait_ge(sem("h_split"), base + k - 1)
                    elif k >= 2:
                        dve.wait_ge(sem("h1_ready"), k - 1)
                    link(TT(tmp[:, k % 2, 0:w], xT[:, k, x0:x0 + w], rst[:, 0:w], ALU.mult))
                    for t0, m, v in segs:
                        src = tmp[:, k % 2, t0:t0 + m]
                        dst = src
                        if not split:
                            nch = m // CH
                            c0 = 0 if v else NCC
                            dst = h1[:, k, :, c0:c0 + nch]
                            src = src.rearrange("p (t c) -> p t c", t=CH)
                        q = TS(dst, src, coef[:, l, 2 * i, k, v:v + 1], mod[:, l, 3 * i, k, v:v + 1], ALU.mult, ALU.add)
                    q.then_inc(sem("h_full" if split else "h1_ready"), 1)
                    if split and k >= 1:
                        rest(k - 1)
                if split:
                    rest(KT - 1)

            def add_branch(l, i, n, xbase, segs, x0, w):
                dve.wait_ge(sem("rstd_ready"), n + 1)
                for k in range(KT):
                    if k >= 2:
                        dve.wait_ge(sem("x_added"), xbase + k - 1)
                    for t0, m, v in segs:
                        q = STT(tmp[:, k % 2, t0:t0 + m], ybuf[:, k, t0:t0 + m], coef[:, l, 2 * i + 1, k, v:v + 1],
                                rst[:, t0:t0 + m], ALU.mult, ALU.mult)
                    link(q)
                    TT(xT[:, k, x0:x0 + w], xT[:, k, x0:x0 + w], tmp[:, k % 2, 0:w], ALU.add).then_inc(sem("x_added"), 1)

            dve.wait_ge(sem("cols_ready"), 1)
            CP(cols[:, 0:90], ps[:, 6, 0:90])
            link(CP(adab[:, :], ps[:, 6, 128:224]))
            TS(cols[:, 89:90], cols[:, 89:90], HD ** -0.5, None, ALU.mult).then_inc(sem("cols_taken"), 1)
            for r in range(6):
                dve.wait_ge(sem("xT_ready"), 2 * r + 2)
                CP(xT[:, 4:8, P * r:P * r + P], ps[:, (2 * r + 1) % 6, :].rearrange("p (k t) -> p k t", k=4)) \
                    .then_inc(sem("xT_dve"), 1)
            for s in range(4):
                dve.wait_ge(sem("rows_ready"), s + 1)
                CP(row_buf(s), ps[:, 6 - s % 2, :]).then_inc(sem("rows_taken"), 1)
            dve.wait_ge(sem("cols_done"), 1)
            dve.wait_ge(sem("cols_taken"), 1)
            link(CP(mod_cols[:, 0:32], ps[:, 7, 0:32]))
            mods(0, 0)
            mods(0, 1)
            dve.wait_ge(sem("mod_ready"), 2)
            apply_norm(0, 0, 0, 0, SEG0, 0, T)
            split_lo(0)
            dve.wait_ge(sem("rope_in"), 16)
            for g, (kind, i) in enumerate(seq):
                dve.wait_ge(sem("acc_ready"), g + 1)
                if kind == "head":
                    gc = 88 if i < HEADS else 89
                    dve.wait_ge(sem("hsq_ready"), i + 1)
                    TS(by_chunk(qk[:, i, :], L0), ring(g, L0), cols[:, gc:gc + 1], None, ALU.mult) \
                        .then_inc(sem("acc_taken"), 1)
                    if i % 2:
                        split_lo((i + 1) // 2)
                elif kind == "turn":
                    q, b, t = qk[:, i, CTX:T], 2 * (g % 4), tmp[:, i % 2, 0:SEQ]
                    if i < HEADS:
                        CP(q_rms[:, 6 * i:6 * i + 6], ps[:, b + 1, 0:6])
                    if i >= 2:
                        dve.wait_ge(sem("q_roped"), i - 1)
                    TT(t, ps[:, b, :], rope[:, SEQ:2 * SEQ], ALU.mult).then_inc(sem("acc_taken"), 1)
                    dve.wait_ge(sem("acc_taken"), seq.index(("head", i)) + 1)
                    link(TT(q, q, rope[:, 0:SEQ], ALU.mult))
                    dve.wait_ge(sem("acc_taken"), g + 1)
                    TT(q, q, t, ALU.add).then_inc(sem("q_roped"), 1)
                elif kind == "squares":
                    dve.wait_ge(sem("q_roped"), i + 1)
                    CP(by_chunk(tmp[:, i % 2, :], L0), ring(g, L0)).then_inc(sem("acc_taken"), 1)
                elif kind == "rows":
                    CP(row_buf(i), ps[:, 2 * (g % 4), :]).then_inc(sem("acc_taken"), 1)
                elif kind == "cols":
                    CP(mod_cols[:, 8 * i:8 * i + 8], ps[:, 2 * (g % 4), 0:8]).then_inc(sem("acc_taken"), 1)
                else:
                    CP(vt[:, i, :], ring(g, [(0, 256)])[:, 0, :]).then_inc(sem("acc_taken"), 1)
            dve.wait_ge(sem("q_roped"), HEADS + KVH)
            for i, hd in enumerate((HEADS, HEADS + 1)):
                dve.wait_ge(sem("k_rstd"), i + 1)
                TT(qk[:, hd, :], qk[:, hd, :], sq[:, hd % 2, :], ALU.mult).then_inc(sem("k_normed"), 1)
            for j in range(2, 6):
                mods(0, j)
            split_lo(6)

            def row_max(t):
                nk = att[t // 2][2]
                ch = L0 if nk == 6 else [(0, 256)]
                dve.wait_ge(sem("s_ready"), t + 1)
                m = nmax[:, t % 2:t % 2 + 1]
                link(nc.vector.tensor_reduce(m, banks(2 * (t % 2), ch), AX.XY, ALU.max, negate=True))
                TT(m, m, q_scale(t), ALU.mult).then_inc(sem("nmax_ready"), 1)

            def normalise(t):
                nk = att[t // 2][2]
                dve.wait_ge(sem("exp_done"), t + 1)
                link(nc.vector.reciprocal(rinv[:, t % 2:t % 2 + 1], rsum[:, t % 2:t % 2 + 1]))
                TS(sq[:, t % 2, 0:P * nk], sq[:, t % 2, 0:P * nk], rinv[:, t % 2:t % 2 + 1], None, ALU.mult) \
                    .then_inc(sem("p_ready"), 1)

            dve.wait_ge(sem("q_rstd"), 1)
            row_max(0)
            row_max(1)
            normalise(0)
            normalise(1)
            for u, (hd, q0, nk) in enumerate(att):
                more = u + 1 < len(att)
                if more:
                    row_max(2 * u + 2)
                    row_max(2 * u + 3)
                dve.wait_ge(sem("pT_ready"), 2 * u + 2)
                if nk == 6:
                    if u >= 2:
                        dve.wait_ge(sem("o_ready"), u - 1)
                    CP(pT[:, u % 2, 2:4, :], ps[:, 5, :].rearrange("p (k t) -> p k t", k=2)) \
                        .then_inc(sem("pT_dve"), 1)
                if more:
                    normalise(2 * u + 2)
                    normalise(2 * u + 3)
                dve.wait_ge(sem("o_hi_done"), u + 1)
                TT(h_lo[:, hd, q0:q0 + 256], ps[:, 7, 0:256],
                   h_hi[:, hd, q0:q0 + 256].bitcast(F32), ALU.subtract).then_inc(sem("o_taken"), 1)
            for u in range(4):
                split_lo(7 + u)
                for j in range(2):
                    g = G_WO + 2 * u + j
                    dve.wait_ge(sem("acc_ready"), g + 1)
                    CP(by_chunk(ybuf[:, 2 * u + j, :], L0), ring(g, L0)).then_inc(sem("acc_taken"), 1)
            add_branch(0, 0, 1, 0, SEG0, 0, T)
            apply_norm(0, 1, 2, KT, SEG0, 0, T)

            def mlp(l, m0, chunks):
                w = sum(c[1] for c in chunks)
                dg = double_groups(l)

                def hidden(group, i=0):
                    for j in range(2):
                        z = 2 * NG * l + 2 * group + j
                        if group >= 1:
                            dve.wait_ge(sem("a_split"), z - 1 + 4 * i)
                        dve.wait_ge(sem("relu_done"), z + 1 + 4 * i)
                        STT(by_chunk(tmp[:, j, 0:w], chunks), ring(g_hidden(l, group, j), chunks), 0.0,
                            by_chunk(sq[:, j, 0:w], chunks), ALU.max, ALU.mult).then_inc(sem("acc_taken"), 1)
                        dve.wait_ge(sem("a_hi_done"), z + 1 + 4 * i)
                        slot = 2 * (group % 2) + j
                        TT(a_lo[:, slot, 0:w], tmp[:, j, 0:w], a_hi[:, slot, 0:w].bitcast(F32), ALU.subtract) \
                            .then_inc(sem("a_split"), 1)

                def output(step, i=0, js=range(KT)):
                    for j in js:
                        g = g_out(l, step, j)
                        dve.wait_ge(sem("acc_ready"), g + 1 + dg * i)
                        if step >= 1:
                            dve.wait_ge(sem("acc_taken"), g_out(l, step - 1, j) + 1 + dg * i)
                        else:
                            dve.wait_ge(sem("y_zero"), l + 1)
                        y = by_chunk(ybuf[:, j, 0:w], chunks)
                        TT(y, y, ring(g, chunks), ALU.add).then_inc(sem("acc_taken"), 1)

                split_lo(m0 + 1)
                hidden(0)

                def double(i, rel):
                    for st in range(2):
                        step, o, m = 2 * rel + st, i - rel, m0 + 2 + 2 * st + 4 * rel
                        split_lo(m, 4 * o)
                        hidden(step + 1, o)
                        split_lo(m + 1, 4 * o)
                        if l == 0 and rel < 6:
                            g = g_rows(step)
                            dve.wait_ge(sem("acc_ready"), g + 1 + dg * o)
                            CP(rst[:, 0:512], ps[:, 2 * (g % 4), :]).then_inc(sem("acc_taken"), 1)
                            output(step, o, range(4))
                            g, c0 = g_cols(step), 8 * (12 + step)
                            dve.wait_ge(sem("acc_ready"), g + 1 + dg * o)
                            dst = mod_cols[:, bass.ds(c0 + 16 * o, 8)] if rel == 1 else mod_cols[:, c0:c0 + 8]
                            CP(dst, ps[:, 2 * (g % 4), 0:8]).then_inc(sem("acc_taken"), 1)
                            output(step, o, range(4, KT))
                        else:
                            output(step, o)

                double(0, 0)
                with dve.Fori(1, 6) as i:
                    double(i, 1)
                double(6, 6)
                split_lo(m0 + 30)
                hidden(15)
                split_lo(m0 + 31)
                output(14)
                output(15)

            mlp(0, M_MLP0, L0)
            for j in range(6):
                mods(1, j)
            dve.wait_ge(sem("mod_ready"), 12)
            add_branch(0, 1, 3, KT, SEG0, 0, T)
            dve.wait_ge(sem("x_added"), 2 * KT)

            dve.wait_ge(sem("s5_in"), 16 * 7)
            dve.wait_ge(sem("dt_ready"), 1)
            TS(lr, are, dtc, None, ALU.mult)
            TS(li, aim, dtc, None, ALU.mult).then_inc(sem("lam_dt"), 1)
            dve.wait_ge(sem("lam_dt"), 1)
            link(TS(kk, li, 1.0 / TWO_PI, MAGIC, ALU.mult, ALU.add))
            link(TS(kk, kk, -MAGIC, None, ALU.add))
            link(STT(t0_, kk, -PI_HI, li, ALU.mult, ALU.add))
            link(STT(t1_, kk, -PI_MID, t0_, ALU.mult, ALU.add))
            link(STT(t2_, kk, -PI_LO, t1_, ALU.mult, ALU.add))
            link(TS(ang, t2_, 3.1415925, -3.1415925, ALU.min, ALU.max))
            link(STT(t0_, ang, -1.0, ang, ALU.mult, ALU.max))
            TS(ang2, t0_, -1.0, math.pi / 2, ALU.mult, ALU.add).then_inc(sem("angles"), 1)
            dve.wait_ge(sem("mag_ready"), 1)
            dve.wait_ge(sem("sin_ready"), 1)
            pw9 = lambda r, e: flat_tok[:, (r * 9 + e) * P:(r * 9 + e) * P + NP]
            nc.vector.memset(pw9(0, 0), 1.0)
            nc.vector.memset(pw9(1, 0), 0.0)
            TT(pw9(0, 1), mag, cs, ALU.mult)
            link(TT(pw9(1, 1), mag, sn, ALU.mult))
            ar, ai = pw9(0, 1), pw9(1, 1)
            for e in range(2, 9):
                TT(t0_, pw9(0, e - 1), ar, ALU.mult)
                TT(t1_, pw9(1, e - 1), ai, ALU.mult)
                TT(t2_, pw9(0, e - 1), ai, ALU.mult)
                link(TT(den, pw9(1, e - 1), ar, ALU.mult))
                TT(pw9(0, e), t0_, t1_, ALU.subtract)
                link(TT(pw9(1, e), t2_, den, ALU.add))
            pw2 = flat_tok[:, 0:18 * P].rearrange("p (n u s) -> p n u s", u=2, s=NP)
            CP(pw2[:, :, 1, :], pw2[:, :, 0, :])
            TS(arm1, ar, -1.0, None, ALU.add)
            TT(t0_, are, are, ALU.mult)
            link(TT(t1_, aim, aim, ALU.mult))
            link(TT(t2_, t0_, t1_, ALU.add))
            link(nc.vector.reciprocal(den, t2_))
            TT(t0_, arm1, are, ALU.mult)
            link(TT(t1_, ai, aim, ALU.mult))
            link(TT(t2_, t0_, t1_, ALU.add))
            link(TT(cre, t2_, den, ALU.mult))
            TT(t0_, ai, are, ALU.mult)
            link(TT(t1_, arm1, aim, ALU.mult))
            link(TT(t2_, t0_, t1_, ALU.subtract))
            link(TT(cim, t2_, den, ALU.mult))
            br = S[:, 0:1024].rearrange("p (s c) -> p s c", s=NP)
            bi = S[:, 1024:2048].rearrange("p (s c) -> p s c", s=NP)
            bb = S[:, 2048:5120].rearrange("p (r s c) -> p r s c", r=3, s=NP)
            f1 = S[:, 5120:6144].rearrange("p (s c) -> p s c", s=NP)
            wide = lambda v: v.unsqueeze(2).to_broadcast([P, NP, SC])
            link(TT(bb[:, 1, :, :], br, wide(cre), ALU.mult))
            link(TT(f1, bi, wide(cim), ALU.mult))
            link(TT(bb[:, 1, :, :], bb[:, 1, :, :], f1, ALU.subtract))
            link(TT(bb[:, 2, :, :], br, wide(cim), ALU.mult))
            link(TT(f1, bi, wide(cre), ALU.mult))
            link(TT(bb[:, 2, :, :], bb[:, 2, :, :], f1, ALU.add))
            TS(S[:, 2048:3072], S[:, 4096:5120], -1.0, None, ALU.mult)
            c3 = S[:, C3:C3 + 3072].rearrange("p (c r s) -> p c r s", r=3, s=NP)
            cr, ci = (S[:, 6144 + 1024 * r:7168 + 1024 * r].rearrange("p (c s) -> p c s", s=NP) for r in range(2))
            CP(c3[:, :, 0, :], cr)
            TS(c3[:, :, 1, :], ci, -1.0, None, ALU.mult)
            TS(c3[:, :, 2, :], cr, -1.0, None, ALU.mult)
            nc.vector.memset(pv[:, 2 * GROUPS * SC:], 0.0).then_inc(sem("prep_ready"), 1)

            i = 0

            def taken(q):
                q.then_inc(sem("turn_taken"), 1)

            for r in range(2):
                for e0, ne in ((0, 4), (4, 4), (8, 1)):
                    dve.wait_ge(sem("turned"), i + 1)
                    taken(CP(powT[:, r, e0:e0 + ne, :], ps[:, i % 4, 0:P * ne].rearrange("p (e n) -> p e n", n=P)))
                    i += 1
            for dst in (pw[:, :, :], qw[:, :, :], pv[:, 0:2 * GROUPS * SC].rearrange("p (g c) -> p g c", c=SC), qv[:, :, :]):
                for c0 in range(0, SC, 4):
                    dve.wait_ge(sem("turned"), i + 1)
                    taken(CP(dst[:, :, c0:c0 + 4], ps[:, i % 4, :].rearrange("p (c n) -> p n c", c=4)))
                    i += 1
            dve.wait_ge(sem("turn_taken"), i)
            for g2 in range(2):
                p = slice(64 * g2, 64 * g2 + 64)
                for r in range(2):
                    src = powT[p, r, 8, :].rearrange("p (d q g) -> p d q g", d=2, g=2)[:, :, :, g2]
                    if r == 0:
                        CP(a8[p, 0, :, 0, :], src)
                        CP(a8[p, 1, :, 1, :], src)
                    else:
                        TS(a8[p, 1, :, 0, :], src, -1.0, None, ALU.mult)
                        q = CP(a8[p, 0, :, 1, :], src)
            q.then_inc(sem("prep_over"), 1)

            apply_norm(1, 0, 4, 0, SEG0, 0, T, split=False)
            dve.wait_ge(sem("h1_ready"), KT)
            for t in range(CH):
                for half in range(2):
                    dve.wait_ge(sem("turned"), i + 1)
                    taken(CP(htok[0:NCH, 32 * half:32 * half + 32, t, :],
                             ps[0:NCH, i % 4, :].rearrange("p (g c) -> p g c", c=SC)))
                    i += 1
            for b in range(16):
                dve.wait_ge(sem("turned"), i + 1)
                taken(CP(U[:, 4 * b:4 * b + 4, :], ps[:, i % 4, 0:4 * NCH].rearrange("p (g n) -> p g n", g=4)))
                i += 1
            dve.wait_ge(sem("turn_taken"), i)
            dve.wait_ge(sem("prep_over"), 1)
            dve.wait_ge(sem("d_in"), 16 * 4)
            nc.vector.memset(Sv[:, 0, :, :, :], 0.0).then_inc(sem("s_zero"), 1)

            def products(j, par, inward, dst, reader, n):
                b, d = (j % 16) // 2, j % 2
                own = j if j < 16 else j - 2 * POOL_BLOCKS
                if own == 16:
                    dve.wait_ge(sem("xv_pool"), 2 * POOL_BLOCKS)
                    dve.wait_ge(sem("restacked_act"), 4)
                if own:
                    dve.wait_ge(sem("wp_sum"), own)
                TT(mul_buf(sq), per_t(par, b, d), power(0, b, d, inward), ALU.mult).then_inc(sem("m1_ready"), 1)
                dve.wait_ge(sem("m1_ready"), own + 1)
                dve.wait_ge(sem("m2_ready"), j + 1)
                if n >= 1:
                    dve.wait_ge(sem(reader), n)
                TT(dst, mul_buf(sq), mul_buf(tmp), ALU.add).then_inc(sem("wp_sum"), 1)

            pvv = pv[:, 0:2 * GROUPS * SC].rearrange("p (g c) -> p g c", c=SC)
            wp4 = wp[:, :, :].rearrange("p g (t c) -> p g t c", t=CH)

            def finish_kernels(b):
                dve.wait_ge(sem("kf_copied"), b + 1)
                lag0 = kernels(b)[:, :, 7 * SC:8 * SC]
                link(TT(lag0, lag0, lag0_of_backward(b), ALU.add))
                TT(lag0, lag0, sdm[:, 2 * b:2 * b + 2, :], ALU.add).then_inc(sem("kf_taken"), 1)

            def in_products(j):
                products(j, pw, True, wp4, "kf_ready", j)

            link(TT(sdm[:, :, :], cmask[:, :].unsqueeze(1).to_broadcast([P, 16, SC]),
                    dcol[:, :].unsqueeze(2).to_broadcast([P, 16, SC]), ALU.mult))
            for b in range(8):
                in_products(2 * b)
                in_products(2 * b + 1)
                if b:
                    finish_kernels(b - 1)
            finish_kernels(7)

            dve.wait_ge(sem("bu_taken"), 16)
            dve.wait_ge(sem("s_zero"), 1)
            moved = rst[:, 0:2 * P].rearrange("p (d c r q) -> p d c r q", c=2, d=2, r=2)
            for i_ in range(NCH):
                c = SCAN_INCS * i_
                for d in range(2):
                    if i_:
                        dve.wait_ge(sem("scan"), c - 1 + d)
                    parts = Sv[:, i_, d, :, :].unsqueeze(2).to_broadcast([P, 2, 2, 32])
                    TT(moved[:, d], a8[:, :, d], parts, ALU.mult).then_inc(sem("scan"), 1)
                for part in range(2):
                    for d in range(2):
                        cur = Sv[:, i_ + 1, d, :, :]
                        dve.wait_ge(sem("scan"), c + 2 * part + d + 1)
                        TT(cur, cur, moved[:, d, part], ALU.add).then_inc(sem("scan"), 1)

            for d in range(2):
                for r in range(2):
                    restack(nc.vector, CP, d, 0, r)
            for b in range(8):
                for d in range(2):
                    if b >= POOL_BLOCKS:
                        products(16 + 2 * b + d, pvv, False, xv_block(b, d), "restacked", 4)
                for hf in range(2):
                    dve.wait_ge(sem("ys_ready"), 2 * b + hf + 1)
                    y = out_half(b, hf)
                    dve.wait_ge(sem("yl_taken"), 16)
                    TT(y, y, ps[0:NCL, (2 * b + hf) % 4, :].rearrange("p (g t c) -> p g t c", g=4, t=CH), ALU.add) \
                        .then_inc(sem("ys_taken"), 1)

            for k in range(KT):
                dve.wait_ge(sem("h_hi_done"), 2 * KT + k + 1)
                TT(h_lo[:, k, 0:SEQ], ybuf[:, k, 0:SEQ], h_hi[:, k, 0:SEQ].bitcast(F32), ALU.subtract) \
                    .then_inc(sem("h_split"), 1)
            split_lo(M_GLU)
            for u in range(4):
                split_lo(M_GLU + u + 1)
                for j in range(2):
                    g = G_GLU + 2 * u + j
                    dve.wait_ge(sem("sig_ready"), 2 * u + j + 1)
                    TT(ybuf[:, 2 * u + j, 0:SEQ], ybuf[:, 2 * u + j, 0:SEQ], sq[:, j, 0:SEQ], ALU.mult) \
                        .then_inc(sem("acc_taken"), 1)
            seg = [(0, SEQ, 0)]
            add_branch(1, 0, 5, 2 * KT, seg, CTX, SEQ)
            apply_norm(1, 1, 6, 3 * KT, seg, CTX, SEQ)
            mlp(1, M_MLP1, L1)
            add_branch(1, 1, 7, 3 * KT, seg, CTX, SEQ)
            for r in range(4):
                dve.wait_ge(sem("oT_ready"), 2 * r + 2)
                CP(xtok[:, r, 512:1024], ps[:, 2 * r + 1, :]).then_inc(sem("o_dve"), 1)


_INS = ["x", "c", "ctx", "c_ctx", "ada_w", "ada_b", "norm_g", "mlp_w1", "mlp_w2", "gqa_w_qkv", "gqa_q_norm",
        "gqa_k_norm", "gqa_w_o", "s5_a_re", "s5_a_im", "s5_log_dt", "s5_b_re", "s5_b_im", "s5_c_re", "s5_c_im",
        "s5_d", "s5_glu_w", "s5_glu_b"]


def shape_constants():
    ident = np.eye(P, dtype=np.float32)
    ones = np.ones((P, P), np.float32)
    rot = np.zeros((P, P), np.float32)
    for m in range(P):
        if (m // 32) % 2 == 0:
            rot[m + 32, m] = -1.0
        else:
            rot[m - 32, m] = 1.0
    mask = (np.arange(P)[:, None] % 32 == np.arange(SC)[None, :]).astype(np.float32)
    half = HD // 2
    inv = (1.0 / (10000.0 ** (np.arange(0, half, 2, dtype=np.float32) / half))).astype(np.float32)
    tok = (np.arange(NCL)[None, :] * CH + np.arange(CH)[:, None]).reshape(-1)
    ang = np.concatenate([np.outer(np.tile(inv, 2), (tok // 64).astype(np.float32)),
                          np.outer(np.tile(inv, 2), (tok % 64).astype(np.float32))]).astype(np.float32)
    return np.concatenate([ident, ones, rot, mask, np.cos(ang), np.sin(ang)], axis=1).astype(np.float32)


def kernel(**inputs):
    import numpy as _np
    import concourse.bacc as _bacc
    from concourse import mybir as _mybir
    from concourse.bass_utils import run_bass_kernel_spmd as _run

    nc = _bacc.Bacc("TRN2", target_bir_lowering=False, num_devices=1)
    arrays, args = {}, {}
    for name in _INS + ["consts"]:
        v = shape_constants() if name == "consts" else _np.ascontiguousarray(inputs[name])
        arrays[f"in_{name}"] = v
        args[name] = nc.dram_tensor(f"in_{name}", v.shape, _mybir.dt.from_np(v.dtype), kind="ExternalInput").ap()
    out = nc.dram_tensor("out_0", (1, SEQ, D), F32, kind="ExternalOutput").ap()
    build(nc, args, out)
    r = _run(nc, [arrays], core_ids=[0])
    return r.results[0]["out_0"]
```

```python
import math
from contextlib import ExitStack

import numpy as np

import concourse.bass as bass
from concourse import mybir

F32 = mybir.dt.float32
F32R = mybir.dt.float32r
ACT = mybir.ActivationFunctionType
ALU = mybir.AluOpType
AX = mybir.AxisListType

P = 128
D = 1024
KT = D // P
SEQ, CTX = 512, 256
T = CTX + SEQ
CH = 8
NCC, NCL = CTX // CH, SEQ // CH
NCH = NCC + NCL
FF = 4 * D
EPS = 1e-6
HD = 128
HEADS, KVH = 8, 2
GROUPS, SC = 64, 16
NP = 64
UNIT = 2048
NRAW = 4
TWO_PI = 2 * math.pi
SCAN_INCS = 6
SCAN_STEPS = NCH - 2
MAGIC = 1.5 * 2 ** 23
PI_HI, PI_MID = 6.28125, 0.0019350051879882812
C3 = 8192
PI_LO = TWO_PI - PI_HI - PI_MID


def build(nc, a, out):
    ctx = ExitStack()
    with ctx:
        sems = {}

        def sem(name):
            if name not in sems:
                sems[name] = ctx.enter_context(nc.semaphore(name))
            return sems[name]

        def sb(stack, name, shape, dt=F32):
            return stack.enter_context(nc.sbuf_tensor(name, shape, dt))

        ps = ctx.enter_context(nc.psum_tensor("ps", [P, 8, 512], F32))
        xT = sb(ctx, "xT", [P, KT, T])
        sq = sb(ctx, "sq", [P, 2, T])
        tmp = sb(ctx, "tmp", [P, 2, T])
        rst = sb(ctx, "rst", [P, T])
        consts = sb(ctx, "shape_consts", [P, 3 * P])
        ident, ones, rotm = consts[:, 0:P], consts[:, P:2 * P], consts[:, 2 * P:3 * P]
        cmask = sb(ctx, "cmask", [P, SC])
        dcol = sb(ctx, "dcol", [P, SC])
        warm = sb(ctx, "warm", [P, 8])
        epsc = sb(ctx, "epsc", [P, 1])
        rows = sb(ctx, "rows", [96, 2, P])
        cols = sb(ctx, "cols", [P, 96])
        adab = sb(ctx, "adab", [P, 96])
        mod = sb(ctx, "mod", [P, 2, 6, KT, 2])
        coef = sb(ctx, "coef", [P, 2, 4, KT, 2])
        nmax = sb(ctx, "nmax", [P, 4])
        rsum = sb(ctx, "rsum", [P, 4])
        rinv = sb(ctx, "rinv", [P, 4])
        q_rms = sb(ctx, "q_rms", [P, 6 * HEADS])

        A = ExitStack()
        sil = sb(A, "sil", [P, KT, 32])
        raw = sb(A, "raw", [P, NRAW, UNIT])
        h_hi = sb(A, "h_hi", [P, KT, T], F32R)
        h_lo = sb(A, "h_lo", [P, KT, T], F32R)
        w_hi = sb(A, "w_hi", [P, 2, UNIT], F32R)
        w_lo = sb(A, "w_lo", [P, 2, UNIT], F32R)
        with ExitStack() as s:
            xtok = sb(s, "xtok", [P, 6, D])
        with ExitStack() as s:
            qk = sb(s, "qk", [P, HEADS + KVH, T])
            vt = sb(s, "vt", [P, 6, KVH * HD])
            pT = sb(s, "pT", [P, 2, 6, 256])
            rope = pT[:, :, :, :].rearrange("p a b c -> p (a b c)")
        with ExitStack() as s:
            ybuf = sb(s, "ybuf", [P, KT, T])
            a_hi = sb(s, "a_hi", [P, 4, T], F32R)
            a_lo = sb(s, "a_lo", [P, 4, T], F32R)
        A.close()
        with ExitStack() as s:
            ytok = sb(s, "ytok", [P, 8, CH, P])
            pv = sb(s, "pv", [P, 2 * GROUPS * SC + SC])
            qv = sb(s, "qv", [P, 2 * GROUPS, SC])
            powT = sb(s, "powT", [P, 2, 9, P])
            a8 = sb(s, "a8", [P, 2, 2, 2, 32])
            S = sb(s, "S", [P, 97 * P])
            with ExitStack() as s1:
                U = sb(s1, "U", [P, GROUPS, NCH])
                pw = sb(s1, "pw", [P, 2 * GROUPS, SC])
                qw = sb(s1, "qw", [P, 2 * GROUPS, SC])
                wp = sb(s1, "wp", [P, 8, P])
                wT = sb(s1, "wT", [P, 8, P])
                ml = sb(s1, "ml", [P, 8, CH, SC])
                sdm = sb(s1, "sdm", [P, 16, SC])
            with ExitStack() as s1:
                sst = sb(s1, "sst", [P, 2, GROUPS, NCL])
                xv = sb(s1, "xv", [P, 2, 2, 8, P])
        flat_tok = ytok[:, :, :, :].rearrange("p b t n -> p (b t n)")
        otok = raw[:, :, 0:D]
        mod_cols = mod[:, :, :, :, :].rearrange("p l j k v -> p (l j k v)")
        htok = flat_tok.rearrange("p (g t c) -> p g t c", g=GROUPS, t=CH)
        Sv = S[:, :].rearrange("p (i d r q) -> p i d r q", d=2, r=2, q=32)
        h1 = U[:, :, :].rearrange("p g n -> p (g n)").rearrange("p (k t c) -> p k t c", k=KT, t=CH)

        units = []

        def square_units(w, n0, n):
            v = w.rearrange("(k p) n -> p k n", p=P)
            return [(True, v[:, :, n0 + 256 * i:n0 + 256 * (i + 1)]) for i in range(n)]

        def ada_units(l, j0, j1):
            v = a["ada_w"][l].rearrange("(k p) n -> p k n", p=P)
            return [(False, v[:, :, 256 * i:256 * (i + 1)]) for i in range(4 * j0, 4 * j1)]

        qkv_units = square_units(a["gqa_w_qkv"][0], 0, 6)
        shift_scale = ada_units(0, 0, 2)
        first = []
        for i in range(4):
            first += ([qkv_units[0]] if i == 3 else []) + [shift_scale[i], shift_scale[4 + i]]
        for u in range(4):
            first += ([qkv_units[u]] if u else []) + ada_units(0, 2 + u, 3 + u)
        first += qkv_units[4:] + square_units(a["gqa_w_o"][0], 0, 4)

        seq = []
        for hd in range(HEADS + KVH):
            seq.append(("head", hd))
            if hd:
                seq.append(("turn", hd - 1))
            if 1 <= hd <= HEADS:
                seq.append(("cols", 4 + hd - 1))
            if hd < HEADS:
                seq.append(("rows", 4 + hd))
        seq += [("squares", HEADS), ("v", 0), ("turn", HEADS + 1), ("squares", HEADS + 1)]
        seq += [("v", r) for r in range(1, 6)]
        NG = FF // 256
        w1v = [a["mlp_w1"][l].rearrange("(k p) (g n) -> g p k n", p=P, n=256) for l in range(2)]
        w2v = [a["mlp_w2"][l].rearrange("(g k p) n -> g p k n", p=P, k=2) for l in range(2)]
        adav = a["ada_w"][1].rearrange("(k p) (u n) -> u p k n", p=P, n=256)
        glu = square_units(a["s5_glu_w"][0], 0, 4)

        def slot_view(n, k):
            return raw[:, n % NRAW, :].rearrange("p (k n) -> p k n", k=k)

        N_MLP0 = len(first)
        M_MLP0 = sum(s for s, _ in first)
        N_GLU = N_MLP0 + 2 * NG + 24
        M_GLU = M_MLP0 + 2 * NG
        N_MLP1 = N_GLU + len(glu)
        M_MLP1 = M_GLU + len(glu)
        G_WO = len(seq)
        G_MLP0 = G_WO + 8
        G_GLU = G_MLP0 + 10 * NG + 24
        G_MLP1 = G_GLU + 8
        assert G_MLP0 % 4 == 0 and G_MLP1 % 4 == 0
        ADA_STEPS = 12

        def step_base(l, i):
            g = (G_MLP0, G_MLP1)[l] + 2 + 10 * i
            return g + 2 * min(i, ADA_STEPS) if l == 0 else g

        def g_hidden(l, group, j=0):
            return j + (step_base(l, group - 1) if group else (G_MLP0, G_MLP1)[l])

        def g_rows(i):
            return step_base(0, i) + 2

        def g_cols(i):
            return step_base(0, i) + 7

        def g_out(l, i, j):
            g = step_base(l, i) + j
            if i == NG - 1:
                return g
            return g + 2 + ((1 if j < 4 else 2) if l == 0 and i < ADA_STEPS else 0)

        def double_groups(l):
            return 24 if l == 0 else 20

        def groups_after(m):
            for l, m0 in ((1, M_MLP1), (0, M_MLP0)):
                c = m - m0
                if 0 <= c < 2 * NG:
                    if c == 2 * NG - 1:
                        return g_out(l, NG - 1, KT - 1) + 1
                    if c == 0 or c % 2:
                        return g_hidden(l, (c + 1) // 2, 1) + 1
                    return g_out(l, c // 2 - 1, KT - 1) + 1
            if m >= M_GLU:
                return G_GLU + 2 * (m - M_GLU + 1)
            if m < 5:
                return seq.index(("head", 2 * m + 1)) + 1
            return G_WO + 2 * (m - 5)

        def unit_of_split(m):
            if m < M_MLP0:
                return [n for n, (s, _) in enumerate(first) if s][m]
            if m < M_GLU:
                c = m - M_MLP0
                return N_MLP0 + (0 if c == 0 else 2 * c - 1 if c <= 24 else c + 24)
            return N_GLU + m - M_GLU

        def unit_of_ada(u):
            return [n for n, (s, _) in enumerate(first) if not s][u]

        L0 = [(0, 384), (384, 384)]
        L1 = [(0, 512)]
        SEG0 = [(0, CTX, 1), (CTX, SEQ, 0)]

        def banks(b, chunks, parts=P):
            n = chunks[0][1]
            return ps[0:parts, b:b + len(chunks), 0:n]

        def ring(g, chunks):
            return banks(2 * (g % 4), chunks)

        def by_chunk(ap, chunks):
            return ap.rearrange("p (c n) -> p c n", c=len(chunks))

        def row_buf(s):
            if s < 4:
                return vt[:, :, :].rearrange("p r n -> p (r n)")[:, 512 * (s % 2):512 * (s % 2) + 512]
            return rst[:, 0:512]

        def first_cols(s):
            return ps[:, (7, 2, 3, 4)[s], 0:8]

        def wait_x(eng, branch, k):
            eng.wait_ge(sem("x_added_pool" if k % 2 else "x_added"), KT // 2 * branch + k // 2 + 1)

        def norm_src(n, k):
            if n in (0, 2):
                return xT[:, k, :]
            if n in (1, 3):
                return ybuf[:, k, :]
            if n == 4:
                return xT[:, k, :]
            if n == 6:
                return xT[:, k, CTX:T]
            return ybuf[:, k, 0:SEQ]

        def norm_chunks(n):
            return L0 if n < 5 else L1

        def mul_buf(t):
            return t[:, :, :].rearrange("p a b -> p (a b)")[:, 0:1024].rearrange("p (g t c) -> p g t c", g=8, t=CH)

        def per_t(t, b, d):
            g0 = d * GROUPS + 8 * b
            return t[:, g0:g0 + 8, :].unsqueeze(2).to_broadcast([P, 8, CH, SC])

        def power(r, b, d, inward):
            g0 = d * GROUPS + 8 * b
            lo = 0 if inward else 1
            v = powT[:, r, lo:lo + 8, g0:g0 + 8]
            if (d == 0) == inward:
                v = powT[:, r, lo:lo + 8, g0:g0 + 8][:, ::-1, :]
            return v.rearrange("p t g -> p g t").unsqueeze(3).to_broadcast([P, 8, CH, SC])

        def in_matrices(j):
            return wp[:, :, :] if j % 2 == 0 else xT[:, :, 0:P]

        def kernels(b):
            return flat_tok[:, 1024 * b:1024 * b + 30 * SC].rearrange("p (q n) -> p q n", q=2)

        def wT_bank(j):
            return (0, 6)[j % 2]

        def lag0_of_backward(b):
            return kernel_bank(b).rearrange("p (d q n) -> p d q n", d=2, q=2)[:, 1, :, 0:SC]

        def kernel_bank(b):
            return ps[:, (2, 5)[b % 2], :]

        POOL_BLOCKS = 3

        def xv_tile(b, d):
            if b < 2:
                return xv[:, b, d, :, :]
            if b == 2:
                return xT[:, :, P * d:P * d + P]
            return S[:, 1024 * (2 * (b - 3) + d):1024 * (2 * (b - 3) + d) + 1024].rearrange("p (g n) -> p g n", g=8)

        def out_half(b, hf):
            return ytok[0:NCL, b, :, 4 * SC * hf:4 * SC * hf + 4 * SC].rearrange("p t (g c) -> p g t c", g=4)

        def xv_block(b, d):
            return xv_tile(b, d).rearrange("p g (t c) -> p g t c", t=CH)

        def pow_src(r, e):
            return flat_tok[:, (r * 9 + e) * P:(r * 9 + e + 1) * P]

        def bc_src(lo, is_b, c):
            if is_b:
                v = S[:, 2048:2048 + 3072].rearrange("p (r s c) -> p r s c", r=3, s=NP)
                return v[:, lo:lo + 2, :, c].rearrange("p r s -> p (r s)")
            return S[:, C3 + 192 * c + NP * lo:C3 + 192 * c + NP * lo + P]

        att = [(hd, q0, nk) for hd in range(HEADS) for q0, nk in ((0, 2), (CTX, 6), (CTX + 256, 6))]

        def q_scale(t):
            hd, q0, _ = att[t // 2]
            c = 6 * hd + q0 // P + t % 2
            return q_rms[:, c:c + 1]

        def prob_rows(t):
            return (sq, tmp)[t // 2 % 2][:, t % 2, :]

        def wide_units(u):
            return sum(nk == 6 for _, _, nk in att[:u])

        def tile64(i):
            return S[:, 11456 + 64 * i:11456 + 64 * (i + 1)]
        are, aim, dtl, dtc = S[:, 11264:11328], S[:, 11328:11392], S[:, 11392:11393], S[:, 11393:11394]
        lr, li, mag, ang, ang2, sn, cs, t0_, t1_, t2_, den, cre, cim, arm1, kk = (tile64(i) for i in range(15))

        def chunk_inputs_out(eng, copy, j, r):
            b, d = j // 2, j % 2
            eng.wait_ge(sem("bu_ready"), j + 1)
            src = ps[:, 3 + r, 0:4 * NCH].rearrange("p (q n) -> p n q", n=NCH)
            dst = Sv[:, :, d, r, 4 * b:4 * b + 4]
            if d == 0:
                return copy(dst[:, 1:1 + NCH], src)
            copy(dst[:, 1:1 + NCC][:, ::-1, :], src[:, 0:NCC, :])
            return copy(dst[:, 1 + NCC:1 + NCH][:, ::-1, :], src[:, NCC:NCH, :])

        b_in = [S[:, 1024 * r:1024 * r + 1024].rearrange("p (s c) -> p s c", s=NP) for r in range(2)]
        b_out = S[:, 2048:5120].rearrange("p (r s c) -> p r s c", r=3, s=NP)
        b_tmp = [S[:, c:c + 1024].rearrange("p (s c) -> p s c", s=NP) for c in (6144, 5120)]

        def by_channel(v):
            return v.unsqueeze(2).to_broadcast([P, NP, SC])

        C_TURNS, P_TURNS, B_TURNS = 8, 6, 8
        H_TURN0 = C_TURNS + P_TURNS + B_TURNS
        U_TURN0 = H_TURN0 + 2 * CH
        TURNS = U_TURN0 + 16

        def act_turn(i):
            return i < C_TURNS or i % 2 == 1

        def wait_turned(eng, i):
            n = sum(act_turn(j) == act_turn(i) for j in range(i + 1))
            eng.wait_ge(sem("turned_act" if act_turn(i) else "turned_dve"), n)

        def turn_bank(i):
            return 2 + i % 4

        def turn_out(i):
            full = ps[:, turn_bank(i), :]
            if i < C_TURNS or C_TURNS + P_TURNS <= i < H_TURN0:
                if i < C_TURNS:
                    v, c0 = divmod(i, 4)
                    dst = (pv[:, 0:2 * GROUPS * SC].rearrange("p (g c) -> p g c", c=SC), qv[:, :, :])[v]
                else:
                    v, c0 = divmod(i - C_TURNS - P_TURNS, 4)
                    dst = (pw[:, :, :], qw[:, :, :])[v]
                return dst[:, :, 4 * c0:4 * c0 + 4], full.rearrange("p (c n) -> p n c", c=4)
            if i < C_TURNS + P_TURNS:
                r, e = divmod(i - C_TURNS, 3)
                ne = (4, 4, 1)[e]
                return powT[:, r, 4 * e:4 * e + ne, :], full[:, 0:P * ne].rearrange("p (e n) -> p e n", n=P)
            if i < U_TURN0:
                t, half = divmod(i - H_TURN0, 2)
                return htok[0:NCH, 32 * half:32 * half + 32, t, :], full[0:NCH, :].rearrange("p (g c) -> p g c", c=SC)
            b = i - U_TURN0
            return U[:, 4 * b:4 * b + 4, :], full[:, 0:4 * NCH].rearrange("p (g n) -> p g n", g=4)

        def restack(eng, copy, d, g2, r):
            eng.wait_ge(sem("scan"), SCAN_INCS * SCAN_STEPS)
            eng.wait_ge(sem("yl_ready"), 16)
            src = Sv[64 * g2:64 * g2 + 64, NCC:NCH, d, r, :]
            if d == 1:
                src = src[:, ::-1, :]
            dst = sst[64 * r:64 * r + 64, d, :, :].rearrange("p (q g) n -> p n q g", g=2)[:, :, :, g2]
            copy(dst, src).then_inc(sem("restacked" if eng is nc.vector else "restacked_act"), 1)

        block = ctx.enter_context(nc.Block())

        @block.sync
        def _(sp):
            def x_rows(t, is_ctx):
                src = a["ctx" if is_ctx else "x"][0].rearrange("(j t) n -> t j n", t=CH)[t]
                nch = NCC if is_ctx else NCL
                per = P // nch
                tile = t // per + (0 if is_ctx else 2)
                return tile, xtok[nch * (t % per):nch * (t % per + 1), tile, :], src

            def load(n, src, k):
                sp.dma_start(slot_view(n, k), src).then_inc(sem(f"raw_landed{n % NRAW}"), 16)

            def free_ada(u):
                if u % 2 == 0:
                    sp.wait_ge(sem("ada_used"), u // 2 + 1)
                elif u < 8:
                    sp.wait_ge(sem("rows_ready"), u // 2 + 1)
                else:
                    sp.wait_ge(sem("acc_ready"), seq.index(("rows", u // 2)) + 1)

            kinds = [s for s, _ in first]

            for is_ctx in (True, False):
                for t in range(CH):
                    tile, dst, src = x_rows(t, is_ctx)
                    sp.dma_start(dst, src).then_inc(sem(f"x_landed{tile}"), 16)
            for n, (is_split, src) in enumerate(first):
                if n >= NRAW:
                    o = n - NRAW
                    if kinds[o]:
                        sp.wait_ge(sem("w_split"), sum(kinds[:o]) + 1)
                    else:
                        free_ada(o - sum(kinds[:o]))
                load(n, src, 8)

            def free_split(m, i=0):
                sp.wait_ge(sem("w_split"), m + 1 + i)

            free_split(M_MLP0 - 4)
            load(N_MLP0, w1v[0][0], 8)
            base = N_MLP0 + 1
            m = M_MLP0 + 1
            def mlp0_slot_free(c, i, loop):
                if not loop and i == 0 and c < 4:
                    sp.wait_ge(sem("w_split"), M_MLP0 - 3 + c + 1)
                elif c % 4 == 1:
                    sp.wait_ge(sem("ada_used"), 2 * i + 12 + c // 4)
                elif c % 4 == 3:
                    if loop:
                        sp.wait_ge(sem("acc_ready"), 24 * (i - 1) + g_rows(1 + c // 4) + 1)
                    else:
                        sp.wait_ge(sem("acc_ready"), g_rows(c // 4 - 1) + 1)
                else:
                    sp.wait_ge(sem("w_split"), 4 * i + m + (c - 4) // 2 + 1)

            def mlp0_double(i, loop):
                for c in range(8):
                    mlp0_slot_free(c, i, loop)
                    step = c // 4
                    if c % 4 == 0:
                        load(base + c, w1v[0][2 * i + 1 + step], 8)
                    elif c % 4 == 2:
                        load(base + c, w2v[0][2 * i + step], 2)
                    else:
                        load(base + c, adav[4 * i + c // 2], 8)

            mlp0_double(0, False)
            with sp.Fori(1, 6) as i:
                mlp0_double(i, True)
            n = base + 48
            mm = m + 24
            tail = [(w1v[0][13], 8), (w2v[0][12], 2), (w1v[0][14], 8), (w2v[0][13], 2),
                    (w1v[0][15], 8), (w2v[0][14], 2), (w2v[0][15], 2)]
            for c, (src, k) in enumerate(tail):
                if c < 4:
                    if c == 1:
                        sp.wait_ge(sem("ada_used"), 24)
                    elif c == 3:
                        sp.wait_ge(sem("acc_ready"), g_rows(ADA_STEPS - 1) + 1)
                    else:
                        sp.wait_ge(sem("w_split"), mm - 2 + c // 2 + 1)
                else:
                    sp.wait_ge(sem("w_split"), mm + c - 4 + 1)
                load(n + c, src, k)
            assert n + 7 == N_GLU and mm + 7 == M_GLU

            sp.wait_ge(sem("acc_ready"), G_GLU)
            for r, name in enumerate(("s5_b_re", "s5_b_im")):
                sp.dma_start(S[:, 1024 * r:1024 * (r + 1)],
                             a[name][0].rearrange("d g p c -> (d g) (p c)")).then_inc(sem("s5_in"), 16)
            for r, name in enumerate(("s5_c_re", "s5_c_im")):
                sp.dma_start(S[:, 6144 + 1024 * r:6144 + 1024 * (r + 1)],
                             a[name][0].rearrange("d g c p -> (d g) (c p)")).then_inc(sem("s5_in"), 16)
            for r, name in enumerate(("s5_a_re", "s5_a_im")):
                sp.dma_start((are, aim)[r],
                             a[name][0].rearrange("d g p -> (d g) p")).then_inc(sem("s5_in"), 16)
            sp.wait_ge(sem("d_zero"), 1)
            with nc.allow_non_contiguous_dma(reason="1 KiB and 4 KiB of parameters"):
                sp.dma_start(dtl, a["s5_log_dt"][0].rearrange("d (g o) -> (d g) o", o=1)) \
                    .then_inc(sem("s5_in"), 16)
                dsrc = a["s5_d"][0].rearrange("(b s c) -> s c b", s=4, c=SC)
                for s in range(4):
                    sp.dma_start(dcol[32 * s:32 * s + SC, :], dsrc[s]).then_inc(sem("d_in"), 16)

            sp.wait_ge(sem("yT_ready"), KT)
            for c, (_, src) in enumerate(glu):
                load(N_GLU + c, src, 8)
            free_split(M_GLU)
            load(N_MLP1, w1v[1][0], 8)

            def mlp1_double(i):
                for c, (v, o, k) in enumerate(((w1v[1], 1, 8), (w2v[1], 0, 2), (w1v[1], 2, 8), (w2v[1], 1, 2))):
                    free_split(M_MLP1 + 1 + c - 4, 4 * i)
                    load(N_MLP1 + 1 + c, v[2 * i + o], k)

            with sp.Fori(0, 7) as i:
                mlp1_double(i)
            for c, (src, k) in enumerate(((w1v[1][15], 8), (w2v[1][14], 2), (w2v[1][15], 2))):
                free_split(M_MLP1 + 29 + c - 4)
                load(N_MLP1 + 29 + c, src, k)

            ov = out[0].rearrange("(j t) n -> t j n", t=CH)
            for half, done in enumerate(("o_act", "o_dve")):
                for r in range(4):
                    sp.wait_ge(sem(done), r + 1)
                    sp.dma_start(ov[2 * r:2 * r + 2, :, 512 * half:512 * half + 512],
                                 otok[:, r, 512 * half:512 * half + 512]).then_inc(sem("stored"), 16)
            sp.wait_ge(sem("stored"), 16 * 8)

        @block.gpsimd
        def _(pool):
            nc.gpsimd.memset(epsc[:, :], EPS).then_inc(sem("eps_set"), 1)

            def add_odd_tiles(branch, x0, w):
                for k in range(1, KT, 2):
                    pool.wait_ge(sem("branch_scaled"), KT // 2 * branch + k // 2 + 1)
                    nc.gpsimd.tensor_tensor(xT[:, k, x0:x0 + w], xT[:, k, x0:x0 + w], tmp[:, 1, 0:w], ALU.add) \
                        .then_inc(sem("x_added_pool"), 1)

            def zero_y(branch):
                pool.wait_ge(sem("x_added"), KT // 2 * (branch + 1))
                nc.gpsimd.memset(ybuf[:, :, :], 0.0).then_inc(sem("y_zero"), 1)

            nc.gpsimd.memset(sil[:, :, :], 0.0).then_inc(sem("sil_zero"), 1)
            nc.gpsimd.memset(dcol[:, :], 0.0).then_inc(sem("d_zero"), 1)
            add_odd_tiles(0, 0, T)
            zero_y(0)

            pool.wait_ge(sem("s5_in"), 16 * 7)
            c3 = S[:, C3:C3 + 3072].rearrange("p (c r s) -> p c r s", r=3, s=NP)
            cr, ci = (S[:, 6144 + 1024 * r:7168 + 1024 * r].rearrange("p (c s) -> p c s", s=NP) for r in range(2))
            nc.gpsimd.tensor_copy(c3[:, :, 0, :], cr)
            nc.gpsimd.tensor_scalar(c3[:, :, 1, :], ci, -1.0, None, ALU.mult)
            nc.gpsimd.tensor_scalar(c3[:, :, 2, :], cr, -1.0, None, ALU.mult)
            nc.gpsimd.memset(pv[:, 2 * GROUPS * SC:], 0.0).then_inc(sem("c_ready"), 1)
            add_odd_tiles(1, 0, T)
            pool.wait_ge(sem("gains_ready"), 1)
            nc.gpsimd.tensor_tensor(b_out[:, 2, :, :], b_in[0], by_channel(cim), ALU.mult).then_inc(sem("b_step"), 1)
            nc.gpsimd.tensor_tensor(b_tmp[1], b_in[1], by_channel(cre), ALU.mult).then_inc(sem("b_step"), 1)
            pool.wait_ge(sem("b_step"), 2)
            nc.gpsimd.tensor_tensor(b_out[:, 2, :, :], b_out[:, 2, :, :], b_tmp[1], ALU.add).then_inc(sem("b_im"), 1)

            wait_turned(pool, H_TURN0 - 1)
            wait_turned(pool, H_TURN0 - 2)
            pool.wait_ge(sem("h1_ready"), KT)
            for b in range(8):
                for d in range(2):
                    i = 2 * b + d
                    if i >= 1:
                        pool.wait_ge(sem("wp_sum"), i)
                    nc.gpsimd.tensor_tensor(mul_buf(tmp), per_t(qw, b, d), power(1, b, d, True), ALU.mult) \
                        .then_inc(sem("m2_ready"), 1)
            pvv = pv[:, 0:2 * GROUPS * SC].rearrange("p (g c) -> p g c", c=SC)
            pool.wait_ge(sem("wp_sum"), 16)
            pool.wait_ge(sem("bu_ready"), 16)
            pool.wait_ge(sem("h1_ready"), KT)
            for b in range(POOL_BLOCKS):
                for d in range(2):
                    j = 2 * b + d
                    if j:
                        pool.wait_ge(sem("xv_pool"), j)
                    nc.gpsimd.tensor_tensor(mul_buf(sq), per_t(pvv, b, d), power(0, b, d, False), ALU.mult) \
                        .then_inc(sem("m1_pool"), 1)
                    nc.gpsimd.tensor_tensor(mul_buf(tmp), per_t(qv, b, d), power(1, b, d, False), ALU.mult) \
                        .then_inc(sem("m2_ready"), 1)
                    pool.wait_ge(sem("m1_pool"), j + 1)
                    pool.wait_ge(sem("m2_ready"), 16 + j + 1)
                    nc.gpsimd.tensor_tensor(xv_block(b, d), mul_buf(sq), mul_buf(tmp), ALU.add) \
                        .then_inc(sem("xv_pool"), 1)
            pool.wait_ge(sem("xv_pool"), 2 * POOL_BLOCKS)
            for b in range(POOL_BLOCKS, 8):
                for d in range(2):
                    j = 2 * (b - POOL_BLOCKS) + d
                    if j:
                        pool.wait_ge(sem("wp_sum"), 16 + j)
                    nc.gpsimd.tensor_tensor(mul_buf(tmp), per_t(qv, b, d), power(1, b, d, False), ALU.mult) \
                        .then_inc(sem("m2_ready"), 1)
            add_odd_tiles(2, CTX, SEQ)
            zero_y(2)
            add_odd_tiles(3, CTX, SEQ)

        @block.tensor
        def _(pe):
            mm = nc.tensor.matmul

            def split_matmul(o, l_hi, l_lo, r_hi, r_lo, chunks, first_, last_):
                q = None
                for i, (lw, rw) in enumerate(((l_hi, r_hi), (l_hi, r_lo), (l_lo, r_hi))):
                    for c, (t0, n) in enumerate(chunks):
                        q = mm(o[:, c, :], lw, rw[:, t0:t0 + n], start=first_ and i == 0,
                               stop=last_ and i == 2)
                return q

            def open_group(g, i=0, static=True):
                if not static or g >= 4:
                    pe.wait_ge(sem("acc_taken"), g - 3 + i)

            def tile(m, j, g, k_tiles, moving, chunks, gi=0, wi=0, static=True):
                wh = w_hi[:, m % 2, :].rearrange("p (k n) -> p k n", k=k_tiles)
                wl = w_lo[:, m % 2, :].rearrange("p (k n) -> p k n", k=k_tiles)
                pe.wait_ge(sem("w_split"), m + 1 + wi)
                open_group(g, gi, static)
                for k in range(k_tiles):
                    rh, rl = moving(k)
                    q = split_matmul(ring(g, chunks), wh[:, k, P * j:P * j + P], wl[:, k, P * j:P * j + P],
                                     rh, rl, chunks, k == 0, k == k_tiles - 1)
                q.then_inc(sem("acc_ready"), 1)

            def ada_rows(bank, n, ni=0):
                for h in range(2):
                    u = n[h]
                    pe.wait_ge(sem(f"raw_landed{u % NRAW}"), 16 * (u // NRAW + 1) + ni)
                    w = slot_view(u, 8)
                    for k in range(KT):
                        q = mm(ps[32 * (k % 4):32 * (k % 4) + 32, bank, 256 * h:256 * h + 256], sil[:, k, :],
                               w[:, k, :], start=k < 4, stop=k >= 4)
                    if h == 0:
                        q.then_inc(sem("ada_used"), 1)
                return q

            def ada_cols(out_, rows_):
                for c in range(4):
                    q = mm(out_[:, 2 * c:2 * c + 2], rows_[:, P * c:P * c + P], cmask[:, 0:2], start=True, stop=True)
                return q

            def norm_sum(n, ks=range(KT)):
                for k in ks:
                    pe.wait_ge(sem("sq_ready"), KT * n + k + 1)
                    for c, (t0, w) in enumerate(norm_chunks(n)):
                        q = mm(ps[:, c, 0:w], ones, sq[:, k % 2, t0:t0 + w], start=k == 0, stop=k == KT - 1)
                    q.then_inc(sem("sq_used"), 1)

            pe.wait_ge(sem("const_in"), 16 * 2)
            pe.wait_ge(sem("rows_in"), 16 * 7)
            nc.tensor.transpose(ps[:, 6, 0:90], rows[0:90, 0, :], ident[0:90, 0:90])
            nc.tensor.transpose(ps[:, 6, 128:224], rows[0:96, 1, :], ident[0:96, 0:96]).then_inc(sem("cols_ready"), 1)
            for r in range(6):
                pe.wait_ge(sem(f"x_landed{r}"), 16 * (4 if r < 2 else 2))
                for half in range(2):
                    e = 2 * r + half
                    if e >= 6:
                        pe.wait_ge(sem("xT_act" if e % 2 == 0 else "xT_dve"), (e - 6) // 2 + 1)
                    for k in range(4):
                        q = nc.tensor.transpose(ps[:, e % 6, P * k:P * k + P],
                                                xtok[:, r, P * (4 * half + k):P * (4 * half + k) + P], ident)
                    q.then_inc(sem("xT_ready"), 1)
            pe.wait_ge(sem("sil_ready"), 1)
            pe.wait_ge(sem("xT_act"), 6)
            pe.wait_ge(sem("xT_dve"), 6)
            norm_sum(0, range(4))
            for s in range(4):
                if s >= 2:
                    pe.wait_ge(sem("rows_taken"), s - 1)
                ada_rows(6 - s % 2, (unit_of_ada(2 * s), unit_of_ada(2 * s + 1))).then_inc(sem("rows_ready"), 1)
                if s == 0:
                    norm_sum(0, range(4, KT))
                pe.wait_ge(sem("rows_taken"), s + 1)
                ada_cols(first_cols(s), row_buf(s)).then_inc(sem("cols_done"), 1)

            def h_tile(k):
                return h_hi[:, k, :], h_lo[:, k, :]

            def h_tile_after(base):
                def f(k):
                    pe.wait_ge(sem("h_split"), base + k + 1)
                    return h_tile(k)
                return f

            wh = w_hi[:, 5 % 2, :].rearrange("p (k n) -> p k n", k=KT)
            wl = w_lo[:, 5 % 2, :].rearrange("p (k n) -> p k n", k=KT)
            for g, (kind, i) in enumerate(seq):
                if kind == "head":
                    tile(i // 2, i % 2, g, KT, h_tile if i else h_tile_after(0), L0)
                elif kind == "turn":
                    pe.wait_ge(sem("acc_taken"), seq.index(("head", i)) + 1)
                    open_group(g)
                    b = 2 * (g % 4)
                    if i < HEADS:
                        for r in range(6):
                            mm(ps[:, b + 1, r:r + 1], sq[:, i % 2, P * r:P * r + P], ones[:, 0:1], start=True, stop=True)
                    mm(ps[:, b, :], rotm, qk[:, i, CTX:T], start=True, stop=True).then_inc(sem("acc_ready"), 1)
                elif kind == "squares":
                    pe.wait_ge(sem("hsq_ready"), i + 1)
                    open_group(g)
                    for c, (t0, w) in enumerate(L0):
                        q = mm(ring(g, L0)[:, c, :], ones, sq[:, i % 2, t0:t0 + w], start=True, stop=True)
                    q.then_inc(sem("acc_ready"), 1)
                elif kind == "rows":
                    open_group(g)
                    n = unit_of_ada(2 * i)
                    ada_rows(2 * (g % 4), (n, n + 1)).then_inc(sem("acc_ready"), 1)
                elif kind == "cols":
                    pe.wait_ge(sem("acc_taken"), seq.index(("rows", i)) + 1)
                    open_group(g)
                    ada_cols(ps[:, 2 * (g % 4), 0:8], row_buf(i)).then_inc(sem("acc_ready"), 1)
                else:
                    pe.wait_ge(sem("w_split"), 6)
                    open_group(g)
                    for k in range(KT):
                        q = split_matmul(ring(g, [(0, 256)]), h_hi[:, k, P * i:P * i + P], h_lo[:, k, P * i:P * i + P],
                                         wh[:, k, :], wl[:, k, :], [(0, 256)], k == 0, k == KT - 1)
                    q.then_inc(sem("acc_ready"), 1)
            pe.wait_ge(sem("acc_taken"), len(seq))

            pe.wait_ge(sem("q_roped"), HEADS + KVH)
            pe.wait_ge(sem("k_normed"), KVH)

            def scores(t):
                hd, q0, nk = att[t // 2]
                if t >= 2:
                    pe.wait_ge(sem("exp_done"), t - 1)
                lhs = qk[:, hd, q0 + P * (t % 2):q0 + P * (t % 2) + P]
                key = qk[:, HEADS + hd // 4, :]
                chunks = L0 if nk == 6 else [(0, 256)]
                for c, (t0, w) in enumerate(chunks):
                    q = mm(ps[:, 2 * (t % 2) + c, 0:w], lhs, key[:, t0:t0 + w], start=True, stop=True)
                q.then_inc(sem("s_ready"), 1)

            scores(0)
            scores(1)
            def transpose_rows(u):
                for t in (2 * u, 2 * u + 1):
                    pe.wait_ge(sem("p_ready"), t + 1)
                    if t == 2 * u and u >= 1:
                        pe.wait_ge(sem("pT_act"), u)
                        if wide_units(u):
                            pe.wait_ge(sem("pT_dve"), wide_units(u))
                    for kt in range(att[u][2]):
                        o = 256 * (kt % 2) + P * (t % 2)
                        q = nc.tensor.transpose(ps[:, 4 + kt // 2, o:o + P], prob_rows(t)[:, P * kt:P * kt + P], ident)
                    q.then_inc(sem("pT_ready"), 1)

            def weigh_values(u):
                hd, _, nk = att[u]
                pe.wait_ge(sem("pT_act"), u + 1)
                if nk == 6:
                    pe.wait_ge(sem("pT_dve"), wide_units(u + 1))
                if u >= 1:
                    pe.wait_ge(sem("o_taken"), u)
                for kt in range(nk):
                    q = mm(ps[:, 7, 0:256], vt[:, kt, HD * (hd // 4):HD * (hd // 4) + HD],
                           pT[:, u % 2, kt, :], start=kt == 0, stop=kt == nk - 1)
                q.then_inc(sem("o_ready"), 1)

            for u in range(len(att)):
                for t in (2 * u, 2 * u + 1):
                    if t + 2 < 2 * len(att):
                        scores(t + 2)
                transpose_rows(u)
                if u >= 1:
                    weigh_values(u - 1)
            weigh_values(len(att) - 1)
            pe.wait_ge(sem("o_taken"), len(att))

            for u in range(4):
                for j in range(2):
                    tile(6 + u, j, G_WO + 2 * u + j, KT, h_tile, L0)
            pe.wait_ge(sem("acc_taken"), G_MLP0)
            norm_sum(1)
            norm_sum(2)

            def mlp(l, m0, n0, h_base, chunks):
                def hidden(m, group, i=0, static=True, moving=h_tile):
                    for j in range(2):
                        tile(m, j, g_hidden(l, group, j), KT, moving if j == 0 else h_tile, chunks,
                             double_groups(l) * i, 4 * i, static)

                def output(m, step, i=0, static=True, js=range(KT)):
                    slot = 2 * (step % 2)
                    pe.wait_ge(sem("a_split"), 2 * NG * l + 2 * step + 2 + 4 * i)
                    for j in js:
                        tile(m, j, g_out(l, step, j), 2, lambda k: (a_hi[:, slot + k, :], a_lo[:, slot + k, :]), chunks,
                             double_groups(l) * i, 4 * i, static)

                def double(i, with_ada, static=False):
                    s0, m1 = (12, m0 + 25) if static else (0, m0 + 1)
                    for st in range(2):
                        hidden(m1 + 2 * st, s0 + st + 1, i, static)
                        if with_ada:
                            g = g_rows(st)
                            n = n0 + 2 + 4 * st
                            open_group(g, 24 * i, False)
                            ada_rows(2 * (g % 4), (n, n + 2), 32 * i).then_inc(sem("acc_ready"), 1)
                            output(m1 + 1 + 2 * st, s0 + st, i, static, range(4))
                            g = g_cols(st)
                            pe.wait_ge(sem("acc_taken"), g_rows(st) + 1 + 24 * i)
                            open_group(g, 24 * i, False)
                            ada_cols(ps[:, 2 * (g % 4), 0:8], rst[:, 0:512]).then_inc(sem("acc_ready"), 1)
                            output(m1 + 1 + 2 * st, s0 + st, i, static, range(4, KT))
                        else:
                            output(m1 + 1 + 2 * st, s0 + st, i, static)

                hidden(m0, 0, moving=h_tile_after(h_base))
                with pe.Fori(0, 6) as i:
                    double(i, l == 0)
                double(0, False, True)
                hidden(m0 + 29, 15)
                output(m0 + 30, 14)
                output(m0 + 31, 15)

            mlp(0, M_MLP0, N_MLP0, KT, L0)
            pe.wait_ge(sem("acc_taken"), G_GLU)
            norm_sum(3)

            def turn(i, srcs):
                if i >= 4:
                    wait_turned(pe, i - 4)
                for c, (src, p, w) in enumerate(srcs):
                    q = nc.tensor.transpose(ps[0:w, turn_bank(i), P * c:P * c + p], src, ident[0:p, 0:p])
                q.then_inc(sem("turned"), 1)

            pe.wait_ge(sem("c_ready"), 1)
            i = 0
            for lo in (0, 1):
                for c0 in range(0, SC, 4):
                    turn(i, [(bc_src(lo, False, c), P, P) for c in range(c0, c0 + 4)])
                    i += 1
            norm_sum(4)
            pe.wait_ge(sem("powers_ready"), 1)
            for r in range(2):
                for e0 in (0, 4, 8):
                    turn(i, [(pow_src(r, e), P, P) for e in range(e0, min(e0 + 4, 9))])
                    i += 1
            pe.wait_ge(sem("b_re"), 1)
            pe.wait_ge(sem("b_im"), 1)
            for lo in (1, 0):
                if lo == 0:
                    pe.wait_ge(sem("b_minus_im"), 1)
                for c0 in range(0, SC, 4):
                    turn(i, [(bc_src(lo, True, c), P, P) for c in range(c0, c0 + 4)])
                    i += 1
            pe.wait_ge(sem("h1_ready"), KT)
            wait_turned(pe, i - 1)
            wait_turned(pe, i - 2)
            for t in range(CH):
                for half in range(2):
                    turn(i, [(h1[:, 4 * half + k, t, :], P, NCH) for k in range(4)])
                    i += 1
            wait_turned(pe, i - 1)
            wait_turned(pe, i - 2)
            for b in range(16):
                wait_turned(pe, i - 4)
                for c in range(4):
                    q = nc.tensor.transpose(ps[:, turn_bank(i), NCH * c:NCH * c + NCH],
                                            htok[0:NCH, 4 * b + c, :, :].rearrange("p t c -> p (t c)"),
                                            ident[0:NCH, 0:NCH])
                q.then_inc(sem("turned"), 1)
                i += 1
            wait_turned(pe, i - 1)
            wait_turned(pe, i - 2)

            def input_matrices(j):
                b, d = j // 2, j % 2
                pe.wait_ge(sem("wp_sum"), j + 1)
                if j >= 2:
                    pe.wait_ge(sem("wT_taken"), j - 1)
                for g in range(8):
                    q = nc.tensor.transpose(ps[:, wT_bank(j) + g // 4, P * (g % 4):P * (g % 4) + P], in_matrices(j)[:, g, :], ident)
                q.then_inc(sem("wT_ready"), 1)
                if d == 0 and b >= 2:
                    pe.wait_ge(sem("kf_taken"), b - 1)
                for g in range(8):
                    g0 = SC * (GROUPS * d + 8 * b + g)
                    c0 = 256 * d + P * (g // 4)
                    q = mm(kernel_bank(b)[32 * (g % 4):32 * (g % 4) + 32, c0:c0 + P], pv[:, g0:g0 + 32], in_matrices(j)[:, g, :],
                           start=True, stop=True)
                q.then_inc(sem("kf_ready"), 1)

            def chunk_inputs(j):
                pe.wait_ge(sem("wT_taken"), j + 1)
                if j >= 1:
                    pe.wait_ge(sem("bu_taken"), j)
                    pe.wait_ge(sem("bu_taken_dve"), j)
                for r in range(2):
                    for g in range(8):
                        q = mm(ps[64 * (g % 2):64 * (g % 2) + 64, 3 + r, NCH * (g // 2):NCH * (g // 2) + NCH],
                               wT[:, g, NP * r:NP * r + NP], U[:, 8 * (j // 2) + g, :], start=True, stop=True)
                q.then_inc(sem("bu_ready"), 1)

            def within_chunks(b):
                for h in range(4):
                    if b:
                        pe.wait_ge(sem("ml_taken"), 4 * (b - 1) + h + 1)
                    for t in range(4):
                        tt = 4 * (h % 2) + t
                        q = nc.tensor.transpose(ps[:, h, P * t:P * t + P],
                                                kernels(b)[:, h // 2, SC * (7 - tt):SC * (7 - tt) + P], ident)
                    q.then_inc(sem("ml_ready"), 1)

            def chunk_outputs(b):
                pe.wait_ge(sem("ml_taken"), 4 * b + 4)
                for hf in range(2):
                    i2 = 2 * b + hf
                    if i2 >= 2:
                        pe.wait_ge(sem("yl_taken"), i2 - 1)
                    for g in range(4):
                        q = mm(ps[0:NCL, 6 + hf, P * g:P * g + P], U[:, 8 * b + 4 * hf + g, NCC:NCH],
                               ml[:, 4 * hf + g, :, :].rearrange("p t c -> p (t c)"), start=True, stop=True)
                    q.then_inc(sem("yl_ready"), 1)

            input_matrices(0)
            for j in range(16):
                if j + 1 < 16:
                    input_matrices(j + 1)
                chunk_inputs(j)
            pe.wait_ge(sem("kf_taken"), 8)
            pe.wait_ge(sem("wT_taken"), 16)
            pe.wait_ge(sem("bu_taken"), 16)
            pe.wait_ge(sem("bu_taken_dve"), 16)
            for b in range(8):
                within_chunks(b)
                chunk_outputs(b)

            def outputs_turned(k):
                if k >= 4:
                    pe.wait_ge(sem("g_ready"), k - 3)
                pe.wait_ge(sem("ys_taken"), 2 * k + 2)
                for t in range(CH):
                    q = nc.tensor.transpose(ps[:, 4 + k % 4, NCL * t:NCL * t + NCL], ytok[0:NCL, k, t, :],
                                            ident[0:NCL, 0:NCL])
                q.then_inc(sem("yT_ready"), 1)

            pe.wait_ge(sem("restacked"), 4)
            pe.wait_ge(sem("restacked_act"), 4)
            pe.wait_ge(sem("ml_taken"), 32)
            for b in range(8):
                if b < POOL_BLOCKS:
                    pe.wait_ge(sem("xv_pool"), 2 * b + 2)
                else:
                    pe.wait_ge(sem("wp_sum"), 16 + 2 * (b - POOL_BLOCKS) + 2)
                for hf in range(2):
                    i2 = 2 * b + hf
                    if i2 >= 4:
                        pe.wait_ge(sem("ys_taken"), i2 - 3)
                    for g in range(4):
                        for d in range(2):
                            q = mm(ps[0:NCL, i2 % 4, P * g:P * g + P], sst[:, d, 8 * b + 4 * hf + g, :],
                                   xv_tile(b, d)[:, 4 * hf + g, :], start=d == 0, stop=d == 1)
                    q.then_inc(sem("ys_ready"), 1)
                if 1 <= b <= 4:
                    outputs_turned(b - 1)
            for k in range(4, KT):
                outputs_turned(k)
            for u in range(4):
                for j in range(2):
                    tile(M_GLU + u, j, G_GLU + 2 * u + j, KT, h_tile if u or j else h_tile_after(2 * KT), L1)
            pe.wait_ge(sem("acc_taken"), G_MLP1)
            norm_sum(5)
            norm_sum(6)
            mlp(1, M_MLP1, N_MLP1, 3 * KT, L1)
            pe.wait_ge(sem("acc_taken"), G_MLP1 + 10 * NG)
            norm_sum(7)
            for half in range(2):
                wait_x(pe, 3, 4 * half + 2)
                wait_x(pe, 3, 4 * half + 3)
                for r in range(4):
                    for k in range(4):
                        q = nc.tensor.transpose(ps[:, 4 * half + r, P * k:P * k + P],
                                                xT[:, 4 * half + k, CTX + P * r:CTX + P * r + P], ident)
                    q.then_inc(sem("oT_ready"), 1)

        @block.scalar
        def _(act):
            A_ = nc.scalar.activation

            act.dma_start(consts[:, :], a["consts"][:, 0:3 * P]).then_inc(sem("const_in"), 16)
            act.dma_start(cmask[:, :], a["consts"][:, 3 * P:3 * P + SC]).then_inc(sem("const_in"), 16)
            act.dma_start(rope[:, 0:2 * SEQ], a["consts"][:, 3 * P + SC:]).then_inc(sem("rope_in"), 16)
            for r0, src in ((0, a["c"][0]), (8, a["c_ctx"]), (16, a["norm_g"]), (80, a["s5_glu_b"]),
                            (88, a["gqa_q_norm"]), (89, a["gqa_k_norm"])):
                names = " ".join("abc"[:len(src.shape)])
                flat = src.rearrange(f"{names} -> ({names})") if len(src.shape) > 1 else src
                v = flat.rearrange("(r n) -> r n", n=P)
                act.dma_start(rows[r0:r0 + v.shape[0], 0, :], v).then_inc(sem("rows_in"), 16)
            act.dma_start(rows[0:96, 1, :], a["ada_b"].rearrange("l n -> (l n)").rearrange("(r n) -> r n", n=P)) \
                .then_inc(sem("rows_in"), 16)

            def split_hi(m, n, gi=0, ni=0):
                act.wait_ge(sem(f"raw_landed{n % NRAW}"), 16 * (n // NRAW + 1) + ni)
                if m >= 2:
                    act.wait_ge(sem("acc_ready"), groups_after(m - 2) + gi)
                A_(w_hi[:, m % 2, :], raw[:, n % NRAW, :], ACT.Copy).then_inc(sem("w_hi_done"), 1)

            def norm_rstd(n, src_ready):
                ch = norm_chunks(n)
                w = sum(c[1] for c in ch)
                for k in range(KT):
                    src_ready(k)
                    if k >= 2:
                        act.wait_ge(sem("sq_used"), KT * n + k - 1)
                    A_(sq[:, k % 2, 0:w], norm_src(n, k), ACT.Square).then_inc(sem("sq_ready"), 1)
                A_(warm[:, n:n + 1], epsc[:, :], ACT.Ln)
                act.wait_ge(sem("sq_used"), KT * (n + 1))
                A_(by_chunk(rst[:, 0:w], ch), banks(0, ch), ACT.Ln, bias=epsc[:, :], scale=1.0 / D) \
                    .then_inc(sem("rln_done"), 1)
                act.wait_ge(sem("rln_done"), n + 1)
                A_(rst[:, 0:w], rst[:, 0:w], ACT.Exp, scale=-0.5).then_inc(sem("rstd_ready"), 1)

            def h_heads(l, i, base, segs):
                for k in range(KT):
                    act.wait_ge(sem("h_scaled"), base + k + 1)
                    for t0, m, v in segs:
                        q = A_(h_hi[:, k, t0:t0 + m], tmp[:, k % 2, t0:t0 + m], ACT.Identity,
                               bias=mod[:, l, 3 * i, k, v:v + 1])
                    q.then_inc(sem("h_hi_done"), 1)

            def turns_out(i0, i1):
                for i in range(i0, i1):
                    if act_turn(i):
                        act.wait_ge(sem("turned"), i + 1)
                        dst, src = turn_out(i)
                        A_(dst, src, ACT.Copy).then_inc(sem("turned_act"), 1)

            for r in range(6):
                if r == 0:
                    act.wait_ge(sem("cols_taken"), 1)
                    act.wait_ge(sem("sil_zero"), 1)
                    A_(sil[:, :, 0:2], cols[:, 0:16].rearrange("p (v k) -> p k v", v=2), ACT.Silu) \
                        .then_inc(sem("sil_ready"), 1)
                act.wait_ge(sem("xT_ready"), 2 * r + 1)
                A_(xT[:, 0:4, P * r:P * r + P], ps[:, (2 * r) % 6, :].rearrange("p (k t) -> p k t", k=4), ACT.Copy) \
                    .then_inc(sem("xT_act"), 1)
            act.wait_ge(sem("eps_set"), 1)

            def x_there(k):
                if k == 0:
                    act.wait_ge(sem("xT_act"), 6)
                    act.wait_ge(sem("xT_dve"), 6)
            norm_rstd(0, x_there)
            split_hi(0, unit_of_split(0))
            h_heads(0, 0, 0, SEG0)

            act.wait_ge(sem("sq_used"), KT)
            for hd in range(HEADS + KVH):
                act.wait_ge(sem("acc_ready"), seq.index(("head", hd)) + 1)
                if hd >= 2:
                    act.wait_ge(sem("acc_ready"), seq.index(("turn", hd - 2)) + 1)
                A_(by_chunk(sq[:, hd % 2, :], L0), ring(seq.index(("head", hd)), L0), ACT.Square, scale=HD ** -0.5) \
                    .then_inc(sem("hsq_ready"), 1)
                if hd % 2:
                    m = (hd + 1) // 2
                    split_hi(m, unit_of_split(m))

            def key_rms(hd):
                return sq[:, hd % 2, :]

            act.wait_ge(sem("acc_taken"), seq.index(("turn", HEADS - 1)) + 1)
            A_(q_rms[:, :], q_rms[:, :], ACT.Ln, bias=epsc[:, :]).then_inc(sem("hln_done"), 1)
            for hd in (HEADS, HEADS + 1):
                act.wait_ge(sem("acc_taken"), seq.index(("squares", hd)) + 1)
                A_(key_rms(hd), tmp[:, hd % 2, :], ACT.Ln, bias=epsc[:, :]).then_inc(sem("hln_done"), 1)
            act.wait_ge(sem("hln_done"), 3)
            for hd in (HEADS, HEADS + 1):
                A_(key_rms(hd), key_rms(hd), ACT.Exp, scale=-0.5).then_inc(sem("k_rstd"), 1)
            A_(q_rms[:, :], q_rms[:, :], ACT.Exp, scale=-0.5).then_inc(sem("q_rstd"), 1)
            act.wait_ge(sem("q_rstd"), 1)
            split_hi(6, unit_of_split(6))

            def softmax_exp(t):
                nk = att[t // 2][2]
                ch = L0 if nk == 6 else [(0, 256)]
                act.wait_ge(sem("nmax_ready"), t + 1)
                if t >= 4:
                    act.wait_ge(sem("pT_ready"), t - 3)
                A_(by_chunk(prob_rows(t)[:, 0:P * nk], ch), banks(2 * (t % 2), ch), ACT.Exp,
                   bias=nmax[:, t % 4:t % 4 + 1], scale=q_scale(t), accum_out=rsum[:, t % 4:t % 4 + 1]).then_inc(sem("exp_done"), 1)

            softmax_exp(0)
            softmax_exp(1)
            def output_head(u):
                hd, q0, _ = att[u]
                act.wait_ge(sem("o_ready"), u + 1)
                A_(h_hi[:, hd, q0:q0 + 256], ps[:, 7, 0:256], ACT.Copy).then_inc(sem("o_hi_done"), 1)

            for u, (_, _, nk) in enumerate(att):
                for t in (2 * u + 2, 2 * u + 3):
                    if t < 2 * len(att):
                        softmax_exp(t)
                act.wait_ge(sem("pT_ready"), 2 * u + 2)
                if u >= 2:
                    act.wait_ge(sem("o_ready"), u - 1)
                for b in ((0, 2) if nk == 6 else (0,)):
                    q = A_(pT[:, u % 2, 2 * b:2 * b + 2, :], ps[:, 4 + b, :].rearrange("p (k t) -> p k t", k=2), ACT.Copy)
                q.then_inc(sem("pT_act"), 1)
                if u >= 1:
                    output_head(u - 1)
            output_head(len(att) - 1)
            for u in range(1, 4):
                split_hi(6 + u, unit_of_split(6 + u))
            split_hi(M_MLP0, N_MLP0)

            def y_there(g0):
                def f(k):
                    act.wait_ge(sem("acc_taken"), g0 + k + 1)
                return f

            def x_updated(branch):
                def f(k):
                    wait_x(act, branch, k)
                return f

            norm_rstd(1, y_there(G_WO))
            norm_rstd(2, x_updated(0))
            h_heads(0, 1, KT, SEG0)

            def mlp(l, m0, n0, chunks, period):
                w = sum(c[1] for c in chunks)
                dg = double_groups(l)

                def hidden(group, i=0):
                    for j in range(2):
                        g = g_hidden(l, group, j)
                        act.wait_ge(sem("acc_ready"), g + 1 + dg * i)
                        if group >= 1:
                            act.wait_ge(sem("acc_taken"), g_hidden(l, group - 1, j) + 1 + dg * i)
                        A_(by_chunk(sq[:, j, 0:w], chunks), ring(g, chunks), ACT.Relu).then_inc(sem("relu_done"), 1)
                        act.wait_ge(sem("acc_taken"), g + 1 + dg * i)
                        if group >= 2:
                            act.wait_ge(sem("acc_ready"), g_out(l, group - 2, KT - 1) + 1 + dg * i)
                        A_(a_hi[:, 2 * (group % 2) + j, 0:w], tmp[:, j, 0:w], ACT.Copy).then_inc(sem("a_hi_done"), 1)

                split_hi(m0 + 1, n0 + 1)
                hidden(0)

                def double(i, rel):
                    landed = 4 * period * i
                    for st in range(2):
                        step = 2 * rel + st
                        m, n = m0 + 2 + 2 * st, n0 + 1 + (2 * st + 1) * period // 4
                        split_hi(m, n, dg * i, landed)
                        hidden(step + 1, i - rel)
                        split_hi(m + 1, n + period // 4, dg * i, landed)

                double(0, 0)
                with act.Fori(1, 6 if period == 8 else 7) as i:
                    double(i, 1)
                if period == 8:
                    n = n0 + 49
                    for st in range(2):
                        split_hi(m0 + 26 + 2 * st, n + 1 + 2 * st)
                        hidden(13 + st)
                        split_hi(m0 + 27 + 2 * st, n + 2 + 2 * st)
                    n = n0 + 53
                else:
                    n = n0 + 29
                split_hi(m0 + 30, n + 1)
                hidden(15)
                split_hi(m0 + 31, n + 2)

            mlp(0, M_MLP0, N_MLP0, L0, 8)
            norm_rstd(3, y_there(G_GLU - 8))

            act.wait_ge(sem("s5_in"), 16 * 7)
            A_(dtc, dtl, ACT.Exp).then_inc(sem("dt_ready"), 1)
            act.wait_ge(sem("lam_dt"), 1)
            A_(mag, lr, ACT.Exp).then_inc(sem("mag_ready"), 1)
            act.wait_ge(sem("angles"), 1)
            A_(sn, ang, ACT.Sin)
            A_(cs, ang2, ACT.Sin).then_inc(sem("sin_ready"), 1)
            turns_out(0, C_TURNS)
            norm_rstd(4, x_updated(1))

            for k in range(KT):
                act.wait_ge(sem("h1_scaled"), k + 1)
                for t0, m, v in SEG0:
                    c0 = 0 if v else NCC
                    q = A_(h1[:, k, :, c0:c0 + m // CH], tmp[:, k % 2, t0:t0 + m].rearrange("p (t c) -> p t c", t=CH),
                           ACT.Identity, bias=mod[:, 1, 0, k, v:v + 1])
                q.then_inc(sem("h1_ready"), 1)
            act.wait_ge(sem("b_im"), 1)
            A_(b_out[:, 0, :, :], b_out[:, 2, :, :], ACT.Copy, scale=-1.0).then_inc(sem("b_minus_im"), 1)
            turns_out(C_TURNS, TURNS)

            def matrices_out(j):
                act.wait_ge(sem("wT_ready"), j + 1)
                if j >= 1:
                    act.wait_ge(sem("bu_ready"), j)
                A_(wT[:, :, :], ps[:, wT_bank(j):wT_bank(j) + 2, :].rearrange("p a (b n) -> p (a b) n", n=P), ACT.Copy) \
                    .then_inc(sem("wT_taken"), 1)

            matrices_out(0)
            for j in range(16):
                b, d = j // 2, j % 2
                if d:
                    act.wait_ge(sem("kf_ready"), j + 1)
                    if b == 0:
                        wait_turned(act, TURNS - 1)
                        wait_turned(act, TURNS - 2)
                    kp = kernel_bank(b).rearrange("p (d q n) -> p d q n", d=2, q=2)
                    A_(kernels(b)[:, :, 0:P], kp[:, 0, :, :], ACT.Copy)
                    A_(kernels(b)[:, :, P:15 * SC], kp[:, 1, :, SC:P], ACT.Copy).then_inc(sem("kf_copied"), 1)
                if j + 1 < 16:
                    matrices_out(j + 1)
                chunk_inputs_out(act, lambda o, i_: A_(o, i_, ACT.Copy), j, 0).then_inc(sem("bu_taken"), 1)
            for b in range(8):
                for h in range(4):
                    act.wait_ge(sem("ml_ready"), 4 * b + h + 1)
                    if h == 0 and b >= 1:
                        act.wait_ge(sem("yl_ready"), 2 * b)
                    src = ps[:, h, :].rearrange("p (t g c) -> p t g c", t=4, g=4)[:, :, :, 0:SC]
                    dst = ml[:, 4 * (h // 2):4 * (h // 2) + 4, 4 * (h % 2):4 * (h % 2) + 4, :] \
                        .rearrange("p g t c -> p t g c")
                    A_(dst, src, ACT.Copy).then_inc(sem("ml_taken"), 1)
                for hf in range(2):
                    act.wait_ge(sem("yl_ready"), 2 * b + hf + 1)
                    A_(out_half(b, hf), ps[0:NCL, 6 + hf, :].rearrange("p (g t c) -> p g t c", g=4, t=CH), ACT.Copy) \
                        .then_inc(sem("yl_taken"), 1)
            for d in range(2):
                for r in range(2):
                    restack(act, lambda o, i_: A_(o, i_, ACT.Copy), d, 1, r)

            for k in range(KT):
                if k == 0:
                    act.wait_ge(sem("ys_ready"), 16)
                act.wait_ge(sem("yT_ready"), k + 1)
                A_(ybuf[:, k, 0:SEQ], ps[:, 4 + k % 4, :], ACT.Gelu_apprx_tanh).then_inc(sem("g_ready"), 1)
                act.wait_ge(sem("g_ready"), k + 1)
                A_(h_hi[:, k, 0:SEQ], ybuf[:, k, 0:SEQ], ACT.Copy).then_inc(sem("h_hi_done"), 1)
            for u in range(4):
                split_hi(M_GLU + u, N_GLU + u) if u == 0 else None
                if u + 1 < 4:
                    split_hi(M_GLU + u + 1, N_GLU + u + 1)
                else:
                    split_hi(M_MLP1, N_MLP1)
                for j in range(2):
                    g = G_GLU + 2 * u + j
                    act.wait_ge(sem("acc_ready"), g + 1)
                    if 2 * u + j >= 2:
                        act.wait_ge(sem("acc_taken"), g - 1)
                    A_(sq[:, j, 0:SEQ], ring(g, L1)[:, 0, :], ACT.Sigmoid, bias=cols[:, 80 + 2 * u + j:81 + 2 * u + j]) \
                        .then_inc(sem("sig_ready"), 1)
            act.wait_ge(sem("acc_taken"), G_MLP1)
            norm_rstd(5, y_there(G_GLU))
            norm_rstd(6, x_updated(2))
            h_heads(1, 1, 2 * KT, [(0, SEQ, 0)])
            mlp(1, M_MLP1, N_MLP1, L1, 4)
            norm_rstd(7, y_there(G_MLP1 + 10 * NG - 8))
            for r in range(4):
                act.wait_ge(sem("oT_ready"), r + 1)
                A_(otok[:, r, 0:512], ps[:, r, :], ACT.Copy).then_inc(sem("o_act"), 1)

        @block.vector
        def _(dve):
            TT = nc.vector.tensor_tensor
            STT = nc.vector.scalar_tensor_tensor
            TS = nc.vector.tensor_scalar
            CP = nc.vector.tensor_copy
            linked = [0]

            def link(q):
                linked[0] += 1
                q.then_inc(sem("dve_step"), 1)
                dve.wait_ge(sem("dve_step"), linked[0])

            def split_lo(m, mi=0):
                dve.wait_ge(sem("w_hi_done"), m + 1 + mi)
                raw_n = unit_of_split(m)
                for p in range(2):
                    s = slice(1024 * p, 1024 * p + 1024)
                    q = TT(w_lo[:, m % 2, s], raw[:, raw_n % NRAW, s], w_hi[:, m % 2, s].bitcast(F32), ALU.subtract)
                q.then_inc(sem("w_split"), 1)

            def mods(l, j):
                b = adab[:, 48 * l + 8 * j:48 * l + 8 * j + 8].unsqueeze(2).to_broadcast([P, KT, 2])
                q = TT(mod[:, l, j, :, :], mod[:, l, j, :, :], b, ALU.add)
                if j == 2 or j == 5:
                    link(q)
                    g = gain(l, 1 if j == 2 else 3)
                    q = TT(coef[:, l, 1 if j == 2 else 3, :, :], mod[:, l, j, :, :], g, ALU.mult)
                elif j == 1 or j == 4:
                    link(q)
                    q = STT(coef[:, l, 0 if j == 1 else 2, :, :], mod[:, l, j, :, :], 1.0, gain(l, 0 if j == 1 else 2),
                            ALU.add, ALU.mult)
                q.then_inc(sem("mod_ready"), 1)

            def gain(l, i):
                c0 = 16 + (4 * l + i) * KT
                return cols[:, c0:c0 + KT].unsqueeze(2).to_broadcast([P, KT, 2])

            def scale(l, i, k, segs, x0):
                for t0, m, v in segs:
                    q = STT(tmp[:, k % 2, t0:t0 + m], xT[:, k, x0 + t0:x0 + t0 + m], coef[:, l, 2 * i, k, v:v + 1],
                            rst[:, t0:t0 + m], ALU.mult, ALU.mult)
                return q

            def apply_norm(l, i, n, base, segs, x0, w, before=None):
                dve.wait_ge(sem("rstd_ready"), n + 1)

                def rest(k):
                    dve.wait_ge(sem("h_hi_done"), base + k + 1)
                    for t0, m, v in segs:
                        q = STT(h_lo[:, k, t0:t0 + m], tmp[:, k % 2, t0:t0 + m], mod[:, l, 3 * i, k, v:v + 1],
                                h_hi[:, k, t0:t0 + m].bitcast(F32), ALU.add, ALU.subtract)
                    q.then_inc(sem("h_split"), 1)

                for k in range(KT):
                    if before:
                        before(k)
                    if k >= 2:
                        dve.wait_ge(sem("h_split"), base + k - 1)
                    scale(l, i, k, segs, x0).then_inc(sem("h_scaled"), 1)
                    if k >= 1:
                        rest(k - 1)
                rest(KT - 1)

            def add_branch(l, i, n, branch, segs, x0, w):
                dve.wait_ge(sem("rstd_ready"), n + 1)
                for k in range(KT):
                    if k >= 2:
                        wait_x(dve, branch, k - 2)
                    for t0, m, v in segs:
                        q = STT(tmp[:, k % 2, t0:t0 + m], ybuf[:, k, t0:t0 + m], coef[:, l, 2 * i + 1, k, v:v + 1],
                                rst[:, t0:t0 + m], ALU.mult, ALU.mult)
                    if k % 2:
                        q.then_inc(sem("branch_scaled"), 1)
                    else:
                        link(q)
                        TT(xT[:, k, x0:x0 + w], xT[:, k, x0:x0 + w], tmp[:, 0, 0:w], ALU.add).then_inc(sem("x_added"), 1)

            dve.wait_ge(sem("cols_ready"), 1)
            CP(cols[:, 0:90], ps[:, 6, 0:90])
            link(CP(adab[:, :], ps[:, 6, 128:224]))
            TS(cols[:, 89:90], cols[:, 89:90], HD ** -0.5, None, ALU.mult).then_inc(sem("cols_taken"), 1)
            for r in range(6):
                dve.wait_ge(sem("xT_ready"), 2 * r + 2)
                CP(xT[:, 4:8, P * r:P * r + P], ps[:, (2 * r + 1) % 6, :].rearrange("p (k t) -> p k t", k=4)) \
                    .then_inc(sem("xT_dve"), 1)

            def rows_out(s):
                dve.wait_ge(sem("rows_ready"), s + 1)
                CP(row_buf(s), ps[:, 6 - s % 2, :]).then_inc(sem("rows_taken"), 1)

            def shift_and_scale(s):
                dve.wait_ge(sem("cols_done"), s + 1)
                dve.wait_ge(sem("cols_taken"), 1)
                k = slice(2 * s, 2 * s + 2)
                for j in range(2):
                    b = adab[:, 8 * j + 2 * s:8 * j + 2 * s + 2].unsqueeze(2).to_broadcast([P, 2, 2])
                    q = TT(mod[:, 0, j, k, :], first_cols(s)[:, 4 * j:4 * j + 4].rearrange("p (k v) -> p k v", v=2),
                           b, ALU.add)
                link(q)
                link(STT(coef[:, 0, 0, k, :], mod[:, 0, 1, k, :], 1.0, gain(0, 0)[:, k, :], ALU.add, ALU.mult))

            def between_tiles(k):
                if k == 3:
                    rows_out(3)
                    split_lo(0)
                elif k == 6:
                    shift_and_scale(3)

            for s in range(3):
                rows_out(s)
                shift_and_scale(s)
            apply_norm(0, 0, 0, 0, SEG0, 0, T, between_tiles)
            dve.wait_ge(sem("rope_in"), 16)
            for g, (kind, i) in enumerate(seq):
                dve.wait_ge(sem("acc_ready"), g + 1)
                if kind == "head":
                    gc = 88 if i < HEADS else 89
                    dve.wait_ge(sem("hsq_ready"), i + 1)
                    TS(by_chunk(qk[:, i, :], L0), ring(g, L0), cols[:, gc:gc + 1], None, ALU.mult) \
                        .then_inc(sem("acc_taken"), 1)
                    if i % 2:
                        split_lo((i + 1) // 2)
                elif kind == "turn":
                    q, b, t = qk[:, i, CTX:T], 2 * (g % 4), tmp[:, i % 2, 0:SEQ]
                    if i < HEADS:
                        CP(q_rms[:, 6 * i:6 * i + 6], ps[:, b + 1, 0:6])
                    if i >= 2:
                        dve.wait_ge(sem("q_roped"), i - 1)
                    TT(t, ps[:, b, :], rope[:, SEQ:2 * SEQ], ALU.mult).then_inc(sem("acc_taken"), 1)
                    dve.wait_ge(sem("acc_taken"), seq.index(("head", i)) + 1)
                    link(TT(q, q, rope[:, 0:SEQ], ALU.mult))
                    dve.wait_ge(sem("acc_taken"), g + 1)
                    TT(q, q, t, ALU.add).then_inc(sem("q_roped"), 1)
                elif kind == "squares":
                    dve.wait_ge(sem("q_roped"), i + 1)
                    CP(by_chunk(tmp[:, i % 2, :], L0), ring(g, L0)).then_inc(sem("acc_taken"), 1)
                elif kind == "rows":
                    CP(row_buf(i), ps[:, 2 * (g % 4), :]).then_inc(sem("acc_taken"), 1)
                elif kind == "cols":
                    CP(mod_cols[:, 8 * i:8 * i + 8], ps[:, 2 * (g % 4), 0:8]).then_inc(sem("acc_taken"), 1)
                else:
                    CP(vt[:, i, :], ring(g, [(0, 256)])[:, 0, :]).then_inc(sem("acc_taken"), 1)
                    if i == 4:
                        dve.wait_ge(sem("q_roped"), HEADS + KVH)
                        for hd in (HEADS, HEADS + 1):
                            dve.wait_ge(sem("k_rstd"), hd - HEADS + 1)
                            TT(qk[:, hd, :], qk[:, hd, :], sq[:, hd % 2, :], ALU.mult).then_inc(sem("k_normed"), 1)
            def row_max(t):
                nk = att[t // 2][2]
                ch = L0 if nk == 6 else [(0, 256)]
                dve.wait_ge(sem("s_ready"), t + 1)
                m = nmax[:, t % 4:t % 4 + 1]
                link(nc.vector.tensor_reduce(m, banks(2 * (t % 2), ch), AX.XY, ALU.max, negate=True))
                TT(m, m, q_scale(t), ALU.mult).then_inc(sem("nmax_ready"), 1)

            def normalise(t):
                nk = att[t // 2][2]
                dve.wait_ge(sem("exp_done"), t + 1)
                link(nc.vector.reciprocal(rinv[:, t % 4:t % 4 + 1], rsum[:, t % 4:t % 4 + 1]))
                TS(prob_rows(t)[:, 0:P * nk], prob_rows(t)[:, 0:P * nk], rinv[:, t % 4:t % 4 + 1], None, ALU.mult) \
                    .then_inc(sem("p_ready"), 1)

            dve.wait_ge(sem("q_rstd"), 1)
            row_max(0)
            row_max(1)
            normalise(0)
            normalise(1)
            for j in range(2, 6):
                mods(0, j)
            split_lo(6)
            def output_rest(u):
                hd, q0, _ = att[u]
                dve.wait_ge(sem("o_hi_done"), u + 1)
                TT(h_lo[:, hd, q0:q0 + 256], ps[:, 7, 0:256],
                   h_hi[:, hd, q0:q0 + 256].bitcast(F32), ALU.subtract).then_inc(sem("o_taken"), 1)

            for u, (_, _, nk) in enumerate(att):
                if u + 1 < len(att):
                    row_max(2 * u + 2)
                    row_max(2 * u + 3)
                    normalise(2 * u + 2)
                    normalise(2 * u + 3)
                dve.wait_ge(sem("pT_ready"), 2 * u + 2)
                if nk == 6:
                    if u >= 2:
                        dve.wait_ge(sem("o_ready"), u - 1)
                    CP(pT[:, u % 2, 2:4, :], ps[:, 5, :].rearrange("p (k t) -> p k t", k=2)) \
                        .then_inc(sem("pT_dve"), 1)
                if u >= 1:
                    output_rest(u - 1)
            output_rest(len(att) - 1)
            for u in range(4):
                split_lo(7 + u)
                for j in range(2):
                    g = G_WO + 2 * u + j
                    dve.wait_ge(sem("acc_ready"), g + 1)
                    CP(by_chunk(ybuf[:, 2 * u + j, :], L0), ring(g, L0)).then_inc(sem("acc_taken"), 1)
            add_branch(0, 0, 1, 0, SEG0, 0, T)
            apply_norm(0, 1, 2, KT, SEG0, 0, T)

            def mlp(l, m0, chunks):
                w = sum(c[1] for c in chunks)
                dg = double_groups(l)

                def hidden(group, i=0):
                    for j in range(2):
                        z = 2 * NG * l + 2 * group + j
                        if group >= 1:
                            dve.wait_ge(sem("a_split"), z - 1 + 4 * i)
                        dve.wait_ge(sem("relu_done"), z + 1 + 4 * i)
                        STT(by_chunk(tmp[:, j, 0:w], chunks), ring(g_hidden(l, group, j), chunks), 0.0,
                            by_chunk(sq[:, j, 0:w], chunks), ALU.max, ALU.mult).then_inc(sem("acc_taken"), 1)
                        dve.wait_ge(sem("a_hi_done"), z + 1 + 4 * i)
                        slot = 2 * (group % 2) + j
                        TT(a_lo[:, slot, 0:w], tmp[:, j, 0:w], a_hi[:, slot, 0:w].bitcast(F32), ALU.subtract) \
                            .then_inc(sem("a_split"), 1)

                def output(step, i=0, js=range(KT)):
                    for j in js:
                        g = g_out(l, step, j)
                        dve.wait_ge(sem("acc_ready"), g + 1 + dg * i)
                        if step >= 1:
                            dve.wait_ge(sem("acc_taken"), g_out(l, step - 1, j) + 1 + dg * i)
                        else:
                            dve.wait_ge(sem("y_zero"), l + 1)
                        y = by_chunk(ybuf[:, j, 0:w], chunks)
                        TT(y, y, ring(g, chunks), ALU.add).then_inc(sem("acc_taken"), 1)

                split_lo(m0 + 1)
                hidden(0)

                def double(i, rel):
                    for st in range(2):
                        step, o, m = 2 * rel + st, i - rel, m0 + 2 + 2 * st + 4 * rel
                        split_lo(m, 4 * o)
                        hidden(step + 1, o)
                        if l == 0 and rel < 6:
                            g = g_rows(step)
                            dve.wait_ge(sem("acc_ready"), g + 1 + dg * o)
                            CP(rst[:, 0:512], ps[:, 2 * (g % 4), :]).then_inc(sem("acc_taken"), 1)
                            output(step, o, range(2))
                            split_lo(m + 1, 4 * o)
                            output(step, o, range(2, 4))
                            g, c0 = g_cols(step), 8 * (12 + step)
                            dve.wait_ge(sem("acc_ready"), g + 1 + dg * o)
                            dst = mod_cols[:, bass.ds(c0 + 16 * o, 8)] if rel == 1 else mod_cols[:, c0:c0 + 8]
                            CP(dst, ps[:, 2 * (g % 4), 0:8]).then_inc(sem("acc_taken"), 1)
                            output(step, o, range(4, KT))
                        else:
                            output(step, o, range(2))
                            split_lo(m + 1, 4 * o)
                            output(step, o, range(2, KT))

                double(0, 0)
                with dve.Fori(1, 6) as i:
                    double(i, 1)
                double(6, 6)
                split_lo(m0 + 30)
                hidden(15)
                split_lo(m0 + 31)
                output(14)
                output(15)

            mlp(0, M_MLP0, L0)
            for j in range(6):
                mods(1, j)
            dve.wait_ge(sem("mod_ready"), 10)

            dve.wait_ge(sem("s5_in"), 16 * 7)
            dve.wait_ge(sem("dt_ready"), 1)
            TS(lr, are, dtc, None, ALU.mult)
            TS(li, aim, dtc, None, ALU.mult).then_inc(sem("lam_dt"), 1)
            dve.wait_ge(sem("lam_dt"), 1)
            link(TS(kk, li, 1.0 / TWO_PI, MAGIC, ALU.mult, ALU.add))
            link(TS(kk, kk, -MAGIC, None, ALU.add))
            link(STT(t0_, kk, -PI_HI, li, ALU.mult, ALU.add))
            link(STT(t1_, kk, -PI_MID, t0_, ALU.mult, ALU.add))
            link(STT(t2_, kk, -PI_LO, t1_, ALU.mult, ALU.add))
            link(TS(ang, t2_, 3.1415925, -3.1415925, ALU.min, ALU.max))
            link(STT(t0_, ang, -1.0, ang, ALU.mult, ALU.max))
            TS(ang2, t0_, -1.0, math.pi / 2, ALU.mult, ALU.add).then_inc(sem("angles"), 1)
            add_branch(0, 1, 3, 1, SEG0, 0, T)
            dve.wait_ge(sem("mag_ready"), 1)
            dve.wait_ge(sem("sin_ready"), 1)
            pw9 = lambda r, e: flat_tok[:, (r * 9 + e) * P:(r * 9 + e) * P + NP]
            nc.vector.memset(pw9(0, 0), 1.0)
            nc.vector.memset(pw9(1, 0), 0.0)
            TT(pw9(0, 1), mag, cs, ALU.mult)
            link(TT(pw9(1, 1), mag, sn, ALU.mult))
            ar, ai = pw9(0, 1), pw9(1, 1)
            for e in range(2, 9):
                TT(t0_, pw9(0, e - 1), ar, ALU.mult)
                TT(t1_, pw9(1, e - 1), ai, ALU.mult)
                TT(t2_, pw9(0, e - 1), ai, ALU.mult)
                link(TT(den, pw9(1, e - 1), ar, ALU.mult))
                TT(pw9(0, e), t0_, t1_, ALU.subtract)
                link(TT(pw9(1, e), t2_, den, ALU.add))
            pw2 = flat_tok[:, 0:18 * P].rearrange("p (n u s) -> p n u s", u=2, s=NP)
            CP(pw2[:, :, 1, :], pw2[:, :, 0, :]).then_inc(sem("powers_ready"), 1)
            TS(arm1, ar, -1.0, None, ALU.add)
            TT(t0_, are, are, ALU.mult)
            link(TT(t1_, aim, aim, ALU.mult))
            link(TT(t2_, t0_, t1_, ALU.add))
            link(nc.vector.reciprocal(den, t2_))
            TT(t0_, arm1, are, ALU.mult)
            link(TT(t1_, ai, aim, ALU.mult))
            link(TT(t2_, t0_, t1_, ALU.add))
            link(TT(cre, t2_, den, ALU.mult))
            TT(t0_, ai, are, ALU.mult)
            link(TT(t1_, arm1, aim, ALU.mult))
            link(TT(t2_, t0_, t1_, ALU.subtract))
            TT(cim, t2_, den, ALU.mult).then_inc(sem("gains_ready"), 1)

            dve.wait_ge(sem("gains_ready"), 1)
            dve.wait_ge(sem("c_ready"), 1)
            TT(b_out[:, 1, :, :], b_in[0], by_channel(cre), ALU.mult)
            link(TT(b_tmp[0], b_in[1], by_channel(cim), ALU.mult))
            TT(b_out[:, 1, :, :], b_out[:, 1, :, :], b_tmp[0], ALU.subtract).then_inc(sem("b_re"), 1)

            def turns_out(i0, i1):
                for i in range(i0, i1):
                    if not act_turn(i):
                        dve.wait_ge(sem("turned"), i + 1)
                        dst, src = turn_out(i)
                        CP(dst, src).then_inc(sem("turned_dve"), 1)

            dve.wait_ge(sem("rstd_ready"), 5)
            for k in range(KT):
                if k >= 2:
                    dve.wait_ge(sem("h1_ready"), k - 1)
                scale(1, 0, k, SEG0, 0).then_inc(sem("h1_scaled"), 1)
            turns_out(C_TURNS, C_TURNS + P_TURNS)
            wait_turned(dve, C_TURNS + P_TURNS - 1)
            wait_turned(dve, C_TURNS + P_TURNS - 2)
            for g2 in range(2):
                p = slice(64 * g2, 64 * g2 + 64)
                for r in range(2):
                    src = powT[p, r, 8, :].rearrange("p (d q g) -> p d q g", d=2, g=2)[:, :, :, g2]
                    if r == 0:
                        CP(a8[p, 0, :, 0, :], src)
                        CP(a8[p, 1, :, 1, :], src)
                    else:
                        TS(a8[p, 1, :, 0, :], src, -1.0, None, ALU.mult)
                        q = CP(a8[p, 0, :, 1, :], src)
            q.then_inc(sem("prep_over"), 1)

            turns_out(C_TURNS + P_TURNS, TURNS)
            wait_turned(dve, TURNS - 1)
            dve.wait_ge(sem("prep_over"), 1)
            dve.wait_ge(sem("d_in"), 16 * 4)

            def products(j, par, inward, dst, reader, n):
                b, d = (j % 16) // 2, j % 2
                own = j if j < 16 else j - 2 * POOL_BLOCKS
                if own == 16:
                    dve.wait_ge(sem("xv_pool"), 2 * POOL_BLOCKS)
                    dve.wait_ge(sem("restacked_act"), 4)
                if own:
                    dve.wait_ge(sem("wp_sum"), own)
                TT(mul_buf(sq), per_t(par, b, d), power(0, b, d, inward), ALU.mult).then_inc(sem("m1_ready"), 1)
                dve.wait_ge(sem("m1_ready"), own + 1)
                dve.wait_ge(sem("m2_ready"), j + 1)
                if n >= 1:
                    dve.wait_ge(sem(reader), n)
                TT(dst, mul_buf(sq), mul_buf(tmp), ALU.add).then_inc(sem("wp_sum"), 1)

            pvv = pv[:, 0:2 * GROUPS * SC].rearrange("p (g c) -> p g c", c=SC)

            def finish_kernels(b):
                dve.wait_ge(sem("kf_copied"), b + 1)
                lag0 = kernels(b)[:, :, 7 * SC:8 * SC]
                link(TT(lag0, lag0, lag0_of_backward(b), ALU.add))
                TT(lag0, lag0, sdm[:, 2 * b:2 * b + 2, :], ALU.add).then_inc(sem("kf_taken"), 1)

            def in_products(j):
                products(j, pw, True, in_matrices(j).rearrange("p g (t c) -> p g t c", t=CH), "kf_ready", j - 1)

            def imaginary_inputs(j):
                chunk_inputs_out(dve, CP, j, 1).then_inc(sem("bu_taken_dve"), 1)

            dve.wait_ge(sem("h1_scaled"), KT)
            link(TT(sdm[:, :, :], cmask[:, :].unsqueeze(1).to_broadcast([P, 16, SC]),
                    dcol[:, :].unsqueeze(2).to_broadcast([P, 16, SC]), ALU.mult))
            for b in range(8):
                if b >= 2:
                    finish_kernels(b - 2)
                for j in (2 * b, 2 * b + 1):
                    in_products(j)
                    if j >= 2:
                        imaginary_inputs(j - 2)
            imaginary_inputs(14)
            imaginary_inputs(15)
            finish_kernels(6)
            finish_kernels(7)

            dve.wait_ge(sem("bu_taken"), 16)
            dve.wait_ge(sem("bu_taken_dve"), 16)
            moved = rst[:, 0:2 * P].rearrange("p (d c r q) -> p d c r q", c=2, d=2, r=2)
            for i_ in range(1, 1 + SCAN_STEPS):
                c = SCAN_INCS * (i_ - 1)
                for d in range(2):
                    if i_ > 1:
                        dve.wait_ge(sem("scan"), c - 1 + d)
                    parts = Sv[:, i_, d, :, :].unsqueeze(2).to_broadcast([P, 2, 2, 32])
                    TT(moved[:, d], a8[:, :, d], parts, ALU.mult).then_inc(sem("scan"), 1)
                for part in range(2):
                    for d in range(2):
                        cur = Sv[:, i_ + 1, d, :, :]
                        dve.wait_ge(sem("scan"), c + 2 * part + d + 1)
                        TT(cur, cur, moved[:, d, part], ALU.add).then_inc(sem("scan"), 1)

            for d in range(2):
                for r in range(2):
                    restack(nc.vector, CP, d, 0, r)
            for b in range(8):
                for d in range(2):
                    ahead = b + POOL_BLOCKS
                    if ahead < 8:
                        products(16 + 2 * ahead + d, pvv, False, xv_block(ahead, d), "restacked", 4)
                for hf in range(2):
                    dve.wait_ge(sem("ys_ready"), 2 * b + hf + 1)
                    y = out_half(b, hf)
                    dve.wait_ge(sem("yl_taken"), 16)
                    TT(y, y, ps[0:NCL, (2 * b + hf) % 4, :].rearrange("p (g t c) -> p g t c", g=4, t=CH), ALU.add) \
                        .then_inc(sem("ys_taken"), 1)

            for k in range(KT):
                dve.wait_ge(sem("h_hi_done"), 2 * KT + k + 1)
                TT(h_lo[:, k, 0:SEQ], ybuf[:, k, 0:SEQ], h_hi[:, k, 0:SEQ].bitcast(F32), ALU.subtract) \
                    .then_inc(sem("h_split"), 1)
            split_lo(M_GLU)
            for u in range(4):
                split_lo(M_GLU + u + 1)
                for j in range(2):
                    g = G_GLU + 2 * u + j
                    dve.wait_ge(sem("sig_ready"), 2 * u + j + 1)
                    TT(ybuf[:, 2 * u + j, 0:SEQ], ybuf[:, 2 * u + j, 0:SEQ], sq[:, j, 0:SEQ], ALU.mult) \
                        .then_inc(sem("acc_taken"), 1)
            seg = [(0, SEQ, 0)]
            add_branch(1, 0, 5, 2, seg, CTX, SEQ)
            apply_norm(1, 1, 6, 3 * KT, seg, CTX, SEQ)
            mlp(1, M_MLP1, L1)
            add_branch(1, 1, 7, 3, seg, CTX, SEQ)
            for r in range(4):
                dve.wait_ge(sem("oT_ready"), 4 + r + 1)
                CP(otok[:, r, 512:1024], ps[:, 4 + r, :]).then_inc(sem("o_dve"), 1)


_INS = ["x", "c", "ctx", "c_ctx", "ada_w", "ada_b", "norm_g", "mlp_w1", "mlp_w2", "gqa_w_qkv", "gqa_q_norm",
        "gqa_k_norm", "gqa_w_o", "s5_a_re", "s5_a_im", "s5_log_dt", "s5_b_re", "s5_b_im", "s5_c_re", "s5_c_im",
        "s5_d", "s5_glu_w", "s5_glu_b"]


def shape_constants():
    ident = np.eye(P, dtype=np.float32)
    ones = np.ones((P, P), np.float32)
    rot = np.zeros((P, P), np.float32)
    for m in range(P):
        if (m // 32) % 2 == 0:
            rot[m + 32, m] = -1.0
        else:
            rot[m - 32, m] = 1.0
    mask = (np.arange(P)[:, None] % 32 == np.arange(SC)[None, :]).astype(np.float32)
    half = HD // 2
    inv = (1.0 / (10000.0 ** (np.arange(0, half, 2, dtype=np.float32) / half))).astype(np.float32)
    tok = (np.arange(NCL)[None, :] * CH + np.arange(CH)[:, None]).reshape(-1)
    ang = np.concatenate([np.outer(np.tile(inv, 2), (tok // 64).astype(np.float32)),
                          np.outer(np.tile(inv, 2), (tok % 64).astype(np.float32))]).astype(np.float32)
    return np.concatenate([ident, ones, rot, mask, np.cos(ang), np.sin(ang)], axis=1).astype(np.float32)


def kernel(**inputs):
    import numpy as _np
    import concourse.bacc as _bacc
    from concourse import mybir as _mybir
    from concourse.bass_utils import run_bass_kernel_spmd as _run

    nc = _bacc.Bacc("TRN2", target_bir_lowering=False, num_devices=1)
    arrays, args = {}, {}
    for name in _INS + ["consts"]:
        v = shape_constants() if name == "consts" else _np.ascontiguousarray(inputs[name])
        arrays[f"in_{name}"] = v
        args[name] = nc.dram_tensor(f"in_{name}", v.shape, _mybir.dt.from_np(v.dtype), kind="ExternalInput").ap()
    out = nc.dram_tensor("out_0", (1, SEQ, D), F32, kind="ExternalOutput").ap()
    build(nc, args, out)
    r = _run(nc, [arrays], core_ids=[0])
    return r.results[0]["out_0"]
```
